# Optimizing a Trainium2 kernel written in Bass

```python
import math
import jax, jax.numpy as jnp
from jax import lax
import numpy as np
import jax
import jax.numpy as jnp

D_MODEL = 1024
BATCH = 1
SEQ = 1024
DEPTH = 1

CHUNK = 64
HEAD_DIM = 64
EPS = 1e-6
ROPE_THETA = 10000.0
A_HEADS = 4
A_LEFT_CHUNKS = 8
A_BAND = (A_LEFT_CHUNKS + 1) * CHUNK
REL_CLIP = 128
B_HEADS = 4
IDX_HEADS = 4
IDX_DIM = 64
TOPK_MAX = 256
Q_BLOCK = 128
C_WIDTH = 512
C_BLOCKS = 8
C_BLOCK_DIM = C_WIDTH // C_BLOCKS
C_CONV = 4
LRU_C = 8.0
N_BRANCH = 3
A_WIDTH = A_HEADS * HEAD_DIM
B_WIDTH = B_HEADS * HEAD_DIM
MIX_WIDTH = A_WIDTH + B_WIDTH + C_WIDTH
D_FF = -(-8 * D_MODEL // (3 * 256)) * 256
IN_SPLITS = (A_WIDTH, A_WIDTH, A_WIDTH,
             B_WIDTH, B_WIDTH, B_WIDTH,
             IDX_HEADS * IDX_DIM, IDX_DIM, IDX_HEADS,
             C_WIDTH, C_WIDTH,
             N_BRANCH * D_MODEL)
D_IN = sum(IN_SPLITS)


def rms_norm(x, g):
    x32 = x.astype(jnp.float32)
    y = x32 * lax.rsqrt(jnp.mean(x32 * x32, axis=-1, keepdims=True) + EPS)
    return (y * g.astype(jnp.float32)).astype(x.dtype)

def rope_tables(seq):
    pos = jnp.arange(seq, dtype=jnp.float32)
    inv = 1.0 / (ROPE_THETA ** (jnp.arange(0, HEAD_DIM, 2, dtype=jnp.float32) / HEAD_DIM))
    ang = pos[:, None] * inv[None, :]
    ang = jnp.concatenate([ang, ang], axis=-1)
    return jnp.cos(ang), jnp.sin(ang)

def apply_rope(x, cos, sin):
    shape = (cos.shape[0],) + (1,) * (x.ndim - 3) + (cos.shape[1],)
    c, s = cos.reshape(shape), sin.reshape(shape)
    x32 = x.astype(jnp.float32)
    x1, x2 = jnp.split(x32, 2, axis=-1)
    rot = jnp.concatenate([-x2, x1], axis=-1)
    return (x32 * c + rot * s).astype(x.dtype)

def split_cols(z):
    offs, acc = [], 0
    for w in IN_SPLITS[:-1]:
        acc += w
        offs.append(acc)
    return jnp.split(z, offs, axis=-1)

def chunk_relpos_attention(q, k, v, rel_bias, rel_idx):
    b, s, h, d = q.shape
    n_c = s // CHUNK
    qc = q.reshape(b, n_c, CHUNK, h, d)
    pad = ((0, 0), (A_LEFT_CHUNKS, 0), (0, 0), (0, 0), (0, 0))
    kp = jnp.pad(k.reshape(b, n_c, CHUNK, h, d), pad)
    vp = jnp.pad(v.reshape(b, n_c, CHUNK, h, d), pad)
    kb = jnp.concatenate([kp[:, j:j + n_c] for j in range(A_LEFT_CHUNKS + 1)], axis=2)
    vb = jnp.concatenate([vp[:, j:j + n_c] for j in range(A_LEFT_CHUNKS + 1)], axis=2)
    sc = jnp.einsum('bcqhd,bckhd->bhcqk', qc, kb).astype(jnp.float32) * (d ** -0.5)
    bias = rel_bias.astype(jnp.float32)[:, rel_idx]
    sc = sc + bias[:, None]
    key_chunk = jnp.arange(n_c)[:, None] - A_LEFT_CHUNKS + jnp.arange(A_BAND)[None, :] // CHUNK
    valid = key_chunk >= 0
    sc = jnp.where(valid[None, None, :, None, :], sc, -jnp.inf)
    p = jax.nn.softmax(sc, axis=-1).astype(v.dtype)
    o = jnp.einsum('bhcqk,bckhd->bcqhd', p, vb)
    return o.reshape(b, s, h * d)

def indexer_sparse_attention(q, k, v, qi, ki, wi):
    b, s, h, d = q.shape
    topk = min(TOPK_MAX, s // 4)
    n_blk = s // Q_BLOCK
    key_chunk = jnp.arange(s) // CHUNK
    bidx = jnp.arange(b)[:, None, None]
    scale = d ** -0.5

    def to_blocks(t):
        return jnp.moveaxis(t.reshape((b, n_blk, Q_BLOCK) + t.shape[2:]), 1, 0)

    def block(args):
        blk, qb, qib, wib = args
        q_chunk = (blk * Q_BLOCK + jnp.arange(Q_BLOCK)) // CHUNK
        admissible = key_chunk[None, :] <= q_chunk[:, None]
        dots = jnp.einsum('bqhe,bse->bqhs', qib, ki).astype(jnp.float32)
        score = jnp.einsum('bqhs,bqh->bqs', jax.nn.relu(dots), wib.astype(jnp.float32))
        score = jnp.where(admissible[None], score, -jnp.inf)
        _, idx = lax.top_k(score, topk)
        sel_valid = (idx // CHUNK) <= q_chunk[None, :, None]
        ks = k[bidx, idx]
        vs = v[bidx, idx]
        att = jnp.einsum('bqhd,bqkhd->bhqk', qb, ks).astype(jnp.float32) * scale
        att = jnp.where(sel_valid[:, None], att, -jnp.inf)
        p = jax.nn.softmax(att, axis=-1).astype(v.dtype)
        return jnp.einsum('bhqk,bqkhd->bqhd', p, vs)

    out = lax.map(block, (jnp.arange(n_blk), to_blocks(q), to_blocks(qi), to_blocks(wi)))
    return jnp.moveaxis(out, 0, 1).reshape(b, s, h * d)

def rglru_branch(xc, yc, conv_w, conv_b, wa, ba, wx, bx, lam):
    b, s, c = xc.shape
    xp = jnp.pad(xc, ((0, 0), (C_CONV - 1, 0), (0, 0)))
    u = conv_b + sum(xp[:, j:j + s] * conv_w[j] for j in range(C_CONV))
    ub = u.reshape(b, s, C_BLOCKS, C_BLOCK_DIM)
    r = jax.nn.sigmoid(jnp.einsum('bsgi,gij->bsgj', ub, wa).reshape(b, s, c) + ba)
    i = jax.nn.sigmoid(jnp.einsum('bsgi,gij->bsgj', ub, wx).reshape(b, s, c) + bx)
    log_a = -LRU_C * r.astype(jnp.float32) * jax.nn.softplus(-lam.astype(jnp.float32))
    a = jnp.exp(log_a)
    gated_in = jnp.sqrt(-jnp.expm1(2.0 * log_a)) * (i * u).astype(jnp.float32)

    def combine(left, right):
        a1, b1 = left
        a2, b2 = right
        return a1 * a2, a2 * b1 + b2

    _, hs = lax.associative_scan(combine, (a, gated_in), axis=1)
    return hs.astype(xc.dtype) * jax.nn.gelu(yc)

def first_inputs(seed: int = 0) -> dict:
    key = jax.random.key(seed)
    ks = jax.random.split(key, 20)
    f32 = jnp.float32
    nrm = lambda k, shp: jax.random.normal(k, shp, f32)
    x = nrm(ks[0], (BATCH, SEQ, D_MODEL))
    g_mix = 1.0 + 0.02 * nrm(ks[1], (DEPTH, D_MODEL))
    w_in = nrm(ks[2], (DEPTH, D_MODEL, D_IN)) * D_MODEL ** -0.5
    qk_gain_a = 1.0 + 0.02 * nrm(ks[3], (DEPTH, 2, HEAD_DIM))
    rel_bias = 0.1 * nrm(ks[4], (DEPTH, A_HEADS, 2 * REL_CLIP + 1))
    qk_gain_b = 1.0 + 0.02 * nrm(ks[5], (DEPTH, 2, HEAD_DIM))
    g_idx_k = 1.0 + 0.02 * nrm(ks[6], (DEPTH, IDX_DIM))
    conv_w = nrm(ks[7], (DEPTH, C_CONV, C_WIDTH)) * C_CONV ** -0.5
    conv_b = 0.01 * nrm(ks[8], (DEPTH, C_WIDTH))
    lru_wa = nrm(ks[9], (DEPTH, C_BLOCKS, C_BLOCK_DIM, C_BLOCK_DIM)) * C_BLOCK_DIM ** -0.5
    lru_ba = 0.01 * nrm(ks[10], (DEPTH, C_WIDTH))
    lru_wx = nrm(ks[11], (DEPTH, C_BLOCKS, C_BLOCK_DIM, C_BLOCK_DIM)) * C_BLOCK_DIM ** -0.5
    lru_bx = 0.01 * nrm(ks[12], (DEPTH, C_WIDTH))
    a_c = jax.random.uniform(ks[13], (DEPTH, C_WIDTH), f32, 0.9, 0.999)
    a0 = a_c ** (1.0 / LRU_C)
    lru_lambda = jnp.log(a0) - jnp.log1p(-a0)
    b_gate = 0.01 * nrm(ks[14], (DEPTH, N_BRANCH * D_MODEL))
    row_scale = jnp.concatenate([jnp.full((A_WIDTH,), A_WIDTH ** -0.5, f32),
                                 jnp.full((B_WIDTH,), B_WIDTH ** -0.5, f32),
                                 jnp.full((C_WIDTH,), C_WIDTH ** -0.5, f32)])
    w_branch = nrm(ks[15], (DEPTH, MIX_WIDTH, D_MODEL)) * row_scale[None, :, None]
    w_out = nrm(ks[16], (DEPTH, D_MODEL, D_MODEL)) * D_MODEL ** -0.5
    g_ffn = 1.0 + 0.02 * nrm(ks[17], (DEPTH, D_MODEL))
    w_ffn_in = nrm(ks[18], (DEPTH, D_MODEL, 2 * D_FF)) * D_MODEL ** -0.5
    w_ffn_out = nrm(ks[19], (DEPTH, D_FF, D_MODEL)) * D_FF ** -0.5
    return {"x": x, "g_mix": g_mix, "w_in": w_in, "qk_gain_a": qk_gain_a, "rel_bias": rel_bias,
            "qk_gain_b": qk_gain_b, "g_idx_k": g_idx_k, "conv_w": conv_w, "conv_b": conv_b,
            "lru_wa": lru_wa, "lru_ba": lru_ba, "lru_wx": lru_wx, "lru_bx": lru_bx,
            "lru_lambda": lru_lambda, "b_gate": b_gate, "w_branch": w_branch, "w_out": w_out,
            "g_ffn": g_ffn, "w_ffn_in": w_ffn_in, "w_ffn_out": w_ffn_out}

def first_block(x, g_mix, w_in, qk_gain_a, rel_bias, qk_gain_b, g_idx_k, conv_w, conv_b,
              lru_wa, lru_ba, lru_wx, lru_bx, lru_lambda, b_gate, w_branch, w_out,
              g_ffn, w_ffn_in, w_ffn_out):
    b, s, _ = x.shape
    cos, sin = rope_tables(s)
    q_in_band = A_LEFT_CHUNKS * CHUNK + jnp.arange(CHUNK)
    rel_idx = jnp.clip(q_in_band[:, None] - jnp.arange(A_BAND)[None, :], -REL_CLIP, REL_CLIP) + REL_CLIP
    for l in range(DEPTH):
        h = rms_norm(x, g_mix[l])
        z = h @ w_in[l]
        aq, ak, av, bq, bk, bv, iq, ik, iw, cx, cy, gt = split_cols(z)
        hd = lambda t, n: t.reshape(b, s, n, HEAD_DIM)
        y_a = chunk_relpos_attention(rms_norm(hd(aq, A_HEADS), qk_gain_a[l, 0]),
                                     rms_norm(hd(ak, A_HEADS), qk_gain_a[l, 1]),
                                     hd(av, A_HEADS), rel_bias[l], rel_idx)
        q_b = apply_rope(rms_norm(hd(bq, B_HEADS), qk_gain_b[l, 0]), cos, sin)
        k_b = apply_rope(rms_norm(hd(bk, B_HEADS), qk_gain_b[l, 1]), cos, sin)
        q_i = apply_rope(iq.reshape(b, s, IDX_HEADS, IDX_DIM), cos, sin)
        k_i = apply_rope(rms_norm(ik, g_idx_k[l]), cos, sin)
        w_i = iw * (IDX_HEADS ** -0.5 * IDX_DIM ** -0.5)
        y_b = indexer_sparse_attention(q_b, k_b, hd(bv, B_HEADS), q_i, k_i, w_i)
        y_c = rglru_branch(cx, cy, conv_w[l], conv_b[l], lru_wa[l], lru_ba[l],
                           lru_wx[l], lru_bx[l], lru_lambda[l])
        gates = jax.nn.sigmoid(gt + b_gate[l]).reshape(b, s, N_BRANCH, D_MODEL)
        wb = w_branch[l]
        merged = (gates[:, :, 0] * (y_a @ wb[:A_WIDTH])
                  + gates[:, :, 1] * (y_b @ wb[A_WIDTH:A_WIDTH + B_WIDTH])
                  + gates[:, :, 2] * (y_c @ wb[A_WIDTH + B_WIDTH:]))
        x = x + merged @ w_out[l]
        gu = rms_norm(x, g_ffn[l]) @ w_ffn_in[l]
        g_, u_ = jnp.split(gu, 2, axis=-1)
        x = x + (jax.nn.silu(g_) * u_) @ w_ffn_out[l]
    return x


DEPTH_2 = 2

GRID_W = 64
CTX_LEN = 256
NEG = -1e30
ROPE_DIM = 64

A_HEADS_2 = 8
A_KV_HEADS = 2
A_HEAD_DIM = ROPE_DIM
A_WINDOW = 128
B_HEAD_DIM = ROPE_DIM
C_HEADS = 4
C_Q_RANK = 256
C_KV_RANK = 128
C_NOPE_DIM = 128
C_ROPE_DIM = ROPE_DIM
C_V_DIM = 128
D_HEADS = 8
D_HEAD_DIM = 64
D_WIN_ROWS = 8
D_WIN_COLS = 16

MIX_EVEN = A_HEADS_2 * A_HEAD_DIM + B_HEADS * 2 * B_HEAD_DIM
MIX_ODD = C_HEADS * C_V_DIM + D_HEADS * D_HEAD_DIM
EVEN_SPLITS = (A_HEADS_2 * A_HEAD_DIM, A_KV_HEADS * A_HEAD_DIM, A_KV_HEADS * A_HEAD_DIM, B_HEADS * 2 * B_HEAD_DIM, B_HEADS * 2 * B_HEAD_DIM, B_HEADS * 2 * B_HEAD_DIM, MIX_EVEN)
ODD_SPLITS = (C_Q_RANK, C_KV_RANK, C_ROPE_DIM, D_HEADS * D_HEAD_DIM, D_HEADS * D_HEAD_DIM, D_HEADS * D_HEAD_DIM, MIX_ODD)
IN_EVEN = sum(EVEN_SPLITS)
IN_ODD = sum(ODD_SPLITS)


def rmsnorm(x, g):
    xf = x.astype(jnp.float32)
    y = xf * lax.rsqrt(jnp.mean(xf * xf, axis=-1, keepdims=True) + EPS)
    return (y * g.astype(jnp.float32)).astype(x.dtype)

def _split(t, sizes):
    return jnp.split(t, np.cumsum(sizes)[:-1].tolist(), axis=-1)

def _axial_rope_tables(S, dim):
    t = jnp.arange(S)
    row = (t // GRID_W).astype(jnp.float32)
    col = (t % GRID_W).astype(jnp.float32)
    quarter = dim // 4
    inv = ROPE_THETA ** (-jnp.arange(quarter, dtype=jnp.float32) / quarter)
    ang_r = row[:, None] * inv[None, :]
    ang_c = col[:, None] * inv[None, :]
    ang = jnp.concatenate([ang_r, ang_r, ang_c, ang_c], axis=-1)
    return jnp.cos(ang), jnp.sin(ang)

def _rope(x, cos, sin):
    half = x.shape[-1] // 2
    qtr = half // 2
    xr, xc = x[..., :half], x[..., half:]
    rot = jnp.concatenate([-xr[..., qtr:], xr[..., :qtr], -xc[..., qtr:], xc[..., :qtr]], axis=-1)
    return (x * cos[:, None, :] + rot * sin[:, None, :]).astype(x.dtype)

def _modulate(x, cond, norm_g, w_ada, b_ada):
    mod = jax.nn.silu(cond) @ w_ada + b_ada
    shift, scale, gate = jnp.split(mod[:, None, :], 3, axis=-1)
    return rmsnorm(x, norm_g) * (1.0 + scale) + shift, gate

def _sweep_query_blocks(fn, q):
    B, S = q.shape[:2]
    nb = S // Q_BLOCK
    qb = jnp.moveaxis(q.reshape((B, nb, Q_BLOCK) + q.shape[2:]), 1, 0)
    out = lax.map(lambda a: fn(a[0], a[1]), (jnp.arange(nb), qb))
    out = jnp.moveaxis(out, 0, 1)
    return out.reshape((B, S) + out.shape[3:])

def _softmax_attend(q, k, v):
    s = jnp.einsum('bqhd,bkhd->bhqk', q, k).astype(jnp.float32) * (q.shape[-1] ** -0.5)
    p = jax.nn.softmax(s, axis=-1).astype(v.dtype)
    return jnp.einsum('bhqk,bkhe->bqhe', p, v)

def _sink_probs(parts, sink):
    base = parts[0]
    Hk, G = base.shape[1], base.shape[2]
    snk = jnp.broadcast_to(sink.astype(jnp.float32).reshape(Hk, G)[None, :, :, None, None], base.shape[:-1] + (1,))
    p = jax.nn.softmax(jnp.concatenate(list(parts) + [snk], axis=-1), axis=-1)
    return p[..., :-1]

def _window_gqa_sink(q, k, v, kc, vc, sink):
    B, S, Hk, G, d = q.shape
    L = kc.shape[1]
    W = A_WINDOW
    span = Q_BLOCK + 2 * W
    scale = d ** -0.5
    kp = jnp.pad(k, ((0, 0), (W, W), (0, 0), (0, 0)))
    vp = jnp.pad(v, ((0, 0), (W, W), (0, 0), (0, 0)))

    def block(n, qn):
        start = n * Q_BLOCK
        kn = lax.dynamic_slice_in_dim(kp, start, span, axis=1)
        vn = lax.dynamic_slice_in_dim(vp, start, span, axis=1)
        qpos = start + jnp.arange(Q_BLOCK)
        kpos = start - W + jnp.arange(span)
        valid = (jnp.abs(qpos[:, None] - kpos[None, :]) <= W) & (kpos >= 0)[None, :] & (kpos < S)[None, :]
        s_loc = jnp.einsum('bqkgd,bskd->bkgqs', qn, kn).astype(jnp.float32) * scale
        s_loc = jnp.where(valid, s_loc, NEG)
        s_ctx = jnp.einsum('bqkgd,bckd->bkgqc', qn, kc).astype(jnp.float32) * scale
        p = _sink_probs([s_loc, s_ctx], sink).astype(v.dtype)
        return (jnp.einsum('bkgqs,bskd->bqkgd', p[..., :span], vn)
                + jnp.einsum('bkgqc,bckd->bqkgd', p[..., span:span + L], vc))

    return _sweep_query_blocks(block, q)

def _ctx_sink_attend(q, k, v, sink):
    s = jnp.einsum('bqkgd,bckd->bkgqc', q, k).astype(jnp.float32) * (q.shape[-1] ** -0.5)
    p = _sink_probs([s], sink).astype(v.dtype)
    return jnp.einsum('bkgqc,bckd->bqkgd', p, v)

def _diff_lambda(b_lambda, lam_init):
    lf = b_lambda.astype(jnp.float32)
    return jnp.exp(jnp.sum(lf[0] * lf[1])) - jnp.exp(jnp.sum(lf[2] * lf[3])) + lam_init

def _diff_attend(q, k, v, lam):
    s = jnp.einsum('bqhte,bkhte->bhtqk', q, k).astype(jnp.float32) * (q.shape[-1] ** -0.5)
    p = jax.nn.softmax(s, axis=-1)
    a = (p[:, :, 0] - lam * p[:, :, 1]).astype(v.dtype)
    return jnp.einsum('bhqk,bkhe->bqhe', a, v)

def _mla_qkv(cq, ckv, kr, q_norm_g, kv_norm_g, w_qb, w_kvb, cos, sin):
    B, T, _ = cq.shape
    q = (rmsnorm(cq, q_norm_g) @ w_qb).reshape(B, T, C_HEADS, C_NOPE_DIM + C_ROPE_DIM)
    kv = (rmsnorm(ckv, kv_norm_g) @ w_kvb).reshape(B, T, C_HEADS, C_NOPE_DIM + C_V_DIM)
    q_nope, q_pe = q[..., :C_NOPE_DIM], q[..., C_NOPE_DIM:]
    k_nope, v = kv[..., :C_NOPE_DIM], kv[..., C_NOPE_DIM:]
    k_pe = kr[:, :, None, :]
    if cos is not None:
        q_pe = _rope(q_pe, cos, sin)
        k_pe = _rope(k_pe, cos, sin)
    q = jnp.concatenate([q_nope, q_pe], axis=-1)
    k = jnp.concatenate([k_nope, jnp.broadcast_to(k_pe, (B, T, C_HEADS, C_ROPE_DIM))], axis=-1)
    return q, k, v

def _neighbourhood_attend(q, k, v, kc, vc, rpb):
    B, S, H, d = q.shape
    L = kc.shape[1]
    rows = S // GRID_W
    kr_n = min(D_WIN_ROWS, rows)
    kw_n = D_WIN_COLS
    n_loc = kr_n * GRID_W
    scale = d ** -0.5
    kg = k.reshape(B, rows, GRID_W, H, d)
    vg = v.reshape(B, rows, GRID_W, H, d)
    cols = jnp.arange(GRID_W)
    cs = jnp.clip(cols - kw_n // 2, 0, GRID_W - kw_n)
    col_ok = (cols[None, :] >= cs[:, None]) & (cols[None, :] < cs[:, None] + kw_n)
    mask = jnp.broadcast_to(col_ok[:, None, :], (GRID_W, kr_n, GRID_W)).reshape(GRID_W, n_loc)
    dc = jnp.clip(cols[None, :] - cols[:, None] + (D_WIN_COLS - 1), 0, 2 * D_WIN_COLS - 2)
    rpb_f = rpb.astype(jnp.float32)
    qg = jnp.moveaxis(q.reshape(B, rows, GRID_W, H, d), 1, 0)

    def row_fn(args):
        r, qr = args
        rs = jnp.clip(r - kr_n // 2, 0, rows - kr_n)
        ks = lax.dynamic_slice_in_dim(kg, rs, kr_n, axis=1).reshape(B, n_loc, H, d)
        vs = lax.dynamic_slice_in_dim(vg, rs, kr_n, axis=1).reshape(B, n_loc, H, d)
        dr = rs + jnp.arange(kr_n) - r + (D_WIN_ROWS - 1)
        bias = rpb_f[:, dr[:, None, None], dc[None, :, :]]
        bias = jnp.transpose(bias, (0, 2, 1, 3)).reshape(H, GRID_W, n_loc)
        s_loc = jnp.einsum('bqhd,bkhd->bhqk', qr, ks).astype(jnp.float32) * scale + bias[None]
        s_loc = jnp.where(mask, s_loc, NEG)
        s_ctx = jnp.einsum('bqhd,bchd->bhqc', qr, kc).astype(jnp.float32) * scale
        p = jax.nn.softmax(jnp.concatenate([s_loc, s_ctx], axis=-1), axis=-1).astype(v.dtype)
        return (jnp.einsum('bhqk,bkhd->bqhd', p[..., :n_loc], vs)
                + jnp.einsum('bhqc,bchd->bqhd', p[..., n_loc:], vc))

    out = lax.map(row_fn, (jnp.arange(rows), qg))
    return jnp.moveaxis(out, 0, 1).reshape(B, S, H, d)

def _even_layer(x, xc, c, c_ctx, li, norm_g, w_ada, b_ada, w_in, a_sink, b_lambda, b_subln_g, w_out, cos, sin, ctx_out):
    B, S, _ = x.shape
    L = xc.shape[1]
    d = A_HEAD_DIM
    e = B_HEAD_DIM
    Hk, G = A_KV_HEADS, A_HEADS_2 // A_KV_HEADS
    h, gate = _modulate(x, c, norm_g, w_ada, b_ada)
    hc, gate_c = _modulate(xc, c_ctx[None, :], norm_g, w_ada, b_ada)
    qa, ka, va, qb, kb, vb, g = _split(h @ w_in, EVEN_SPLITS)
    qac, kac, vac, qbc, kbc, vbc, gc = _split(hc @ w_in, EVEN_SPLITS)
    qa = _rope(qa.reshape(B, S, A_HEADS_2, d), cos, sin).reshape(B, S, Hk, G, d)
    ka = _rope(ka.reshape(B, S, Hk, d), cos, sin)
    va = va.reshape(B, S, Hk, d)
    kac = kac.reshape(B, L, Hk, d)
    vac = vac.reshape(B, L, Hk, d)
    ya = _window_gqa_sink(qa, ka, va, kac, vac, a_sink)
    qb = _rope(qb.reshape(B, S, B_HEADS * 2, e), cos, sin).reshape(B, S, B_HEADS, 2, e)
    kb = _rope(kb.reshape(B, S, B_HEADS * 2, e), cos, sin).reshape(B, S, B_HEADS, 2, e)
    vb = vb.reshape(B, S, B_HEADS, 2 * e)
    kbc = kbc.reshape(B, L, B_HEADS, 2, e)
    vbc = vbc.reshape(B, L, B_HEADS, 2 * e)
    lam_init = 0.8 - 0.6 * math.exp(-0.3 * li)
    lam = _diff_lambda(b_lambda, lam_init)
    kb_all = jnp.concatenate([kb, kbc], axis=1)
    vb_all = jnp.concatenate([vb, vbc], axis=1)
    yb = _sweep_query_blocks(lambda n, qn: _diff_attend(qn, kb_all, vb_all, lam), qb)
    yb = rmsnorm(yb, b_subln_g) * (1.0 - lam_init)
    y = jnp.concatenate([ya.reshape(B, S, -1), yb.reshape(B, S, -1)], axis=-1) * jax.nn.silu(g)
    x = x + gate * (y @ w_out)
    if ctx_out:
        yac = _ctx_sink_attend(qac.reshape(B, L, Hk, G, d), kac, vac, a_sink)
        ybc = rmsnorm(_diff_attend(qbc.reshape(B, L, B_HEADS, 2, e), kbc, vbc, lam), b_subln_g) * (1.0 - lam_init)
        yc = jnp.concatenate([yac.reshape(B, L, -1), ybc.reshape(B, L, -1)], axis=-1) * jax.nn.silu(gc)
        xc = xc + gate_c * (yc @ w_out)
    return x, xc

def _odd_layer(x, xc, c, c_ctx, norm_g, w_ada, b_ada, w_in, q_norm_g, kv_norm_g, w_qb, w_kvb, rpb, w_out, cos, sin, ctx_out):
    B, S, _ = x.shape
    L = xc.shape[1]
    dd = D_HEAD_DIM
    h, gate = _modulate(x, c, norm_g, w_ada, b_ada)
    hc, gate_c = _modulate(xc, c_ctx[None, :], norm_g, w_ada, b_ada)
    cq, ckv, kr, qd, kd, vd, g = _split(h @ w_in, ODD_SPLITS)
    cqc, ckvc, krc, qdc, kdc, vdc, gc = _split(hc @ w_in, ODD_SPLITS)
    qm, km, vm = _mla_qkv(cq, ckv, kr, q_norm_g, kv_norm_g, w_qb, w_kvb, cos, sin)
    qmc, kmc, vmc = _mla_qkv(cqc, ckvc, krc, q_norm_g, kv_norm_g, w_qb, w_kvb, None, None)
    km_all = jnp.concatenate([km, kmc], axis=1)
    vm_all = jnp.concatenate([vm, vmc], axis=1)
    ym = _sweep_query_blocks(lambda n, qn: _softmax_attend(qn, km_all, vm_all), qm)
    kdc = kdc.reshape(B, L, D_HEADS, dd)
    vdc = vdc.reshape(B, L, D_HEADS, dd)
    yd = _neighbourhood_attend(qd.reshape(B, S, D_HEADS, dd), kd.reshape(B, S, D_HEADS, dd), vd.reshape(B, S, D_HEADS, dd), kdc, vdc, rpb)
    y = jnp.concatenate([ym.reshape(B, S, -1), yd.reshape(B, S, -1)], axis=-1) * jax.nn.silu(g)
    x = x + gate * (y @ w_out)
    if ctx_out:
        ymc = _softmax_attend(qmc, kmc, vmc)
        ydc = _softmax_attend(qdc.reshape(B, L, D_HEADS, dd), kdc, vdc)
        yc = jnp.concatenate([ymc.reshape(B, L, -1), ydc.reshape(B, L, -1)], axis=-1) * jax.nn.silu(gc)
        xc = xc + gate_c * (yc @ w_out)
    return x, xc

def second_inputs(seed: int = 0) -> dict:
    key = jax.random.key(seed)
    keys = iter(jax.random.split(key, 24))

    def nrm(shape, std):
        return std * jax.random.normal(next(keys), shape, jnp.float32)

    D = D_MODEL
    n_ev = (DEPTH_2 + 1) // 2
    n_od = DEPTH_2 // 2
    return {
        'x': nrm((BATCH, SEQ, D), 1.0),
        'c': nrm((BATCH, D), 1.0),
        'ctx': nrm((BATCH, CTX_LEN, D), 1.0),
        'c_ctx': nrm((D,), 1.0),
        'ev_norm_g': 1.0 + nrm((n_ev, D), 0.02),
        'ev_w_ada': nrm((n_ev, D, 3 * D), D ** -0.5),
        'ev_b_ada': nrm((n_ev, 3 * D), 0.02),
        'ev_w_in': nrm((n_ev, D, IN_EVEN), D ** -0.5),
        'ev_a_sink': nrm((n_ev, A_HEADS_2), 0.5),
        'ev_b_lambda': nrm((n_ev, 4, B_HEAD_DIM), 0.1),
        'ev_b_subln_g': 1.0 + nrm((n_ev, 2 * B_HEAD_DIM), 0.02),
        'ev_w_out': nrm((n_ev, MIX_EVEN, D), MIX_EVEN ** -0.5),
        'od_norm_g': 1.0 + nrm((n_od, D), 0.02),
        'od_w_ada': nrm((n_od, D, 3 * D), D ** -0.5),
        'od_b_ada': nrm((n_od, 3 * D), 0.02),
        'od_w_in': nrm((n_od, D, IN_ODD), D ** -0.5),
        'od_c_q_norm_g': 1.0 + nrm((n_od, C_Q_RANK), 0.02),
        'od_c_kv_norm_g': 1.0 + nrm((n_od, C_KV_RANK), 0.02),
        'od_c_w_qb': nrm((n_od, C_Q_RANK, C_HEADS * (C_NOPE_DIM + C_ROPE_DIM)), C_Q_RANK ** -0.5),
        'od_c_w_kvb': nrm((n_od, C_KV_RANK, C_HEADS * (C_NOPE_DIM + C_V_DIM)), C_KV_RANK ** -0.5),
        'od_d_rpb': nrm((n_od, D_HEADS, 2 * D_WIN_ROWS - 1, 2 * D_WIN_COLS - 1), 0.02),
        'od_w_out': nrm((n_od, MIX_ODD, D), MIX_ODD ** -0.5),
        'final_norm_g': 1.0 + nrm((D,), 0.02),
    }

def second_block(x, c, ctx, c_ctx, ev_norm_g, ev_w_ada, ev_b_ada, ev_w_in, ev_a_sink, ev_b_lambda, ev_b_subln_g, ev_w_out, od_norm_g, od_w_ada, od_b_ada, od_w_in, od_c_q_norm_g, od_c_kv_norm_g, od_c_w_qb, od_c_w_kvb, od_d_rpb, od_w_out, final_norm_g):
    S = x.shape[1]
    cos, sin = _axial_rope_tables(S, ROPE_DIM)
    xl, xc = x, ctx
    for i in range(DEPTH_2):
        ctx_out = i < DEPTH_2 - 1
        j = i // 2
        if i % 2 == 0:
            xl, xc = _even_layer(xl, xc, c, c_ctx, i, ev_norm_g[j], ev_w_ada[j], ev_b_ada[j], ev_w_in[j], ev_a_sink[j], ev_b_lambda[j], ev_b_subln_g[j], ev_w_out[j], cos, sin, ctx_out)
        else:
            xl, xc = _odd_layer(xl, xc, c, c_ctx, od_norm_g[j], od_w_ada[j], od_b_ada[j], od_w_in[j], od_c_q_norm_g[j], od_c_kv_norm_g[j], od_c_w_qb[j], od_c_w_kvb[j], od_d_rpb[j], od_w_out[j], cos, sin, ctx_out)
    return rmsnorm(xl, final_norm_g)


def setup_inputs(seed=0):
    out = dict(first_inputs(seed))
    for name, value in second_inputs(seed + 1).items():
        if name != "x":
            out[name + "_2"] = value
    return out


def reference(
    x, g_mix, w_in, qk_gain_a, rel_bias, qk_gain_b, g_idx_k, conv_w, conv_b, lru_wa, lru_ba,
    lru_wx, lru_bx, lru_lambda, b_gate, w_branch, w_out, g_ffn, w_ffn_in, w_ffn_out, c_2, ctx_2,
    c_ctx_2, ev_norm_g_2, ev_w_ada_2, ev_b_ada_2, ev_w_in_2, ev_a_sink_2, ev_b_lambda_2,
    ev_b_subln_g_2, ev_w_out_2, od_norm_g_2, od_w_ada_2, od_b_ada_2, od_w_in_2, od_c_q_norm_g_2,
    od_c_kv_norm_g_2, od_c_w_qb_2, od_c_w_kvb_2, od_d_rpb_2, od_w_out_2, final_norm_g_2,
):
    x = first_block(
        x, g_mix, w_in, qk_gain_a, rel_bias, qk_gain_b, g_idx_k, conv_w, conv_b, lru_wa, lru_ba,
        lru_wx, lru_bx, lru_lambda, b_gate, w_branch, w_out, g_ffn, w_ffn_in, w_ffn_out,
    )
    return second_block(
        x, c_2, ctx_2, c_ctx_2, ev_norm_g_2, ev_w_ada_2, ev_b_ada_2, ev_w_in_2, ev_a_sink_2,
        ev_b_lambda_2, ev_b_subln_g_2, ev_w_out_2, od_norm_g_2, od_w_ada_2, od_b_ada_2,
        od_w_in_2, od_c_q_norm_g_2, od_c_kv_norm_g_2, od_c_w_qb_2, od_c_w_kvb_2, od_d_rpb_2,
        od_w_out_2, final_norm_g_2,
    )


_drawn_inputs = setup_inputs


def setup_inputs(seed=0):
    import zlib

    import numpy as np

    out = dict(_drawn_inputs(seed))
    spreads = {}
    factors = {'g_mix': 4.74,
     'qk_gain_a': 8.0,
     'rel_bias': 8.0,
     'qk_gain_b': 8.0,
     'g_idx_k': 8.0,
     'conv_b': 2.806,
     'lru_ba': 8.0,
     'lru_bx': 8.0,
     'b_gate': 8.0,
     'g_ffn': 3.933,
     'ev_norm_g_2': 8.0,
     'ev_b_ada_2': 3.501,
     'ev_a_sink_2': 8.0,
     'ev_b_lambda_2': 8.0,
     'ev_b_subln_g_2': 8.0,
     'od_norm_g_2': 8.0,
     'od_b_ada_2': 5.267,
     'od_c_q_norm_g_2': 8.0,
     'od_c_kv_norm_g_2': 8.0,
     'od_d_rpb_2': 64.0,
     'final_norm_g_2': 9.018}
    for name, (base, spread) in spreads.items():
        noise = np.random.default_rng([zlib.crc32(name.encode()), seed]).standard_normal(out[name].shape)
        drawn = base * np.exp(spread * noise) if base else spread * noise
        out[name] = jnp.asarray(drawn.astype(out[name].dtype))
    for name, factor in factors.items():
        out[name] = (out[name] * factor).astype(out[name].dtype)
    return out
```

```python
import numpy as np
import concourse.bass as bass
from concourse import mybir

F = mybir.dt.float32
R = mybir.dt.float32r
ACT = mybir.ActivationFunctionType
ALU = mybir.AluOpType
AX = mybir.AxisListType

P = 128
T = 1024
TC = 1280
EPS = 1e-6
NEG = -1e30
OUT_OF_RANGE = -3.0e38
TAKEN = -3.3e38
FFN_GROUPS = [5, 5, 4, 4, 4]
CH1 = [(0, 512), (512, 512)]
CH2 = [(0, 512), (512, 512), (1024, 256)]



def weight_tiles():
    tiles = [("iq0", 8, 128), ("iq1", 8, 128), ("ikw", 8, 68)]
    for j in range(2):
        tiles += [(f"aq{j}", 8, 128), (f"ak{j}", 8, 128), (f"av{j}", 8, 128)]
    for j in range(4):
        tiles += [(f"cx{j}", 8, 128), (f"cy{j}", 8, 128)]
    for j in range(2):
        tiles += [(f"bq{j}", 8, 128), (f"bk{j}", 8, 128), (f"bv{j}", 8, 128)]
    for d in range(8):
        tiles += [(f"gt{i}_{d}", 8, 128) for i in range(3)] + [(f"wb{d}", 8, 128)]
    tiles += [(f"wo{d}", 8, 128) for d in range(8)]
    f0 = 0
    for n, g in enumerate(FFN_GROUPS):
        for f in range(f0, f0 + g):
            tiles += [(f"fg{f}", 8, 128), (f"fu{f}", 8, 128)]
        tiles += [(f"fo{n}_{d}", g, 128) for d in range(8)]
        f0 += g
    tiles += [(f"ea{m}", 8, 128) for m in range(24)]
    for j in range(4):
        tiles += [(f"eq{j}", 8, 128)]
        if j % 2 == 0:
            tiles += [(f"ek{j // 2}", 8, 128)]
        if j == 0:
            tiles += [("ev", 8, 128)]
        tiles += [(f"eg{j}", 8, 128)]
    for j in range(4):
        tiles += [(f"fq{j}", 8, 128), (f"fk{j}", 8, 128), (f"fv{j}", 8, 128), (f"eg{4 + j}", 8, 128)]
    tiles += [(f"eo{d}", 8, 128) for d in range(8)]
    tiles += [(f"oa{m}", 8, 128) for m in range(24)]
    for j in range(4):
        tiles += [(f"dq{j}", 8, 128), (f"dk{j}", 8, 128), (f"dv{j}", 8, 128), (f"og{4 + j}", 8, 128)]
    tiles += [("cq0", 8, 128), ("cq1", 8, 128), ("ckv", 8, 128), ("ckr", 8, 128)]
    tiles += [(f"og{h}", 8, 128) for h in range(4)]
    for h in range(4):
        if h % 2 == 0:
            tiles += [(f"qp{h // 2}", 2, 128)]
        tiles += [(f"qn{h}", 2, 128), (f"kn{h}", 1, 128), (f"vn{h}", 1, 128)]
    tiles += [(f"oo{d}", 8, 128) for d in range(8)]
    return tiles


def weight_offsets():
    at, out = 0, {}
    for name, kt, m in weight_tiles():
        out[name] = (at, kt, m)
        at += P * kt * m
    return out, at


VECS = [("g_mix", 8), ("aq_g", 1), ("ak_g", 1), ("bq_g", 1), ("bk_g", 1), ("ik_g", 1), ("conv_w", 16),
        ("conv_b", 4), ("lru_ba", 4), ("lru_bx", 4), ("lam", 4), ("b_gate", 24), ("g_ffn", 8),
        ("ev_g", 8), ("ev_b", 24), ("sink", 8), ("blam", 256), ("subln", 1), ("od_g", 8), ("od_b", 24),
        ("qn_g", 2), ("kvn_g", 1), ("fin_g", 8), ("cond", 16)]
CONSTS = [("ident", 128), ("o1024", 128), ("o64", 128), ("o256", 128), ("o128", 128), ("swap32", 128),
          ("swap16", 128), ("win", 384), ("col", 64)]


def offsets(table):
    at, out = 0, {}
    for name, n in table:
        out[name] = (at, n)
        at += n
    return out, at




class Tok:
    def __init__(self, sem, value=None):
        self.sem, self.value, self.wanted = sem, value, False


class Slot:

    def __init__(self, sem):
        self.sem, self.count = sem, 0


class Queue:
    def __init__(self, sem):
        self.sem, self.items, self.last = sem, [], None

    def wait(self, *toks):
        for t in toks:
            if isinstance(t, (list, tuple)):
                self.wait(*t)
            elif t is not None:
                t.wanted = True
                self.items.append((None, t))

    def op(self, fn, *waits):
        self.wait(*waits)
        t = Tok(self.sem)
        self.items.append((fn, t))
        self.last = t
        return t

    def dma(self, out, in_, slot, *waits):
        self.wait(*waits)
        slot.count += 16
        t = Tok(slot.sem, slot.count)
        self.items.append((lambda e: e.dma_start(out, in_), t))
        return t

    def number(self):
        n = 0
        for fn, t in self.items:
            if fn is not None and t.sem is self.sem and t.wanted:
                n += 1
                t.value = n

    def emit(self, e):
        seen = {}
        for fn, t in self.items:
            if fn is None:
                if seen.get(id(t.sem), 0) < t.value:
                    e.wait_ge(t.sem, t.value)
                    seen[id(t.sem)] = t.value
            else:
                ins = fn(e)
                if t.sem is not self.sem:
                    ins.then_inc(t.sem, 16)
                elif t.wanted:
                    ins.then_inc(t.sem, 1)


class Memory:

    def __init__(self, nc):
        self.nc, self.at, self.n, self.marks = nc, (nc.sbuf_base + 63) // 64 * 64, 0, []

    def __call__(self, shape, dt=F):
        size = 4
        for s in shape[1:]:
            size *= s
        t = self.nc.alloc_sbuf_tensor_at(f"m{self.n}", list(shape), dt, offset=self.at)
        self.n += 1
        self.at += (size + 63) // 64 * 64
        assert self.at <= self.nc.sbuf_usable_end, (self.at, self.nc.sbuf_usable_end)
        return t

    def __enter__(self):
        self.marks.append(self.at)
        return self

    def __exit__(self, *a):
        self.at = self.marks.pop()

    def over(self, at):
        self.marks.append(self.at)
        self.at = at
        return _Over(self)


class _Over:
    def __init__(self, mem):
        self.mem = mem

    def __enter__(self):
        return self.mem

    def __exit__(self, *a):
        self.mem.at = self.mem.marks.pop()


def build(nc, w, vec_d, cst_d, tab_d, xT, ctxT, biasA, biasD, lruw, out):
    W_AT, _ = weight_offsets()
    V_AT, NVEC = offsets(VECS)
    C_AT, NCST = offsets(CONSTS)

    sems = {}

    def sem(name):
        sems[name] = nc.alloc_semaphore(name)
        return sems[name]

    PE, A, V, G, SP = (Queue(sem(f"s_{n}")) for n in ("pe", "act", "dve", "pool", "sp"))
    free_slots = [Slot(sem(f"s_dma{i}")) for i in range(12)]
    slot_turn = [0]
    pending = []

    mem = Memory(nc)
    PS = nc.alloc_psum_tensor("PS", [P, 4096], F)
    x1_d = nc.dram_tensor("x1_scratch", [8, P, T], F, kind="Internal").ap()
    y_d = nc.dram_tensor("y_scratch", [8, P, TC], F, kind="Internal").ap()
    m_d = nc.dram_tensor("m_scratch", [8, P, T], F, kind="Internal").ap()

    def move(out_ap, in_ap, *waits):
        s = free_slots[slot_turn[0] % len(free_slots)]
        slot_turn[0] += 1
        if s.count:
            G.wait(Tok(s.sem, s.count))
        t = G.dma(out_ap, in_ap, s, *waits)
        pending.append(t)
        return t

    def barrier():
        lasts = [q.last for q in (PE, A, V, G) if q.last is not None]
        for q in (PE, A, V, G):
            q.wait(*[t for t in lasts if t is not q.last], *pending)
        pending.clear()

    bank_free = [[] for _ in range(8)]
    turn = [0]

    def bank(b):
        return PS[:, 512 * b:512 * b + 512]

    def take(first=0, n=6):
        b = first + turn[0] % n
        turn[0] += 1
        PE.wait(*bank_free[b])
        return b

    h_at = mem.at
    Hh = mem([P, 8, TC], R)
    Hl = mem([P, 8, TC], R)
    NRAW, NSPL = 3, 2
    raw = [mem([P, 1024]) for _ in range(NRAW)]
    whi = [mem([P, 1024], R) for _ in range(NSPL)]
    wlo = [mem([P, 1024], R) for _ in range(NSPL)]
    vec = mem([P, NVEC])
    cst = mem([P, NCST])
    tabs = mem([P, 2, T])
    epst = mem([P, 1])
    lam_t = mem([P, 8])
    mod = mem([P, 24, 2])
    gs = mem([P, 8, 2])
    csil = mem([P, 16])
    nsink = mem([P, 8])

    def vc(name, i=0, n=1):
        a = V_AT[name][0] + i
        return vec[:, a:a + n]

    def cc(name, r=P, n=None):
        a, m = C_AT[name]
        return cst[0:r, a:a + (n or m)]

    ident = cc("ident")

    order = weight_tiles()
    raw_slot = [Slot(sem(f"s_w{i}")) for i in range(NRAW)]
    raw_free = [[] for _ in range(NRAW)]
    spl_free = [[] for _ in range(NSPL)]
    st = {"load": 0, "prep": 0, "use": 0, "spl": 0}
    loaded, parts = {}, {}

    def w_load(upto):
        while st["load"] < min(upto, len(order)):
            i = st["load"]
            name, kt, m = order[i]
            s = i % NRAW
            at = W_AT[name][0]
            loaded[i] = SP.dma(raw[s][:, 0:kt * m],
                               w[at:at + P * kt * m].rearrange("(p c) -> p c", p=P), raw_slot[s], *raw_free[s])
            st["load"] += 1

    def w_prep(upto):
        while st["prep"] < min(upto, len(order)):
            i = st["prep"]
            name, kt, m = order[i]
            if name[:2] not in ("ea", "oa"):
                s, c, r = st["spl"] % NSPL, kt * m, i % NRAW
                hi, lo, src = whi[s][:, 0:c], wlo[s][:, 0:c], raw[r][:, 0:c]
                t1 = A.op(lambda e, hi=hi, src=src: e.copy(hi, src), loaded[i], spl_free[s])
                t2 = V.op(lambda e, hi=hi, lo=lo, src=src: e.tensor_tensor(lo, src, hi.bitcast(F), ALU.subtract),
                          loaded[i], spl_free[s], t1)
                raw_free[r] = [t1, t2]
                parts[i] = (s, [t1, t2])
                st["spl"] += 1
            st["prep"] += 1

    def w_get(name):
        i = st["use"]
        assert order[i][0] == name, (order[i], name)
        st["use"] += 1
        _, kt, m = order[i]
        w_load(i + NRAW)
        w_prep(i + 2)
        if i not in parts:
            r = i % NRAW
            PE.wait(loaded[i])

            def release(tok):
                raw_free[r] = [tok]
            return (lambda k: raw[r][:, k * m:(k + 1) * m]), kt, release
        s, toks = parts[i]
        PE.wait(*toks)

        def release(tok):
            spl_free[s] = [tok]
        return (lambda k: (whi[s][:, k * m:(k + 1) * m], wlo[s][:, k * m:(k + 1) * m])), kt, release

    def mm3(o, L, Rr, start, stop):
        PE.op(lambda e: e.matmul(o, L[0], Rr[0], start=start, stop=False))
        PE.op(lambda e: e.matmul(o, L[0], Rr[1], start=False, stop=False))
        return PE.op(lambda e: e.matmul(o, L[1], Rr[0], start=False, stop=stop))

    def mm(o, L, Rr, start=True, stop=True):
        return PE.op(lambda e: e.matmul(o, L, Rr, start=start, stop=stop))

    def linear(name, rhs, chunks, evac, rows=P):
        get, kt, release = w_get(name)
        for t0, tn in chunks:
            b = take()
            o = bank(b)[0:rows, 0:tn]
            for k in range(kt):
                tok = mm3(o, get(k), rhs(k, t0, tn), k == 0, k == kt - 1)
            bank_free[b] = evac(o, t0, tn, tok)
        release(tok)
        return tok

    def h_rhs(k, t0, tn):
        return Hh[:, k, t0:t0 + tn], Hl[:, k, t0:t0 + tn]

    def act(out_, in_, f, *waits, **kw):
        return A.op(lambda e: e.activation(out_, in_, f, **kw), *waits)

    def split(hi, lo, src, *waits):
        t1 = A.op(lambda e: e.copy(hi, src), *waits)
        t2 = V.op(lambda e: e.tensor_tensor(lo, src, hi.bitcast(F), ALU.subtract), *waits, t1)
        return [t1, t2]

    def tt(out_, a, b, op, *waits, q=None):
        return (q or V).op(lambda e: e.tensor_tensor(out_, a, b, op), *waits)

    def ts(out_, a, s1, s2, o0, o1, *waits):
        if s2 is None:
            return V.op(lambda e: e.tensor_scalar(out_, a, s1, None, o0), *waits)
        return V.op(lambda e: e.tensor_scalar(out_, a, s1, s2, o0, o1), *waits)

    def stt(out_, a, s, b, o0, o1, *waits):
        return V.op(lambda e: e.scalar_tensor_tensor(out=out_, in0=a, scalar=s, in1=b, op0=o0, op1=o1), *waits)

    def root(rs, ps, tok):
        n = rs.shape[0]
        t = act(rs, ps, ACT.Sqrt, tok, bias=epst[0:n, 0:1])
        return V.op(lambda e: e.reciprocal(rs, rs), t), t

    def norm_split(src, kt, ones, chunks, g, shift, ready, hi, lo, bufs=None):
        out_toks = []
        with mem:
            bufs = bufs or [mem([P, 512]) for _ in range(7)]
            sq, rs, tmp = bufs[0:2], bufs[2:4], bufs[4:7]
            sq_free, rs_free, tmp_free, n, nt = [[], []], [[], []], [[], [], []], 0, 0
            for c, (t0, tn) in enumerate(chunks):
                b = take()
                o = bank(b)[:, 0:tn]
                for k in range(kt):
                    s = sq[n % 2][:, 0:tn]
                    t = act(s, src(k, t0, tn), ACT.Square, ready, sq_free[n % 2])
                    PE.wait(t)
                    m = mm(o, ones, s, k == 0, k == kt - 1)
                    sq_free[n % 2] = [m]
                    n += 1
                r = rs[c % 2][:, 0:tn]
                A.wait(rs_free[c % 2])
                t, ta = root(r, o, m)
                bank_free[b] = [ta]
                for k in range(kt):
                    q = tmp[nt % 3][:, 0:tn]
                    t1 = stt(q, src(k, t0, tn), g(k, c), r, ALU.mult, ALU.mult, t, tmp_free[nt % 3], ready)
                    h, l_ = hi(k, t0, tn), lo(k, t0, tn)
                    sh = shift(k, c) if shift else None
                    if sh is None:
                        t2 = A.op(lambda e, h=h, q=q: e.copy(h, q), t1)
                        t3 = tt(l_, q, h.bitcast(F), ALU.subtract, t2)
                    else:
                        t2 = act(h, q, ACT.Identity, t1, bias=sh)
                        t3 = stt(l_, q, sh, h.bitcast(F), ALU.add, ALU.subtract, t2)
                    tmp_free[nt % 3] = [t3]
                    nt += 1
                    out_toks = [t2, t3]
                rs_free[c % 2] = [t1]
        return out_toks

    t_c = [move(vec[:, :], vec_d), move(cst[:, :], cst_d)]
    t_tab = move(tabs[:, :, :], tab_d[0].rearrange("a p t -> p a t"))
    t_e = V.op(lambda e: e.memset(epst[:, :], EPS))
    w_load(NRAW)
    for q in (PE, A, V, G):
        q.wait(*t_c, t_tab, t_e)

    def copy_to(dst, scale=1.0):
        toks = []

        def evac(o, t0, tn, tok):
            d = dst(t0, tn)
            if scale == 1.0:
                t = A.op(lambda e: e.copy(d, o), tok)
            else:
                t = A.op(lambda e: e.mul(d, o, scale), tok)
            toks.append(t)
            return [t]
        evac.toks = toks
        return evac

    def post(z, rows, chunks, gain, swap, hi, lo, tmp, z_toks, ones="o64", rope_end=T):
        sq, rs, t1b, t2b = tmp
        toks = list(z_toks)
        for t0, tn in chunks:
            zc = z[0:rows, t0:t0 + tn]
            if gain is not None:
                s, r = sq[0:rows, 0:tn], rs[0:rows, 0:tn]
                t = act(s, zc, ACT.Square, *toks)
                PE.wait(t)
                b = take()
                o = bank(b)[0:rows, 0:tn]
                m = mm(o, cst[0:rows, C_AT[ones][0]:C_AT[ones][0] + rows], s)
                A.wait(V.last)
                t, ta = root(r, o, m)
                bank_free[b] = [ta]
                t = stt(zc, zc, gain[0:rows, :], r, ALU.mult, ALU.mult, t, *toks)
                A.wait(m)
                toks_c = [t]
            else:
                toks_c = list(toks)
            if swap is not None and t0 < rope_end:
                PE.wait(*toks_c)
                b = take()
                o = bank(b)[0:rows, 0:tn]
                m = mm(o, cst[0:rows, C_AT[swap][0]:C_AT[swap][0] + rows], zc)
                u, v = t1b[0:rows, 0:tn], t2b[0:rows, 0:tn]
                tg = tt(u, zc, tabs[0:rows, 0, t0:t0 + tn], ALU.mult, *toks_c, V.last, q=G)
                tv = tt(v, o, tabs[0:rows, 1, t0:t0 + tn], ALU.mult, m)
                bank_free[b] = [tv]
                t = tt(zc, u, v, ALU.add, tg, tv, m)
                toks_c = [t]
            out_t = split(hi[0:rows, t0:t0 + tn], lo[0:rows, t0:t0 + tn], zc, *toks_c)
        return out_t

    def to_token_major(z, chunks_n, dst, z_toks):
        out_t = None
        PE.wait(*z_toks)
        for k0 in range(0, chunks_n, 4):
            n = min(4, chunks_n - k0)
            b = take()
            for i in range(n):
                o = PS[:, 512 * b + 128 * i:512 * b + 128 * i + 128]
                src = z[:, (k0 + i) * 128:(k0 + i) * 128 + 128]
                m = PE.op(lambda e, o=o, src=src: e.transpose(o, src, ident))
            d = dst[:, k0:k0 + n, :]
            o = PS[:, 512 * b:512 * b + 128 * n].rearrange("p (a c) -> p a c", c=128)
            out_t = V.op(lambda e, d=d, o=o: e.tensor_copy(d, o), m)
            bank_free[b] = [out_t]
        return out_t

    class Attention:

        def __init__(self, sw, width, ne):
            self.sw, self.ne = sw, ne
            self.E = [mem([P, width]) for _ in range(ne)]
            self.S = [mem([P, 8]) for _ in range(ne)]
            self.e_free = [[] for _ in range(ne)]
            self.pt = [mem([P, 512]) for _ in range(4)]
            self.pt_free = [[] for _ in range(4)]
            self.O = [mem([P, 128]) for _ in range(2)]
            self.o_free = [[], []]
            self.nf = self.ng = self.nb = self.nq = 0

        def front(self, f):
            i = self.nf
            self.nf += 1
            s0 = (i % 2) * self.sw
            n = f["n"]
            banks = list(range(s0, s0 + (n + 511) // 512))
            for b in banks:
                PE.wait(*bank_free[b])
            for c0, cn, terms in f["chunks"]:
                o = PS[:, 512 * s0 + c0:512 * s0 + c0 + cn]
                for a, (L, Rr) in enumerate(terms):
                    tok = mm3(o, L, Rr, a == 0, a == len(terms) - 1)
            e = i % self.ne
            E, S = self.E[e], self.S[e]
            V.wait(tok, self.e_free[e])
            A.wait(self.e_free[e])
            scale = f.get("scale", 1.0)
            pieces = f["pieces"]
            plain = []
            mt = []
            for a, (c0, c1, bias) in enumerate(pieces):
                src = PS[:, 512 * s0 + c0:512 * s0 + c1]
                if bias is None:
                    neg = len(pieces) == 1 and scale == 1.0
                    mt.append(V.op(lambda e_, src=src, a=a, neg=neg: e_.tensor_reduce(
                        S[:, 0:1] if neg else S[:, 1 + a:2 + a], src, AX.X, ALU.max, negate=neg)))
                    plain.append((c0, c1, src, a, None))
                else:
                    d = E[:, c0:c1]
                    t = V.op(lambda e_, d=d, src=src, bias=bias, a=a: e_.tensor_tensor_reduce(
                        d, src, bias, 1.0, OUT_OF_RANGE, ALU.add, ALU.max, S[:, 1 + a:2 + a]))
                    mt.append(t)
                    plain.append((c0, c1, d, a, t))
            nm = S[:, 0:1]
            t = mt[-1]
            if len(pieces) == 2:
                t = ts(nm, S[:, 1:2], S[:, 2:3], -scale, ALU.max, ALU.mult, *mt)
            elif not (pieces[0][2] is None and scale == 1.0):
                t = ts(nm, S[:, 1:2], -scale, None, ALU.mult, None, *mt)
            if "sink" in f:
                t = ts(nm, nm, nsink[:, f["sink"]:f["sink"] + 1], None, ALU.min, None, t)
            A.wait(t)
            et = []
            for c0, c1, src, a, tk in plain:
                et.append(act(E[:, c0:c1], src, ACT.Exp, bias=nm, scale=scale, accum_out=S[:, 3 + a:4 + a]))
            for b in banks:
                bank_free[b] = [mt[-1], et[-1]]
            rs, ss = S[:, 6:7], S[:, 3:4]
            if "sink" in f:
                ex = act(S[:, 5:6], vc("sink", f["sink"]), ACT.Exp, bias=nm)
                ss = S[:, 7:8]
                t = ts(ss, S[:, 3:4], S[:, 4:5] if len(pieces) == 2 else 0.0, S[:, 5:6], ALU.add, ALU.add, ex, *et) \
                    if len(pieces) == 2 else tt(ss, S[:, 3:4], S[:, 5:6], ALU.add, ex, *et)
            elif len(pieces) == 2:
                ss = S[:, 7:8]
                t = tt(ss, S[:, 3:4], S[:, 4:5], ALU.add, *et)
            else:
                t = et[-1]
            tr = V.op(lambda e_: e_.reciprocal(rs, ss), t, *et)
            return {"E": E, "rs": rs, "tok": [et[-1]], "tr": tr, "slot": e}

        def pt_bank(self):
            first = 2 * self.sw
            b = first + self.nb % (7 - first)
            self.nb += 1
            PE.wait(*bank_free[b])
            return b

        def back(self, u, st_):
            if u.get("lam"):
                f0, f1 = st_
                n = u["n"]
                c = f1["rs"]
                t = ts(c, c, lam_t[:, 1:2], None, ALU.mult, None, f1["tr"])
                t = ts(f1["E"][:, 0:n], f1["E"][:, 0:n], c, None, ALU.mult, None, t, f1["tok"])
                ready = [stt(f0["E"][:, 0:n], f0["E"][:, 0:n], f0["rs"], f1["E"][:, 0:n], ALU.mult, ALU.add, t,
                             f0["tr"], f0["tok"])]
                self.e_free[f1["slot"]] = [ready[0]]
                src = f0
            else:
                src = st_[0]
                ready = src["tok"]
            E = src["E"]
            PE.wait(*ready)
            kts = u["keys"]
            groups = [kts[i:i + 4] for i in range(0, len(kts), 4)]
            O = PS[:, 3584:3584 + u["dv"]]

            def turn_over(g):
                b = self.pt_bank()
                for i, (c0, _) in enumerate(g):
                    o, s = PS[:, 512 * b + 128 * i:512 * b + 128 * i + 128], E[:, c0:c0 + 128]
                    m = PE.op(lambda e, o=o, s=s: e.transpose(o, s, ident))
                p = self.ng % 4
                self.ng += 1
                d, s = self.pt[p][:, 0:128 * len(g)], PS[:, 512 * b:512 * b + 128 * len(g)]
                if self.ng % 2:
                    t = A.op(lambda e: e.copy(d, s), m, self.pt_free[p])
                else:
                    t = V.op(lambda e: e.tensor_copy(d, s), m, self.pt_free[p])
                bank_free[b] = [t]
                return p, t

            nxt = turn_over(groups[0])
            done = 0
            for gi, g in enumerate(groups):
                cur = nxt
                if gi + 1 < len(groups):
                    nxt = turn_over(groups[gi + 1])
                PE.wait(cur[1])
                if gi == 0:
                    PE.wait(*bank_free[7])
                for i, (_, v) in enumerate(g):
                    L = self.pt[cur[0]][:, 128 * i:128 * i + 128]
                    m = mm(O, L, v, done == 0, done == len(kts) - 1)
                    done += 1
                self.pt_free[cur[0]] = [m]
            ob = self.nq % 2
            d = self.O[ob][:, u["o0"]:u["o0"] + u["dv"]]
            V.wait(self.o_free[ob])
            if u.get("lam"):
                t = V.op(lambda e: e.tensor_copy(d, O), m)
            else:
                t = ts(d, O, src["rs"], None, ALU.mult, None, m, src["tr"])
            bank_free[7] = [t]
            self.e_free[src["slot"]] = [t]
            if u["last"]:
                PE.wait(t)
                b = self.pt_bank()
                o, s = PS[:, 512 * b:512 * b + 128], self.O[ob][:, :]
                m = PE.op(lambda e: e.transpose(o, s, ident))
                bank_free[b] = u["evac"](o, m)
                self.o_free[ob] = [m]
                self.nq += 1
            return m

        def run(self, units, ready):
            PE.wait(*ready)
            pend = None
            for u in units:
                st_ = [self.front(f) for f in u["fronts"]]
                if pend is not None:
                    self.back(*pend)
                pend = (u, st_)
            return self.back(*pend)

    def pair(hi, lo, p0, p1, a, n):
        return hi[p0:p1, a:a + n], lo[p0:p1, a:a + n]

    def chunks_of(n, q, kfun):
        return [(c, min(512, n - c), [(q, kfun(c, min(512, n - c)))]) for c in range(0, n, 512)]

    def y_store(j, yt, n, *waits):
        return move(y_d[j][:, 0:n], yt[:, 0:n], *waits)

    with mem:
        X = mem([P, 8, T])
        t_x = [move(X[:, :, :], xT.rearrange("k p t -> p k t"))]
        norm_split(lambda k, t0, tn: X[:, k, t0:t0 + tn], 8, cc("o1024"), CH1,
                   lambda k, c: vc("g_mix", k), None, t_x,
                   lambda k, t0, tn: Hh[:, k, t0:t0 + tn], lambda k, t0, tn: Hl[:, k, t0:t0 + tn])
        barrier()

    with mem:
        score = [mem([P, 128 * (b + 1)]) for b in range(8)]
        with mem:
            iqh, iql = [mem([P, T], R) for _ in range(2)], [mem([P, T], R) for _ in range(2)]
            ikh, ikl = mem([P, T], R), mem([P, T], R)
            z = [mem([P, T]) for _ in range(3)]
            tmp = [mem([P, 512]) for _ in range(4)]
            relu = [mem([P, T]) for _ in range(2)]
            wi = mem([P, 8, 4])
            m8 = [mem([P, 8]) for _ in range(2)]
            ev = []
            for j, name in enumerate(("iq0", "iq1", "ikw")):
                r = P if j < 2 else 68
                e_ = copy_to(lambda t0, tn, j=j, r=r: z[j][0:r, t0:t0 + tn])
                linear(name, h_rhs, CH1, e_, rows=r)
                ev.append(e_.toks)
            q_t = []
            for j in range(2):
                q_t += post(z[j], P, CH1, None, "swap32", iqh[j], iql[j], tmp, ev[j])
            PE.wait(*ev[2])
            b = take()
            for i in range(8):
                o = PS[:, 512 * b + 4 * i:512 * b + 4 * i + 4]
                s = z[2][64:68, 128 * i:128 * i + 128]
                m = PE.op(lambda e, o=o, s=s: e.transpose(o, s, ident[64:68, 64:68]))
            o = PS[:, 512 * b:512 * b + 32].rearrange("p (a c) -> p a c", c=4)
            t_w = ts(wi[:, :, :], o, 0.0625, None, ALU.mult, None, m)
            bank_free[b] = [t_w]
            k_t = post(z[2], 64, CH1, vc("ik_g"), "swap32", ikh, ikl, tmp, ev[2])
            d1 = move(ikh[64:128, :], ikh[0:64, :], *k_t)
            d2 = move(ikl[64:128, :], ikl[0:64, :], *k_t)
            PE.wait(*q_t, *k_t, d1, d2)
            r_free = [[], []]
            nr = 0
            prev = None
            t_w = [t_w]
            for b in range(2, 8):
                n = 128 * (b + 1)
                sc = score[b]
                for h in range(4):
                    p0 = 64 * (h % 2)
                    s0 = (nr % 3) * 2
                    banks = list(range(s0, s0 + (n + 511) // 512))
                    for x_ in banks:
                        PE.wait(*bank_free[x_])
                    for c0 in range(0, n, 512):
                        cn = min(512, n - c0)
                        m = mm3(PS[:, 512 * s0 + c0:512 * s0 + c0 + cn],
                                pair(iqh[h // 2], iql[h // 2], p0, p0 + 64, 128 * b, 128),
                                pair(ikh, ikl, p0, p0 + 64, c0, cn), True, True)
                    rl = relu[nr % 2][:, 0:n]
                    t = act(rl, PS[:, 512 * s0:512 * s0 + n], ACT.Relu, m, r_free[nr % 2])
                    for x_ in banks:
                        bank_free[x_] = [t]
                    if h == 0:
                        prev = ts(sc[:, :], rl, wi[:, b, 0:1], None, ALU.mult, None, t, *t_w)
                    else:
                        prev = stt(sc[:, :], rl, wi[:, b, h:h + 1], sc[:, :], ALU.mult, ALU.add, t, prev)
                    r_free[nr % 2] = [prev]
                    nr += 1
                prev = V.op(lambda e, sc=sc, n=n: e.memset(sc[0:64, n - 64:n], OUT_OF_RANGE), prev)
            barrier()
            for b0 in (2, 4, 6):
                last = {b0: None, b0 + 1: None}
                for it in range(32):
                    for b in (b0, b0 + 1):
                        sc, mx = score[b], m8[b % 2]
                        t = V.op(lambda e, mx=mx, sc=sc: e.max(mx[:, :], sc[:, :]), last[b])
                        last[b] = t
                    for b in (b0, b0 + 1):
                        sc, mx = score[b], m8[b % 2]
                        last[b] = V.op(lambda e, mx=mx, sc=sc: e.match_replace(sc[:, :], mx[:, :], sc[:, :], TAKEN),
                                       last[b])
                for b in (b0, b0 + 1):
                    sc = score[b]
                    ts(sc[:, :], sc[:, :], TAKEN, NEG, ALU.not_equal, ALU.mult, last[b])
            for b in range(2):
                n = 128 * (b + 1)
                t = V.op(lambda e, b=b: e.memset(score[b][:, :], 0.0))
                V.op(lambda e, b=b, n=n: e.memset(score[b][0:64, n - 64:n], NEG), t)
            barrier()

        def branch(kind):
            with mem:
                z = [mem([P, T]) for _ in range(3)]
                tmp = [mem([P, 512]) for _ in range(4)]
                qh, ql, kh, kl = (mem([P, T], R) for _ in range(4))
                vt = mem([P, 8, 128])
                g2 = mem([P, 1])
                if kind == "a":
                    bias = mem([P, 2, 640])
                at = Attention(2, T, 3)
                yt = z[0]
                t_g = ts(g2[:, :], vc(f"{kind}q_g"), 0.125, None, ALU.mult, None)
                for j in range(2):
                    if kind == "a":
                        t_b = move(bias[:, :, :], biasA[:, 2 * j:2 * j + 2, :])
                        V.wait(t_b)
                        for i in range(2):
                            V.op(lambda e, i=i: e.memset(bias[0:64, i, 576:640], NEG))
                            t_b = V.op(lambda e, i=i: e.memset(bias[64:128, i, 0:64], NEG))
                    evs = []
                    for i, s in enumerate("qkv"):
                        e_ = copy_to(lambda t0, tn, i=i: z[i][:, t0:t0 + tn])
                        linear(f"{kind}{s}{j}", h_rhs, CH1, e_)
                        evs.append(e_.toks)
                    sw = "swap32" if kind == "b" else None
                    r1 = post(z[0], P, CH1, g2, sw, qh, ql, tmp, evs[0] + [t_g])
                    r2 = post(z[1], P, CH1, vc(f"{kind}k_g"), sw, kh, kl, tmp, evs[1])
                    r3 = to_token_major(z[2], 8, vt, evs[2])
                    barrier()
                    units = []
                    for b in range(8):
                        k0 = 128 * max(0, b - 4) if kind == "a" else 0
                        n = 128 * (b + 1) - k0
                        for i in range(2):
                            p0 = 64 * i
                            bi = bias[:, i, 640 - n:640] if kind == "a" else score[b][:, :]
                            q = pair(qh, ql, p0, p0 + 64, 128 * b, 128)

                            def ev_y(o, m, b=b):
                                return [act(yt[:, 128 * b:128 * b + 128], o, ACT.Copy, m)]
                            units.append({
                                "fronts": [{"n": n, "pieces": [(0, n, bi)], "chunks": chunks_of(
                                    n, q, lambda c, cn, p0=p0, k0=k0: pair(kh, kl, p0, p0 + 64, k0 + c, cn))}],
                                "keys": [(128 * i_, vt[:, k0 // 128 + i_, p0:p0 + 64]) for i_ in range(n // 128)],
                                "o0": p0, "dv": 64, "last": i == 1, "evac": ev_y})
                    at.run(units, r1 + r2 + [r3])
                    y_store((0 if kind == "a" else 2) + j, yt, T, A.last)
                    barrier()

        branch("a")

        with mem:
            lw = mem([P, 4, 2, 128])
            t_l = move(lw[:, :, :, :], lruw)
            c8, nc8, sa, sb_, sc_, sd_ = (mem([P, 4]) for _ in range(6))
            lam = vc("lam", 0, 4)
            t = ts(sa[:, :], lam, -1.0, None, ALU.mult, None)
            t = tt(sb_[:, :], sa[:, :], lam, ALU.max, t)
            t1 = act(sb_[:, :], sb_[:, :], ACT.Exp, t, scale=-1.0)
            t = ts(sc_[:, :], sb_[:, :], 2.0, None, ALU.add, None, t1)
            t = V.op(lambda e: e.reciprocal(sc_[:, :], sc_[:, :]), t)
            t = tt(sb_[:, :], sb_[:, :], sc_[:, :], ALU.mult, t)
            t = tt(sc_[:, :], sb_[:, :], sb_[:, :], ALU.mult, t)
            t = ts(sd_[:, :], sc_[:, :], 1.0 / 17.0, None, ALU.mult, None, t)
            for n in (15, 13, 11, 9, 7, 5, 3):
                t = stt(sd_[:, :], sd_[:, :], 1.0 / n, sc_[:, :], ALU.add, ALU.mult, t)
            t = stt(sd_[:, :], sd_[:, :], 1.0, sb_[:, :], ALU.add, ALU.mult, t)
            t = ts(sa[:, :], sa[:, :], 0.0, None, ALU.max, None, t)
            t = stt(sd_[:, :], sd_[:, :], 2.0, sa[:, :], ALU.mult, ALU.add, t)
            t = ts(c8[:, :], sd_[:, :], -8.0, None, ALU.mult, None, t)
            t_s = [ts(nc8[:, :], sd_[:, :], 8.0, None, ALU.mult, None, t), t]
            A.wait(*t_s)
            PE.wait(t_l)
            xc = [mem([P, T + 3]) for _ in range(2)]
            gl = [mem([P, T]) for _ in range(2)]
            u, r, i_, a_, th, yc = (mem([P, T]) for _ in range(6))
            for s in range(2):
                t_z = G.op(lambda e, s=s: e.memset(xc[s][:, 0:3], 0.0))
            V.wait(t_z)
            done = [[], []]
            t_y = None
            prev_scan = None
            for c in range(4):
                s = c % 2
                A.wait(done[s])
                e1 = copy_to(lambda t0, tn: xc[s][:, 3 + t0:3 + t0 + tn])
                linear(f"cx{c}", h_rhs, CH1, e1)
                gt = []

                def ev_g(o, t0, tn, tok):
                    gt.append(act(gl[s][:, t0:t0 + tn], o, ACT.Gelu_apprx_tanh, tok))
                    return [gt[-1]]
                linear(f"cy{c}", h_rhs, CH1, ev_g)
                t = ts(u[:, :], xc[s][:, 0:T], vc("conv_w", c), vc("conv_b", c), ALU.mult, ALU.add, *e1.toks, PE.last)
                for j in range(1, 4):
                    t = stt(u[:, :], xc[s][:, j:j + T], vc("conv_w", 4 * j + c), u[:, :], ALU.mult, ALU.add, t)
                PE.wait(t)
                A.wait(prev_scan)
                for w_i, (dst, bn) in enumerate(((r, "lru_ba"), (i_, "lru_bx"))):
                    for t0, tn in CH1:
                        b = take()
                        m = mm(bank(b), lw[:, c, w_i, :], u[:, t0:t0 + tn])
                        ts_ = act(dst[:, t0:t0 + tn], bank(b), ACT.Sigmoid, m, bias=vc(bn, c))
                        bank_free[b] = [ts_]
                ta = act(a_[:, :], r[:, :], ACT.Exp, ts_, scale=c8[:, c:c + 1])
                tth = act(th[:, :], r[:, :], ACT.Tanh, scale=nc8[:, c:c + 1])
                t = tt(i_[:, :], i_[:, :], u[:, :], ALU.mult, ts_)
                t1 = tt(r[:, :], a_[:, :], a_[:, :], ALU.mult, ta, tth)
                t1 = stt(r[:, :], r[:, :], 1.0, th[:, :], ALU.add, ALU.mult, t1, tth)
                t2 = act(r[:, :], r[:, :], ACT.Sqrt, t1)
                t = tt(i_[:, :], i_[:, :], r[:, :], ALU.mult, t, t2)
                t = V.op(lambda e: e.tensor_tensor_scan(th[:, :], a_[:, :], i_[:, :], 0.0, ALU.mult, ALU.add), t, ta)
                t = tt(yc[:, :], th[:, :], gl[s][:, :], ALU.mult, t, *gt, t_y)
                prev_scan = t
                done[s] = [t]
                t_y = y_store(4 + c, yc, T, t)
            barrier()

        branch("b")

    with mem:
        Yh, Yl = mem([P, 8, T], R), mem([P, 8, T], R)
        gate = [mem([P, 512]) for _ in range(6)]
        mg = mem([P, 512])
        t1b = mem([P, 512])
        with mem:
            src_free = [[], []]
        yl2 = [gate[0], gate[3]]
        nl = 0
        for k in range(8):
            for t0, tn in CH1:
                s = yl2[nl % 2]
                t_d = move(s[:, :], y_d[k][:, t0:t0 + tn], *src_free[nl % 2])
                src_free[nl % 2] = split(Yh[:, k, t0:t0 + tn], Yl[:, k, t0:t0 + tn], s[:, :], t_d)
                nl += 1
        y_ready = list(src_free[0]) + list(src_free[1])
        A.wait(*y_ready)
        PE.wait(*y_ready)
        g_free = [[] for _ in range(6)]
        t_m = None
        for d in range(8):
            sig = {}
            for i in range(3):
                def ev_s(o, t0, tn, tok, i=i):
                    n = 2 * i + t0 // 512
                    sig[n] = act(gate[n][:, :], o, ACT.Sigmoid, tok, g_free[n], bias=vc("b_gate", 8 * i + d))
                    return [sig[n]]
                linear(f"gt{i}_{d}", h_rhs, CH1, ev_s)
            get, kt, release = w_get(f"wb{d}")
            for c, (t0, tn) in enumerate(CH1):
                last = None
                for i, (k0, k1) in enumerate(((0, 2), (2, 4), (4, 8))):
                    b = take()
                    for k in range(k0, k1):
                        m = mm3(bank(b), get(k), (Yh[:, k, t0:t0 + tn], Yl[:, k, t0:t0 + tn]), k == k0, k == k1 - 1)
                    n = 2 * i + c
                    if i == 0:
                        last = tt(mg[:, :], bank(b), gate[n][:, :], ALU.mult, m, sig[n], t_m)
                        bank_free[b] = [last]
                    else:
                        t = tt(t1b[:, :], bank(b), gate[n][:, :], ALU.mult, m, sig[n], last)
                        bank_free[b] = [t]
                        last = tt(mg[:, :], mg[:, :], t1b[:, :], ALU.add, t, last)
                    g_free[n] = [last]
                t_m = move(m_d[d][:, t0:t0 + tn], mg[:, :], last)
            release(m)
        barrier()

    def load_split(src_d, n):
        with mem:
            s = [mem([P, TC]) for _ in range(3)]
            fr = [[], [], []]
            for k in range(8):
                t_d = move(s[k % 3][:, 0:n], src_d[k][:, 0:n], *fr[k % 3])
                fr[k % 3] = split(Hh[:, k, 0:n], Hl[:, k, 0:n], s[k % 3][:, 0:n], t_d)
        return [t for f in fr for t in f]

    with mem:
        X = mem([P, 8, TC])
        t_x = [move(X[:, :, 0:T], xT.rearrange("k p t -> p k t")),
               move(X[:, :, T:TC], ctxT.rearrange("k p t -> p k t"))]
        PE.wait(*load_split(m_d, T))
        V.wait(*t_x)

        def add_to(d):
            def evac(o, t0, tn, tok):
                return [tt(X[:, d, t0:t0 + tn], X[:, d, t0:t0 + tn], o, ALU.add, tok)]
            return evac

        for d in range(8):
            linear(f"wo{d}", h_rhs, CH1, add_to(d))
        barrier()
        norm_split(lambda k, t0, tn: X[:, k, t0:t0 + tn], 8, cc("o1024"), CH1,
                   lambda k, c: vc("g_ffn", k), None, [],
                   lambda k, t0, tn: Hh[:, k, t0:t0 + tn], lambda k, t0, tn: Hl[:, k, t0:t0 + tn])
        barrier()
        with mem:
            GM = max(FFN_GROUPS)
            uh, ul = mem([P, GM, T], R), mem([P, GM, T], R)
            sg = [mem([P, 512]) for _ in range(2)]
            sg_free = [[], []]
            f0 = 0
            for n, g in enumerate(FFN_GROUPS):
                fin_t = []
                for f in range(g):
                    sil = {}

                    def ev_g(o, t0, tn, tok):
                        c = t0 // 512
                        sil[c] = act(sg[c][:, :], o, ACT.Silu, tok, sg_free[c])
                        return [sil[c]]

                    def ev_u(o, t0, tn, tok):
                        c = t0 // 512
                        t = tt(sg[c][:, :], sg[c][:, :], o, ALU.mult, tok, sil[c])
                        sg_free[c] = split(uh[:, f, t0:t0 + tn], ul[:, f, t0:t0 + tn], sg[c][:, :], t)
                        return [t]
                    if f == 0:
                        A.wait(PE.last)
                        V.wait(PE.last)
                    linear(f"fg{f0 + f}", h_rhs, CH1, ev_g)
                    linear(f"fu{f0 + f}", h_rhs, CH1, ev_u)
                    fin_t = [sg_free[0], sg_free[1]]
                PE.wait(*fin_t)
                for d in range(8):
                    linear(f"fo{n}_{d}", lambda k, t0, tn: (uh[:, k, t0:t0 + tn], ul[:, k, t0:t0 + tn]), CH1,
                           add_to(d))
                f0 += g
        barrier()
        move(x1_d.rearrange("k p t -> p k t"), X[:, :, 0:T])

        def modulation(kind):
            t = act(csil[:, :], vc("cond", 0, 16), ACT.Silu)
            PE.wait(t)
            b = take()
            for m_ in range(24):
                get, kt, release = w_get(f"{'ea' if kind == 'ev' else 'oa'}{m_}")
                for k in range(8):
                    m = mm(PS[:, 512 * b + 2 * m_:512 * b + 2 * m_ + 2], get(k), csil[:, 2 * k:2 * k + 2],
                           k == 0, k == 7)
                release(m)
            o = PS[:, 512 * b:512 * b + 48].rearrange("p (a c) -> p a c", c=2)
            bb = vc(f"{kind}_b", 0, 24).rearrange("p (a c) -> p a c", c=1).to_broadcast([P, 24, 2])
            t = tt(mod[:, :, :], o, bb, ALU.add, m)
            bank_free[b] = [t]
            for s in range(2):
                t2 = stt(gs[:, :, s], mod[:, 8:16, s], 1.0, vc(f"{kind}_g", 0, 8), ALU.add, ALU.mult, t)
            return [t, t2]

        def cond_of(c):
            return 1 if c == 2 else 0

        barrier()
        t_m = modulation("ev")
        A.wait(*t_m)
        norm_split(lambda k, t0, tn: X[:, k, t0:t0 + tn], 8, cc("o1024"), CH2,
                   lambda k, c: gs[:, k, cond_of(c):cond_of(c) + 1],
                   lambda k, c: mod[:, k, cond_of(c):cond_of(c) + 1], t_m,
                   lambda k, t0, tn: Hh[:, k, t0:t0 + tn], lambda k, t0, tn: Hl[:, k, t0:t0 + tn])
        barrier()

    t_tab = move(tabs[:, :, :], tab_d[1].rearrange("a p t -> p a t"))
    for q in (A, V, G):
        q.wait(t_tab)
    with mem:
        ld = mem([P, 64])
        bl = [vc("blam", 64 * i, 64) for i in range(4)]
        t = None
        for i in range(2):
            t = V.op(lambda e, i=i: e.tensor_tensor_reduce(ld[:, :], bl[2 * i], bl[2 * i + 1], 1.0, 0.0, ALU.mult,
                                                           ALU.add, lam_t[:, 2 + i:3 + i]), t)
        t = act(lam_t[:, 4:6], lam_t[:, 2:4], ACT.Exp, t)
        t = tt(lam_t[:, 0:1], lam_t[:, 4:5], lam_t[:, 5:6], ALU.subtract, t)
        t = ts(lam_t[:, 1:2], lam_t[:, 0:1], 0.8 - 0.6, -1.0, ALU.add, ALU.mult, t)
        t = ts(nsink[:, :], vc("sink", 0, 8), -1.0, None, ALU.mult, None, t)
        barrier()

    def gate_evac(gt, n=TC):
        toks = []

        def evac(o, t0, tn, tok):
            toks.append(act(gt[:, t0:t0 + tn], o, ACT.Silu, tok))
            return [toks[-1]]
        evac.toks = toks
        return evac

    def gated(yt, gt, b):
        def evac(o, m):
            s = slice(128 * b, 128 * b + 128)
            return [tt(yt[:, s], o, gt[:, s], ALU.mult, m)]
        return evac

    with mem:
        zq, zk = mem([P, TC]), mem([P, TC])
        tmp = [mem([P, 512]) for _ in range(4)]
        qh, ql, kh, kl = (mem([P, TC], R) for _ in range(4))
        vt = mem([P, 10, 128])
        gt = mem([P, TC])
        at = Attention(2, 640, 3)
        yt = zq
        for j in range(4):
            kv = j // 2
            eq = copy_to(lambda t0, tn: zq[:, t0:t0 + tn], 0.125)
            linear(f"eq{j}", h_rhs, CH2, eq)
            ready = []
            if j % 2 == 0:
                ek = copy_to(lambda t0, tn: zk[:, t0:t0 + tn])
                linear(f"ek{kv}", h_rhs, CH2, ek)
            ready += post(zq, P, CH2, None, "swap16", qh, ql, tmp, eq.toks)
            if j % 2 == 0:
                ready += post(zk, P, CH2, None, "swap16", kh, kl, tmp, ek.toks)
            if j == 0:
                e_ = copy_to(lambda t0, tn: zk[:, t0:t0 + tn])
                A.wait(*ready)
                linear("ev", h_rhs, CH2, e_)
                ready.append(to_token_major(zk, 10, vt, e_.toks))
            eg = gate_evac(gt)
            linear(f"eg{j}", h_rhs, CH2, eg)
            barrier()
            units = []
            for b in range(10):
                for i in range(2):
                    p0 = 64 * i
                    q = pair(qh, ql, p0, p0 + 64, 128 * b, 128)
                    if b < 8:
                        k0, k1 = 128 * max(0, b - 1), 128 * min(8, b + 2)
                        n1 = k1 - k0
                        m0 = 128 if b == 0 else 0
                        mask = cst[:, C_AT["win"][0] + m0:C_AT["win"][0] + m0 + n1]
                        n = n1 + 256
                        c1 = min(256, 512 - n1)
                        chunks = [(0, n1, [(q, pair(kh, kl, p0, p0 + 64, k0, n1))]),
                                  (n1, c1, [(q, pair(kh, kl, p0, p0 + 64, T, c1))])]
                        if c1 < 256:
                            chunks.append((512, 256 - c1, [(q, pair(kh, kl, p0, p0 + 64, T + c1, 256 - c1))]))
                        pieces = [(0, n1, mask), (n1, n, None)]
                        kt = list(range(k0 // 128, k1 // 128)) + [8, 9]
                    else:
                        n = 256
                        chunks = [(0, 256, [(q, pair(kh, kl, p0, p0 + 64, T, 256))])]
                        pieces = [(0, 256, None)]
                        kt = [8, 9]
                    units.append({"fronts": [{"n": n, "pieces": pieces, "chunks": chunks, "sink": 2 * j + i}],
                                  "keys": [(128 * x_, vt[:, y_, 64 * kv:64 * kv + 64]) for x_, y_ in enumerate(kt)],
                                  "o0": p0, "dv": 64, "last": i == 1, "evac": gated(yt, gt, b)})
            at.run(units, ready)
            y_store(j, yt, TC, V.last)
            barrier()

    with mem:
        zq, zk = mem([P, TC]), mem([P, TC])
        qh, ql, kh, kl = (mem([P, TC], R) for _ in range(4))
        vt = mem([P, 10, 128])
        gt = zk
        g8 = mem([P, 1])
        at = Attention(3, TC, 4)
        tmp = [x[:, 0:512] for x in at.E]
        yt = zq
        t_g8 = ts(g8[:, :], vc("subln"), 1.0 - (0.8 - 0.6), None, ALU.mult, None)
        for h in range(4):
            eq = copy_to(lambda t0, tn: zq[:, t0:t0 + tn], 0.125)
            linear(f"fq{h}", h_rhs, CH2, eq)
            ek = copy_to(lambda t0, tn: zk[:, t0:t0 + tn])
            linear(f"fk{h}", h_rhs, CH2, ek)
            r1 = post(zq, P, CH2, None, "swap16", qh, ql, tmp, eq.toks)
            r2 = post(zk, P, CH2, None, "swap16", kh, kl, tmp, ek.toks)
            A.wait(*r1)
            e_ = copy_to(lambda t0, tn: zq[:, t0:t0 + tn])
            linear(f"fv{h}", h_rhs, CH2, e_)
            r3 = to_token_major(zq, 10, vt, e_.toks)
            A.wait(*r2)
            eg = gate_evac(gt)
            linear(f"eg{4 + h}", h_rhs, CH2, eg)
            barrier()
            units = []
            for b in range(10):
                n, k0 = (TC, 0) if b < 8 else (256, T)
                fronts = []
                for i in range(2):
                    p0 = 64 * i
                    q = pair(qh, ql, p0, p0 + 64, 128 * b, 128)
                    fronts.append({"n": n, "pieces": [(0, n, None)], "chunks": chunks_of(
                        n, q, lambda c, cn, p0=p0, k0=k0: pair(kh, kl, p0, p0 + 64, k0 + c, cn))})

                def ev_y(o, m, b=b):
                    return [act(yt[:, 128 * b:128 * b + 128], o, ACT.Copy, m)]
                units.append({"fronts": fronts, "lam": True, "n": n,
                              "keys": [(128 * x_, vt[:, k0 // 128 + x_, :]) for x_ in range(n // 128)],
                              "o0": 0, "dv": 128, "last": True, "evac": ev_y})
            at.run(units, r1 + r2 + [r3])
            barrier()
            for t0, tn in CH2:
                yc, s, r = yt[:, t0:t0 + tn], tmp[0][:, 0:tn], tmp[1][:, 0:tn]
                t = act(s, yc, ACT.Square, V.last)
                PE.wait(t)
                b = take()
                m = mm(bank(b)[:, 0:tn], cc("o128"), s)
                t, ta = root(r, bank(b)[:, 0:tn], m)
                bank_free[b] = [ta]
                t = stt(yc, yc, g8[:, 0:1], r, ALU.mult, ALU.mult, t)
                t = tt(yc, yc, gt[:, t0:t0 + tn], ALU.mult, t)
            y_store(4 + h, yt, TC, t)
            barrier()

    with mem:
        X = mem([P, 8, TC])
        t_x = [move(X[:, :, 0:T], x1_d.rearrange("k p t -> p k t")),
               move(X[:, :, T:TC], ctxT.rearrange("k p t -> p k t"))]
        PE.wait(*load_split(y_d, TC))
        V.wait(*t_x)

        def add_gated(d):
            def evac(o, t0, tn, tok):
                s = 1 if t0 >= T else 0
                return [stt(X[:, d, t0:t0 + tn], o, mod[:, 16 + d, s:s + 1], X[:, d, t0:t0 + tn], ALU.mult, ALU.add,
                            tok)]
            return evac

        for d in range(8):
            linear(f"eo{d}", h_rhs, CH2, add_gated(d))
        barrier()
        move(x1_d.rearrange("k p t -> p k t"), X[:, :, 0:T])
        t_m = modulation("od")
        A.wait(*t_m)
        norm_split(lambda k, t0, tn: X[:, k, t0:t0 + tn], 8, cc("o1024"), CH2,
                   lambda k, c: gs[:, k, cond_of(c):cond_of(c) + 1],
                   lambda k, c: mod[:, k, cond_of(c):cond_of(c) + 1], t_m,
                   lambda k, t0, tn: Hh[:, k, t0:t0 + tn], lambda k, t0, tn: Hl[:, k, t0:t0 + tn])
        barrier()

    with mem:
        zq, zk = mem([P, T]), mem([P, TC])
        qh, ql = mem([P, T], R), mem([P, T], R)
        kh, kl = mem([P, TC], R), mem([P, TC], R)
        vt = mem([P, 10, 128])
        gt = mem([P, T])
        bt = [mem([P, 14, 64]) for _ in range(2)]
        bi = [mem([P, 640]) for _ in range(2)]
        at = Attention(2, 896, 3)
        yt = zq
        START = {0: (0, 7), 1: (0, 5), 6: (8, 3), 7: (8, 1)}
        for j in range(4):
            t_b = []
            for i in range(2):
                t = move(bt[i][:, :, :], biasD[2 * j + i])
                cm = cc("col").rearrange("p (a c) -> p a c", a=1).to_broadcast([P, 14, 64])
                t = tt(bt[i][:, :, :], bt[i][:, :, :], cm, ALU.add, t, q=G)
                t = V.op(lambda e, i=i: e.tensor_copy(bi[i][:, :], bt[i][:, 2:12, :].rearrange("p a c -> p (a c)")), t)
                for rows, c0, c1 in (((0, 64), 512, 640), ((64, 128), 0, 64), ((64, 128), 576, 640)):
                    t = V.op(lambda e, i=i, rows=rows, c0=c0, c1=c1: e.memset(bi[i][rows[0]:rows[1], c0:c1], NEG), t)
                t_b.append(t)
            V.wait(*t_b)

            def ev_q(o, t0, tn, tok):
                d = zq[:, t0:t0 + tn]
                t = A.op(lambda e: e.mul(d, o, 0.125), tok)
                q_t.extend(split(qh[:, t0:t0 + tn], ql[:, t0:t0 + tn], zq[:, t0:t0 + tn], t))
                return [t]
            q_t = []
            linear(f"dq{j}", h_rhs, CH1, ev_q)
            k_t = []

            def ev_k(o, t0, tn, tok):
                t = split(kh[:, t0:t0 + tn], kl[:, t0:t0 + tn], o, tok)
                k_t.extend(t)
                return t
            linear(f"dk{j}", h_rhs, CH2, ev_k)
            e_ = copy_to(lambda t0, tn: zk[:, t0:t0 + tn])
            linear(f"dv{j}", h_rhs, CH2, e_)
            r3 = to_token_major(zk, 10, vt, e_.toks)
            eg = gate_evac(gt)
            linear(f"og{4 + j}", h_rhs, CH1, eg)
            barrier()
            units = []
            for b in range(8):
                inner = 2 <= b <= 5
                ws = 2 * b - 4 if inner else START[b][0]
                nl = 640 if inner else 512
                for i in range(2):
                    p0 = 64 * i
                    if inner:
                        bias = bi[i][:, :]
                    else:
                        v0 = START[b][1] - 1
                        bias = bt[i][:, v0:v0 + 8, :].rearrange("p a c -> p (a c)")
                    q = pair(qh, ql, p0, p0 + 64, 128 * b, 128)
                    k0 = 64 * ws
                    n = nl + 256
                    chunks = [(0, 512, [(q, pair(kh, kl, p0, p0 + 64, k0, 512))])]
                    if inner:
                        chunks.append((512, 128, [(q, pair(kh, kl, p0, p0 + 64, k0 + 512, 128))]))
                    chunks.append((nl, 256, [(q, pair(kh, kl, p0, p0 + 64, T, 256))]))
                    kt = list(range(k0 // 128, (k0 + nl) // 128)) + [8, 9]
                    units.append({"fronts": [{"n": n, "pieces": [(0, nl, bias), (nl, n, None)], "chunks": chunks}],
                                  "keys": [(128 * x_, vt[:, y_, p0:p0 + 64]) for x_, y_ in enumerate(kt)],
                                  "o0": p0, "dv": 64, "last": i == 1, "evac": gated(yt, gt, b)})
            at.run(units, q_t + k_t + [r3])
            y_store(4 + j, yt, T, V.last)
            barrier()

    SC = 192.0 ** -0.5
    with mem:
        cqh, cql = mem([P, 2, T], R), mem([P, 2, T], R)
        ckh, ckl = mem([P, TC], R), mem([P, TC], R)
        rph, rpl = mem([P, TC], R), mem([P, TC], R)
        gts = [mem([P, T]) for _ in range(4)]
        with mem:
            zc = mem([P, 2, T])
            zk, zr = mem([P, TC]), mem([P, TC])
            tmp = [mem([P, 512]) for _ in range(4)]
            evs = []
            for j in range(2):
                e_ = copy_to(lambda t0, tn, j=j: zc[:, j, t0:t0 + tn])
                linear(f"cq{j}", h_rhs, CH1, e_)
                evs += e_.toks
            ek = copy_to(lambda t0, tn: zk[:, t0:t0 + tn])
            linear("ckv", h_rhs, CH2, ek)
            er = copy_to(lambda t0, tn: zr[:, t0:t0 + tn])
            linear("ckr", h_rhs, CH2, er)
            half = [g[:, a:a + 512] for g in gts for a in (0, 512)]
            norm_split(lambda k, t0, tn: zc[:, k, t0:t0 + tn], 2, cc("o256"), CH1,
                       lambda k, c: vc("qn_g", k), None, evs,
                       lambda k, t0, tn: cqh[:, k, t0:t0 + tn], lambda k, t0, tn: cql[:, k, t0:t0 + tn], half)
            barrier()
            norm_split(lambda k, t0, tn: zk[:, t0:t0 + tn], 1, cc("o128"), CH2,
                       lambda k, c: vc("kvn_g"), None, ek.toks,
                       lambda k, t0, tn: ckh[:, t0:t0 + tn], lambda k, t0, tn: ckl[:, t0:t0 + tn], half)
            post(zr, P, CH2, None, "swap16", rph, rpl, tmp, er.toks)
            barrier()
            for h in range(4):
                linear(f"og{h}", h_rhs, CH1, gate_evac(gts[h]))
            barrier()
        with mem.over(h_at):
            zq = mem([P, TC])
            tmp = [mem([P, 512]) for _ in range(4)]
            qnh, qnl = mem([P, T], R), mem([P, T], R)
            qph, qpl = mem([P, T], R), mem([P, T], R)
            knh, knl = mem([P, TC], R), mem([P, TC], R)
            vt = mem([P, 10, 128])
            at = Attention(3, TC, 2)
            yt = zq

            def q_rhs(k, t0, tn):
                return cqh[:, k, t0:t0 + tn], cql[:, k, t0:t0 + tn]

            def kv_rhs(k, t0, tn):
                return ckh[:, t0:t0 + tn], ckl[:, t0:t0 + tn]

            def ev_split(hi, lo):
                toks = []

                def evac(o, t0, tn, tok):
                    t = split(hi[:, t0:t0 + tn], lo[:, t0:t0 + tn], o, tok)
                    toks.extend(t)
                    return t
                evac.toks = toks
                return evac

            for h in range(4):
                ready = []
                if h % 2 == 0:
                    e_ = copy_to(lambda t0, tn: zq[:, t0:t0 + tn])
                    linear(f"qp{h // 2}", q_rhs, CH1, e_)
                    ready += post(zq, P, CH1, None, "swap16", qph, qpl, tmp, e_.toks)
                e1 = ev_split(qnh, qnl)
                linear(f"qn{h}", q_rhs, CH1, e1)
                e2 = ev_split(knh, knl)
                linear(f"kn{h}", kv_rhs, CH2, e2)
                A.wait(*ready)
                e3 = copy_to(lambda t0, tn: zq[:, t0:t0 + tn])
                linear(f"vn{h}", kv_rhs, CH2, e3)
                ready.append(to_token_major(zq, 10, vt, e3.toks))
                barrier()
                p0 = 64 * (h % 2)
                units = []
                for b in range(8):
                    chunks = []
                    for c in range(0, TC, 512):
                        cn = min(512, TC - c)
                        chunks.append((c, cn, [
                            (pair(qnh, qnl, 0, P, 128 * b, 128), pair(knh, knl, 0, P, c, cn)),
                            (pair(qph, qpl, p0, p0 + 64, 128 * b, 128), pair(rph, rpl, p0, p0 + 64, c, cn))]))
                    units.append({"fronts": [{"n": TC, "pieces": [(0, TC, None)], "chunks": chunks, "scale": SC}],
                                  "keys": [(128 * x_, vt[:, x_, :]) for x_ in range(10)],
                                  "o0": 0, "dv": 128, "last": True, "evac": gated(yt, gts[h], b)})
                at.run(units, ready + e1.toks + e2.toks)
                y_store(h, yt, T, V.last)
                barrier()

    with mem:
        X = mem([P, 8, T])
        t_x = [move(X[:, :, :], x1_d.rearrange("k p t -> p k t"))]
        PE.wait(*load_split(y_d, T))
        V.wait(*t_x)
        for d in range(8):
            linear(f"oo{d}", h_rhs, CH1, add_gated(d))
        barrier()
        sq = [mem([P, 512]) for _ in range(2)]
        rs = [mem([P, 512]) for _ in range(2)]
        n, sq_free = 0, [[], []]
        for c, (t0, tn) in enumerate(CH1):
            b = take()
            for k in range(8):
                s = sq[n % 2]
                t = act(s[:, :], X[:, k, t0:t0 + tn], ACT.Square, sq_free[n % 2])
                PE.wait(t)
                m = mm(bank(b), cc("o1024"), s[:, :], k == 0, k == 7)
                sq_free[n % 2] = [m]
                n += 1
            t, ta = root(rs[c][:, :], bank(b), m)
            bank_free[b] = [ta]
            for k in range(8):
                t1 = stt(X[:, k, t0:t0 + tn], X[:, k, t0:t0 + tn], vc("fin_g", k), rs[c][:, :], ALU.mult, ALU.mult, t)
        s_out = Slot(sem("s_out"))
        t_o = SP.dma(out.rearrange("k p t -> p k t"), X[:, :, :], s_out, t1)
        SP.wait(t_o)
        barrier()

    queues = (PE, A, V, G, SP)
    for q in queues:
        q.number()
    with nc.Block() as block:
        @block.tensor
        def _(e):
            PE.emit(e)

        @block.scalar
        def _(e):
            A.emit(e)

        @block.vector
        def _(e):
            V.emit(e)

        @block.gpsimd
        def _(e):
            G.emit(e)

        @block.sync
        def _(e):
            SP.emit(e)




def columns(v):
    return np.ascontiguousarray(np.asarray(v).reshape(-1, P).T)


def constants():
    p = np.arange(P)
    out = {"ident": np.eye(P)}
    for n in (1024, 256, 128):
        out[f"o{n}"] = np.full((P, P), 1.0 / n)
    out["o64"] = (p[:, None] // 64 == p[None, :] // 64) / 64.0
    out["swap32"] = (p[:, None] == (p ^ 32)[None, :]) * 1.0
    out["swap16"] = (p[:, None] == (p ^ 16)[None, :]) * 1.0
    j = np.arange(384)
    out["win"] = np.where(np.abs(p[:, None] - j[None, :] + 128) <= 128, 0.0, NEG)
    c = np.arange(64)
    cs = np.clip(p % 64 - 8, 0, 48)[:, None]
    out["col"] = np.where((c[None, :] >= cs) & (c[None, :] < cs + 16), 0.0, NEG)
    cst = np.concatenate([out[n] for n, _ in CONSTS], axis=1).astype(np.float32)

    f = np.float32
    e = np.arange(0, 64, 2, dtype=f) / f(64)
    inv = f(1) / (10000.0 ** e.astype(np.float64)).astype(f)
    t = np.arange(T)
    ang = (t.astype(f)[:, None] * inv[None, :]).astype(f)
    ang1 = np.concatenate([ang, ang], axis=1)
    inv2 = (10000.0 ** (-np.arange(16) / 16)).astype(f)
    ar = ((t // 64).astype(f)[:, None] * inv2[None, :]).astype(f)
    ac = ((t % 64).astype(f)[:, None] * inv2[None, :]).astype(f)
    ang2 = np.concatenate([ar, ar, ac, ac], axis=1)
    d = np.arange(64)
    tabs = []
    for a, sign in ((ang1, np.where(d % 64 < 32, -1.0, 1.0)), (ang2, np.where(d % 32 < 16, -1.0, 1.0))):
        a = a.astype(np.float64)
        tabs.append([np.tile(np.cos(a).T, (2, 1)), np.tile((np.sin(a) * sign[None, :]).T, (2, 1))])
    return cst, np.array(tabs).astype(f)


def layout(inp):
    i = {k: np.asarray(v) for k, v in inp.items()}
    wi = i["w_in"][0]
    cuts = np.cumsum([256] * 6 + [256, 64, 4, 512, 512])
    aq, ak, av, bq, bk, bv, iq, ik, iw, cx, cy, gtw = np.split(wi, cuts, axis=1)
    ev = np.split(i["ev_w_in_2"][0], np.cumsum([512, 128, 128, 512, 512, 512]), axis=1)
    od = np.split(i["od_w_in_2"][0], np.cumsum([256, 128, 64, 512, 512, 512]), axis=1)
    wqb = i["od_c_w_qb_2"][0].reshape(256, 4, 192)
    wkv = i["od_c_w_kvb_2"][0].reshape(128, 4, 256)
    fi, fo = i["w_ffn_in"][0], i["w_ffn_out"][0]
    DFF = fo.shape[0]
    parts = {}

    def cols(a, j):
        return a[:, 128 * j:128 * j + 128]

    for j in range(2):
        for n, a in (("iq", iq), ("aq", aq), ("ak", ak), ("av", av), ("bq", bq), ("bk", bk), ("bv", bv)):
            parts[f"{n}{j}"] = cols(a, j)
        k_ = ev[1][:, 64 * j:64 * j + 64]
        parts[f"ek{j}"] = np.concatenate([k_, k_], axis=1)
        parts[f"qp{j}"] = wqb[:, 2 * j:2 * j + 2, 128:].reshape(256, 128)
        parts[f"cq{j}"] = cols(od[0], j)
    parts["ikw"] = np.concatenate([ik, iw], axis=1)
    parts["ev"] = ev[2]
    parts["ckv"] = od[1]
    parts["ckr"] = np.concatenate([od[2], od[2]], axis=1)
    for j in range(4):
        for n, a in (("cx", cx), ("cy", cy), ("eq", ev[0]), ("fq", ev[3]), ("fk", ev[4]), ("fv", ev[5]),
                     ("dq", od[3]), ("dk", od[4]), ("dv", od[5])):
            parts[f"{n}{j}"] = cols(a, j)
        parts[f"qn{j}"] = wqb[:, j, :128]
        parts[f"kn{j}"] = wkv[:, j, :128]
        parts[f"vn{j}"] = wkv[:, j, 128:]
    for d in range(8):
        for n in range(3):
            parts[f"gt{n}_{d}"] = cols(gtw, 8 * n + d)
        for n, a in (("wb", i["w_branch"][0]), ("wo", i["w_out"][0]), ("eo", i["ev_w_out_2"][0]),
                     ("oo", i["od_w_out_2"][0]), ("eg", ev[6]), ("og", od[6])):
            parts[f"{n}{d}"] = cols(a, d)
        f0 = 0
        for n, g in enumerate(FFN_GROUPS):
            parts[f"fo{n}_{d}"] = fo[128 * f0:128 * (f0 + g), 128 * d:128 * d + 128]
            f0 += g
    for f in range(DFF // 128):
        parts[f"fg{f}"] = cols(fi, f)
        parts[f"fu{f}"] = cols(fi[:, DFF:], f)
    for m in range(24):
        parts[f"ea{m}"] = cols(i["ev_w_ada_2"][0], m)
        parts[f"oa{m}"] = cols(i["od_w_ada_2"][0], m)
    at, total = weight_offsets()
    w = np.empty(total, np.float32)
    for name, (a, kt, m) in at.items():
        w[a:a + P * kt * m] = parts[name].reshape(kt, P, m).transpose(1, 0, 2).reshape(-1)

    def two(v):
        return np.concatenate([v, v])[:, None]

    vecs = {
        "g_mix": columns(i["g_mix"][0]), "aq_g": two(i["qk_gain_a"][0, 0]), "ak_g": two(i["qk_gain_a"][0, 1]),
        "bq_g": two(i["qk_gain_b"][0, 0]), "bk_g": two(i["qk_gain_b"][0, 1]), "ik_g": two(i["g_idx_k"][0]),
        "conv_w": np.concatenate([columns(i["conv_w"][0, j]) for j in range(4)], axis=1),
        "conv_b": columns(i["conv_b"][0]), "lru_ba": columns(i["lru_ba"][0]), "lru_bx": columns(i["lru_bx"][0]),
        "lam": columns(i["lru_lambda"][0]), "b_gate": columns(i["b_gate"][0]), "g_ffn": columns(i["g_ffn"][0]),
        "ev_g": columns(i["ev_norm_g_2"][0]), "ev_b": columns(i["ev_b_ada_2"][0]),
        "sink": np.broadcast_to(i["ev_a_sink_2"][0], (P, 8)),
        "blam": np.broadcast_to(i["ev_b_lambda_2"][0].reshape(1, 256), (P, 256)),
        "subln": i["ev_b_subln_g_2"][0][:, None], "od_g": columns(i["od_norm_g_2"][0]),
        "od_b": columns(i["od_b_ada_2"][0]), "qn_g": columns(i["od_c_q_norm_g_2"][0]),
        "kvn_g": columns(i["od_c_kv_norm_g_2"][0]), "fin_g": columns(i["final_norm_g_2"]),
        "cond": np.stack([columns(i["c_2"][0]), columns(i["c_ctx_2"])], axis=2).reshape(P, 16),
    }
    vec = np.concatenate([vecs[n] for n, _ in VECS], axis=1).astype(np.float32)
    cst, tabs = constants()
    xT = np.ascontiguousarray(i["x"][0].T).reshape(8, P, T)
    ctxT = np.ascontiguousarray(i["ctx_2"][0].T).reshape(8, P, 256)
    p, j = np.arange(P)[:, None], np.arange(640)[None, :]
    biasA = np.ascontiguousarray(i["rel_bias"][0][:, np.clip(512 + p - j, -128, 128) + 128].transpose(1, 0, 2))
    dc = np.clip(np.arange(64)[None, :] - (np.arange(P) % 64)[:, None] + 15, 0, 30)
    v = np.arange(1, 15)[None, :] - (np.arange(P) >= 64)[:, None]
    biasD = np.ascontiguousarray(i["od_d_rpb_2"][0][:, v[:, :, None], dc[:, None, :]])
    lru = np.zeros((P, 4, 2, P), np.float32)
    for n, a in enumerate((i["lru_wa"][0], i["lru_wx"][0])):
        for g in range(8):
            o = 64 * (g % 2)
            lru[o:o + 64, g // 2, n, o:o + 64] = a[g]
    return {"w": w, "vec": vec, "cst": cst, "tab": tabs, "xT": xT, "ctxT": ctxT, "biasA": biasA, "biasD": biasD,
            "lru": lru}


def kernel(**inputs):
    import concourse.bacc as _bacc
    from concourse.bass_utils import run_bass_kernel_spmd as _run

    arrays = layout(inputs)
    nc = _bacc.Bacc("TRN2", target_bir_lowering=False, num_devices=1)
    feed, args = {}, []
    for name, a in arrays.items():
        feed[f"in_{name}"] = np.ascontiguousarray(a)
        args.append(nc.dram_tensor(f"in_{name}", a.shape, F, kind="ExternalInput").ap())
    out = nc.dram_tensor("out_0", (8, P, T), F, kind="ExternalOutput").ap()
    build(nc, *args, out)
    r = _run(nc, [feed], core_ids=[0])
    got = r.results[0]["out_0"]
    return np.ascontiguousarray(np.asarray(got).reshape(1024, T).T).reshape(1, T, 1024)
```

```python
import numpy as np
import concourse.bass as bass
from concourse import mybir

F = mybir.dt.float32
R = mybir.dt.float32r
ACT = mybir.ActivationFunctionType
ALU = mybir.AluOpType
AX = mybir.AxisListType

P = 128
T = 1024
TC = 1280
EPS = 1e-6
NEG = -1e30
OUT_OF_RANGE = -3.0e38
TAKEN = -3.3e38
SOFT2_AT = 1
FFN_GROUPS = [5, 5, 4, 4, 4]
CH1 = [(0, 512), (512, 512)]
CH2 = [(0, 512), (512, 512), (1024, 256)]



def weight_tiles():
    tiles = [("iq0", 8, 128), ("iq1", 8, 128), ("ikw", 8, 68)]
    for j in range(4):
        tiles += [(f"cx{j}", 8, 128), (f"cy{j}", 8, 128)]
    tiles += [(f"gt{i}_{d}", 8, 128) for d in range(8) for i in range(3)]
    tiles += [(f"{x}{m}", 8, 128) for x in ("ea", "oa") for m in range(24)]
    tiles += [("aq0", 8, 128), ("ak0", 8, 128)]
    pairs = ["a0", "a1", "b0", "b1"]
    for n, x in enumerate(pairs):
        tiles += [(f"{x[0]}v{x[1]}", 8, 128)]
        if n < 3:
            tiles += [(f"{pairs[n + 1][0]}{s}{pairs[n + 1][1]}", 8, 128) for s in "qk"]
    for d in range(8):
        tiles += [(f"wb{d}", 8, 128)]
    tiles += [(f"wo{d}", 8, 128) for d in range(8)]
    f0 = 0
    for n, g in enumerate(FFN_GROUPS):
        for f in range(f0, f0 + g):
            tiles += [(f"fg{f}", 8, 128), (f"fu{f}", 8, 128)]
        tiles += [(f"fo{n}_{d}", g, 128) for d in range(8)]
        f0 += g
    tiles += [("eq0", 8, 128), ("ek0", 8, 128), ("ev", 8, 128)]
    for j in range(4):
        tiles += [(f"eg{j}", 8, 128)]
        if j < 3:
            tiles += [(f"eq{j + 1}", 8, 128)]
        if j == 1:
            tiles += [("ek1", 8, 128)]
    tiles += [("fq0", 8, 128), ("fk0", 8, 128)]
    for h in range(4):
        tiles += [(f"fv{h}", 8, 128), (f"eg{4 + h}", 8, 128)]
        if h < 3:
            tiles += [(f"fq{h + 1}", 8, 128), (f"fk{h + 1}", 8, 128)]
    tiles += [(f"eo{d}", 8, 128) for d in range(8)]
    tiles += [("dq0", 8, 128), ("dk0", 8, 128)]
    for j in range(4):
        tiles += [(f"dv{j}", 8, 128), (f"og{4 + j}", 8, 128)]
        if j < 3:
            tiles += [(f"dq{j + 1}", 8, 128), (f"dk{j + 1}", 8, 128)]
    tiles += [("cq0", 8, 128), ("cq1", 8, 128), ("ckv", 8, 128), ("ckr", 8, 128)]
    tiles += [(f"og{h}", 8, 128) for h in range(4)]
    for h in range(4):
        if h % 2 == 0:
            tiles += [(f"qp{h // 2}", 2, 128)]
        tiles += [(f"qn{h}", 2, 128), (f"kn{h}", 1, 128), (f"vn{h}", 1, 128)]
    tiles += [(f"oo{d}", 8, 128) for d in range(8)]
    return tiles


def weight_offsets():
    at, out = 0, {}
    for name, kt, m in weight_tiles():
        out[name] = (at, kt, m)
        at += P * kt * m
    return out, at


VECS = [("g_mix", 8), ("aq_g", 1), ("ak_g", 1), ("bq_g", 1), ("bk_g", 1), ("ik_g", 1), ("conv_w", 16),
        ("conv_b", 4), ("lru_ba", 4), ("lru_bx", 4), ("lam", 4), ("b_gate", 24), ("g_ffn", 8),
        ("ev_g", 8), ("ev_b", 24), ("sink", 8), ("blam", 256), ("subln", 1), ("od_g", 8), ("od_b", 24),
        ("qn_g", 2), ("kvn_g", 1), ("fin_g", 8), ("cond", 16)]
CONSTS = [("ident", 128), ("o1024", 128), ("o64", 128), ("o256", 128), ("o128", 128), ("swap32", 128),
          ("swap16", 128), ("win", 384), ("col", 64)]


def offsets(table):
    at, out = 0, {}
    for name, n in table:
        out[name] = (at, n)
        at += n
    return out, at




class Tok:
    def __init__(self, sem, value=None):
        self.sem, self.value, self.wanted = sem, value, False


class Slot:

    def __init__(self, sem):
        self.sem, self.count = sem, 0


class Queue:
    def __init__(self, sem):
        self.sem, self.items, self.last = sem, [], None

    def wait(self, *toks):
        for t in toks:
            if isinstance(t, (list, tuple)):
                self.wait(*t)
            elif t is not None:
                t.wanted = True
                self.items.append((None, t))

    def op(self, fn, *waits):
        self.wait(*waits)
        t = Tok(self.sem)
        self.items.append((fn, t))
        self.last = t
        return t

    def dma(self, out, in_, slot, *waits):
        self.wait(*waits)
        slot.count += 16
        t = Tok(slot.sem, slot.count)
        self.items.append((lambda e: e.dma_start(out, in_), t))
        return t

    def number(self):
        n = 0
        for fn, t in self.items:
            if fn is not None and t.sem is self.sem and t.wanted:
                n += 1
                t.value = n

    def emit(self, e):
        seen = {}
        for fn, t in self.items:
            if fn is None:
                if seen.get(id(t.sem), 0) < t.value:
                    e.wait_ge(t.sem, t.value)
                    seen[id(t.sem)] = t.value
            else:
                ins = fn(e)
                if t.sem is not self.sem:
                    ins.then_inc(t.sem, 16)
                elif t.wanted:
                    ins.then_inc(t.sem, 1)


class Memory:

    def __init__(self, nc):
        self.nc, self.at, self.n, self.marks = nc, (nc.sbuf_base + 63) // 64 * 64, 0, []

    def __call__(self, shape, dt=F):
        size = 4
        for s in shape[1:]:
            size *= s
        t = self.nc.alloc_sbuf_tensor_at(f"m{self.n}", list(shape), dt, offset=self.at)
        self.n += 1
        self.at += (size + 63) // 64 * 64
        assert self.at <= self.nc.sbuf_usable_end, (self.at, self.nc.sbuf_usable_end)
        return t

    def __enter__(self):
        self.marks.append(self.at)
        return self

    def __exit__(self, *a):
        self.at = self.marks.pop()

    def over(self, at):
        self.marks.append(self.at)
        self.at = at
        return _Over(self)


class _Over:
    def __init__(self, mem):
        self.mem = mem

    def __enter__(self):
        return self.mem

    def __exit__(self, *a):
        self.mem.at = self.mem.marks.pop()


def build(nc, w, vec_d, cst_d, tab_d, xT, ctxT, biasA, biasD, lruw, out):
    W_AT, _ = weight_offsets()
    V_AT, NVEC = offsets(VECS)
    C_AT, NCST = offsets(CONSTS)

    sems = {}

    def sem(name):
        sems[name] = nc.alloc_semaphore(name)
        return sems[name]

    PE, A, V, G, SP = (Queue(sem(f"s_{n}")) for n in ("pe", "act", "dve", "pool", "sp"))
    free_slots = [Slot(sem(f"s_dma{i}")) for i in range(12)]
    slot_turn = [0]
    pending = []

    mem = Memory(nc)
    PS = nc.alloc_psum_tensor("PS", [P, 4096], F)
    x1_d = nc.dram_tensor("x1_scratch", [8, P, T], F, kind="Internal").ap()
    y_d = nc.dram_tensor("y_scratch", [8, P, TC], F, kind="Internal").ap()
    g_d = nc.dram_tensor("g_scratch", [24, P, T], F, kind="Internal").ap()
    m_d = nc.dram_tensor("m_scratch", [8, P, T], F, kind="Internal").ap()

    def move(out_ap, in_ap, *waits):
        s = free_slots[slot_turn[0] % len(free_slots)]
        slot_turn[0] += 1
        if s.count:
            G.wait(Tok(s.sem, s.count))
        t = G.dma(out_ap, in_ap, s, *waits)
        pending.append(t)
        return t

    def barrier():
        lasts = [q.last for q in (PE, A, V, G) if q.last is not None]
        for q in (PE, A, V, G):
            q.wait(*[t for t in lasts if t is not q.last], *pending)
        pending.clear()

    bank_free = [[] for _ in range(8)]
    turn, fill_turn = [0], [0]

    def bank(b):
        return PS[:, 512 * b:512 * b + 512]

    def take(first=0, n=6):
        b = first + turn[0] % n
        turn[0] += 1
        PE.wait(*bank_free[b])
        return b

    h_at = mem.at
    Hh = mem([P, 8, TC], R)
    Hl = mem([P, 8, TC], R)
    NRAW, NSPL = 2, 2
    raw = [mem([P, 1024]) for _ in range(NRAW)]
    whi = [mem([P, 1024], R) for _ in range(NSPL)]
    wlo = [mem([P, 1024], R) for _ in range(NSPL)]
    vec = mem([P, NVEC])
    cst = mem([P, NCST])
    tabs = mem([P, 2, T])
    epst = mem([P, 1])
    lam_t = mem([P, 8])
    mods = {kind: (mem([P, 24, 2]), mem([P, 8, 2])) for kind in ("ev", "od")}
    csil = mem([P, 16])
    nsink = mem([P, 8])

    def vc(name, i=0, n=1):
        a = V_AT[name][0] + i
        return vec[:, a:a + n]

    def cc(name, r=P, n=None):
        a, m = C_AT[name]
        return cst[0:r, a:a + (n or m)]

    ident = cc("ident")

    order = weight_tiles()
    raw_slot = [Slot(sem(f"s_w{i}")) for i in range(NRAW)]
    raw_free = [[] for _ in range(NRAW)]
    spl_free = [[] for _ in range(NSPL)]
    st = {"load": 0, "prep": 0, "use": 0, "spl": 0, "lo": V}
    loaded, parts = {}, {}

    def w_load(upto):
        while st["load"] < min(upto, len(order)):
            i = st["load"]
            name, kt, m = order[i]
            s = i % NRAW
            at = W_AT[name][0]
            loaded[i] = SP.dma(raw[s][:, 0:kt * m],
                               w[at:at + P * kt * m].rearrange("(p c) -> p c", p=P), raw_slot[s], *raw_free[s])
            st["load"] += 1

    def w_prep(upto):
        while st["prep"] < min(upto, len(order)):
            i = st["prep"]
            name, kt, m = order[i]
            if name[:2] not in ("ea", "oa"):
                s, c, r = st["spl"] % NSPL, kt * m, i % NRAW
                hi, lo, src = whi[s][:, 0:c], wlo[s][:, 0:c], raw[r][:, 0:c]
                t1 = A.op(lambda e, hi=hi, src=src: e.copy(hi, src), loaded[i], spl_free[s])
                t2 = st["lo"].op(lambda e, hi=hi, lo=lo, src=src: e.tensor_tensor(lo, src, hi.bitcast(F), ALU.subtract),
                                 loaded[i], spl_free[s], t1)
                raw_free[r] = [t1, t2]
                parts[i] = (s, [t1, t2])
                st["spl"] += 1
            st["prep"] += 1

    def w_get(name):
        i = st["use"]
        assert order[i][0] == name, (order[i], name)
        st["use"] += 1
        _, kt, m = order[i]
        w_load(i + NRAW)
        w_prep(i + 2)
        if i not in parts:
            r = i % NRAW
            PE.wait(loaded[i])

            def release(tok):
                raw_free[r] = [tok]
            return (lambda k: raw[r][:, k * m:(k + 1) * m]), kt, release
        s, toks = parts[i]
        PE.wait(*toks)

        def release(tok):
            spl_free[s] = [tok]
        return (lambda k: (whi[s][:, k * m:(k + 1) * m], wlo[s][:, k * m:(k + 1) * m])), kt, release

    def mm3(o, L, Rr, start, stop):
        PE.op(lambda e: e.matmul(o, L[0], Rr[0], start=start, stop=False))
        PE.op(lambda e: e.matmul(o, L[0], Rr[1], start=False, stop=False))
        return PE.op(lambda e: e.matmul(o, L[1], Rr[0], start=False, stop=stop))

    def mm(o, L, Rr, start=True, stop=True):
        return PE.op(lambda e: e.matmul(o, L, Rr, start=start, stop=stop))

    def linear_steps(name, rhs, chunks, evac, rows=P, banks=None):
        get, kt, release = w_get(name)
        for n, (t0, tn) in enumerate(chunks):
            if banks:
                b = banks[fill_turn[0] % len(banks)]
                fill_turn[0] += 1
                PE.wait(*bank_free[b])
            else:
                b = take()
            o = bank(b)[0:rows, 0:tn]
            for k in range(kt):
                tok = mm3(o, get(k), rhs(k, t0, tn), k == 0, k == kt - 1)
                if k == kt - 1:
                    bank_free[b] = evac(o, t0, tn, tok)
                    if n == len(chunks) - 1:
                        release(tok)
                yield

    def linear(*args, **kw):
        for _ in linear_steps(*args, **kw):
            pass

    class Fill:

        def __init__(self, jobs, steps):
            self.jobs, self.left = jobs, steps

        def pull(self, n):
            while n > 0 and self.left > 0:
                next(self.jobs)
                self.left -= 1
                n -= 1
            if not self.left:
                for _ in self.jobs:
                    pass

    def h_rhs(k, t0, tn):
        return Hh[:, k, t0:t0 + tn], Hl[:, k, t0:t0 + tn]

    def act(out_, in_, f, *waits, **kw):
        return A.op(lambda e: e.activation(out_, in_, f, **kw), *waits)

    def split(hi, lo, src, *waits):
        t1 = A.op(lambda e: e.copy(hi, src), *waits)
        t2 = V.op(lambda e: e.tensor_tensor(lo, src, hi.bitcast(F), ALU.subtract), *waits, t1)
        return [t1, t2]

    def tt(out_, a, b, op, *waits, q=None):
        return (q or V).op(lambda e: e.tensor_tensor(out_, a, b, op), *waits)

    def ts(out_, a, s1, s2, o0, o1, *waits):
        if s2 is None:
            return V.op(lambda e: e.tensor_scalar(out_, a, s1, None, o0), *waits)
        return V.op(lambda e: e.tensor_scalar(out_, a, s1, s2, o0, o1), *waits)

    def stt(out_, a, s, b, o0, o1, *waits):
        return V.op(lambda e: e.scalar_tensor_tensor(out=out_, in0=a, scalar=s, in1=b, op0=o0, op1=o1), *waits)

    def root(rs, ps, tok):
        n = rs.shape[0]
        t = act(rs, ps, ACT.Sqrt, tok, bias=epst[0:n, 0:1])
        return V.op(lambda e: e.reciprocal(rs, rs), t), t

    def norm_split(src, kt, ones, chunks, g, shift, ready, hi, lo, bufs=None):
        out_toks = []
        with mem:
            bufs = bufs or [mem([P, 512]) for _ in range(7)]
            sq, rs, tmp = bufs[0:2], bufs[2:4], bufs[4:7]
            sq_free, rs_free, tmp_free, n, nt = [[], []], [[], []], [[], [], []], 0, 0
            for c, (t0, tn) in enumerate(chunks):
                b = take()
                o = bank(b)[:, 0:tn]
                for k in range(kt):
                    s = sq[n % 2][:, 0:tn]
                    t = act(s, src(k, t0, tn), ACT.Square, ready, sq_free[n % 2])
                    PE.wait(t)
                    m = mm(o, ones, s, k == 0, k == kt - 1)
                    sq_free[n % 2] = [m]
                    n += 1
                r = rs[c % 2][:, 0:tn]
                A.wait(rs_free[c % 2])
                t, ta = root(r, o, m)
                bank_free[b] = [ta]
                for k in range(kt):
                    q = tmp[nt % 3][:, 0:tn]
                    t1 = stt(q, src(k, t0, tn), g(k, c), r, ALU.mult, ALU.mult, t, tmp_free[nt % 3], ready)
                    h, l_ = hi(k, t0, tn), lo(k, t0, tn)
                    sh = shift(k, c) if shift else None
                    if sh is None:
                        t2 = A.op(lambda e, h=h, q=q: e.copy(h, q), t1)
                        t3 = tt(l_, q, h.bitcast(F), ALU.subtract, t2)
                    else:
                        t2 = act(h, q, ACT.Identity, t1, bias=sh)
                        t3 = stt(l_, q, sh, h.bitcast(F), ALU.add, ALU.subtract, t2)
                    tmp_free[nt % 3] = [t3]
                    nt += 1
                    out_toks = [t2, t3]
                rs_free[c % 2] = [t1]
        return out_toks

    t_c = [move(vec[:, :], vec_d), move(cst[:, :], cst_d)]
    t_tab = move(tabs[:, :, :], tab_d[0].rearrange("a p t -> p a t"))
    t_e = V.op(lambda e: e.memset(epst[:, :], EPS))
    w_load(NRAW)
    for q in (PE, A, V, G):
        q.wait(*t_c, t_tab, t_e)

    def copy_to(dst, scale=1.0):
        toks = []

        def evac(o, t0, tn, tok):
            d = dst(t0, tn)
            if scale == 1.0:
                t = A.op(lambda e: e.copy(d, o), tok)
            else:
                t = A.op(lambda e: e.mul(d, o, scale), tok)
            toks.append(t)
            return [t]
        evac.toks = toks
        return evac

    def post(items, bufs, between=None):
        work = [(it, t0, tn) for it in items for t0, tn in it[2]]
        out_t, old = [], []
        deep = len(bufs) // 2
        for w0 in range(0, len(work), deep):
            batch = []
            for n, ((z, rows, _, gain, swap, hi, lo, toks), t0, tn) in enumerate(work[w0:w0 + deep]):
                batch.append({"z": z[0:rows, t0:t0 + tn], "rows": rows, "t0": t0, "tn": tn, "gain": gain,
                              "swap": swap if t0 < T else None, "hi": hi[0:rows, t0:t0 + tn],
                              "lo": lo[0:rows, t0:t0 + tn], "t": list(toks),
                              "x": bufs[2 * n][0:rows, 0:tn], "y": bufs[2 * n + 1][0:rows, 0:tn]})
            normed = [c for c in batch if c["gain"] is not None]
            for c in normed:
                t = act(c["x"], c["z"], ACT.Square, *c["t"], *old)
                PE.wait(t)
                c["b"] = take()
                c["o"] = bank(c["b"])[0:c["rows"], 0:c["tn"]]
                c["m"] = mm(c["o"], cc("o64", c["rows"], c["rows"]), c["x"])
            if normed and between:
                between()
            for c in normed:
                t, ta = root(c["x"], c["o"], c["m"])
                bank_free[c["b"]] = [ta]
                c["t"] = [stt(c["z"], c["z"], c["gain"][0:c["rows"], :], c["x"], ALU.mult, ALU.mult, t, *c["t"])]
            for c in batch:
                if c["swap"]:
                    PE.wait(*c["t"])
                    b = take()
                    o = bank(b)[0:c["rows"], 0:c["tn"]]
                    m = mm(o, cc(c["swap"], c["rows"], c["rows"]), c["z"])
                    cos, sin = (tabs[0:c["rows"], i, c["t0"]:c["t0"] + c["tn"]] for i in range(2))
                    tg = tt(c["x"], c["z"], cos, ALU.mult, *c["t"], *old, q=G)
                    tv = tt(c["y"], o, sin, ALU.mult, m, *old)
                    bank_free[b] = [tv]
                    c["t"] = [tg, tv, m]
            if between:
                between()
            last = []
            for c in batch:
                if c["swap"]:
                    c["t"] = [tt(c["z"], c["x"], c["y"], ALU.add, *c["t"])]
                last += split(c["hi"], c["lo"], c["z"], *c["t"])
            old = last
            out_t += last
        return out_t

    def to_token_major(z, tiles, parts_, z_toks):
        out_t = []
        PE.wait(*z_toks)
        for k0 in range(0, tiles, 4):
            n = min(4, tiles - k0)
            b = take()
            for i in range(n):
                o = PS[:, 512 * b + 128 * i:512 * b + 128 * i + 128]
                src = z[:, (k0 + i) * 128:(k0 + i) * 128 + 128]
                m = PE.op(lambda e, o=o, src=src: e.transpose(o, src, ident))
            o = PS[:, 512 * b:512 * b + 128 * n].rearrange("p (a c) -> p a c", c=128)
            t_h = [act(vh[:, k0:k0 + n, c0:c0 + fn], o[:, :, f0:f0 + fn], ACT.Copy, m)
                   for vh, _, c0, f0, fn in parts_]
            bank_free[b] = [tt(vl[:, k0:k0 + n, c0:c0 + fn], o[:, :, f0:f0 + fn],
                               vh[:, k0:k0 + n, c0:c0 + fn].bitcast(F), ALU.subtract, *t_h)
                            for vh, vl, c0, f0, fn in parts_]
            out_t += bank_free[b]
        return out_t

    class Attention:

        def __init__(self, s_banks, pt_banks, o_banks, fill_banks, width, npt=2, second=0):
            self.s_at = [512 * b[0] for b in s_banks]
            self.s_banks, self.pt_banks, self.o_banks, self.fill_banks = s_banks, pt_banks, o_banks, fill_banks
            self.E = [mem([P, width]) for _ in range(4 + second)]
            self.second = second
            self.S = [mem([P, 8]) for _ in range(4 + second)]
            self.pth = [mem([P, 512], R) for _ in range(npt)]
            self.ptl = [mem([P, 512], R) for _ in range(npt)]
            self.npt = npt

        def start(self):
            for b in range(8):
                PE.wait(*bank_free[b])
            ne = len(self.E)
            self.e_free = [[] for _ in range(ne)]
            self.e_unread = [False] * ne
            self.pt_free = [[] for _ in range(self.npt)]
            self.s_free = [[] for _ in self.s_at]
            self.ns = self.nb = self.nr = self.np = 0
            self.n_e = [0, 0]
            self.todo, self.behind = [], None

        def qk(self, f):
            s = f["s"] = self.ns % len(self.s_at)
            self.ns += 1
            out_ = []
            for c0, cn, terms in f["chunks"]:
                at = self.s_at[s] + c0
                while cn:
                    m = min(cn, 512 - at % 512)
                    out_.append((PS[:, at:at + m], [(L, kf(m)) for L, kf in terms]))
                    terms = [(L, kf.after(m)) for L, kf in terms]
                    at, cn = at + m, cn - m
            PE.wait(*self.s_free[s])
            return out_

        def soft1(self, f):
            k = 1 if f.get("second") else 0
            e = 4 + self.n_e[1] % self.second if k else self.n_e[0] % 4
            self.n_e[k] += 1
            while self.e_unread[e]:
                self.step()
            f["e"], free = e, self.e_free[e]
            E, S = self.E[e], self.S[e]
            f["E"], f["S"] = E, S
            f["pad_t"] = []
            for c in f.get("pads", ()):
                pad = E[:, c:c + 128]
                f["pad_t"].append(G.op(lambda e_: e_.memset(pad, 0.0), *free))
            V.wait(f["tok"], free)
            scale, pieces = f.get("scale", 1.0), f["pieces"]
            base = self.s_at[f["s"]]
            mt, f["exp"] = [], []
            for a, (c0, n, e0, bias) in enumerate(pieces):
                src, d = PS[:, base + c0:base + c0 + n], E[:, e0:e0 + n]
                if bias is None:
                    neg = len(pieces) == 1 and scale == 1.0
                    o = S[:, 0:1] if neg else S[:, 1 + a:2 + a]
                    mt.append(self.reduce(o, src, neg))
                    f["exp"].append((d, src, a))
                else:
                    mt.append(self.biased(d, src, bias, S[:, 1 + a:2 + a]))
                    f["exp"].append((d, d, a))
            nm, t = S[:, 0:1], mt[-1]
            if len(pieces) == 2:
                t = ts(nm, S[:, 1:2], S[:, 2:3], -scale, ALU.max, ALU.mult, *mt)
            elif not (pieces[0][3] is None and scale == 1.0):
                t = ts(nm, S[:, 1:2], -scale, None, ALU.mult, None, *mt)
            if "sink" in f:
                t = ts(nm, nm, nsink[:, f["sink"]:f["sink"] + 1], None, ALU.min, None, t)
            f["nm_t"], f["mt"] = t, mt

        def reduce(self, o, src, neg):
            return V.op(lambda e: e.tensor_reduce(o, src, AX.X, ALU.max, negate=neg))

        def biased(self, d, src, bias, o):
            return V.op(lambda e: e.tensor_tensor_reduce(d, src, bias, 1.0, OUT_OF_RANGE, ALU.add, ALU.max, o))

        def soft2(self, f):
            S, scale = f["S"], f.get("scale", 1.0)
            A.wait(f["nm_t"], self.e_free[f["e"]])
            et = []
            for d, src, a in f["exp"]:
                et.append(act(d, src, ACT.Exp, bias=S[:, 0:1], scale=scale, accum_out=S[:, 3 + a:4 + a]))
            self.s_free[f["s"]] = [f["mt"][-1], et[-1]]
            if "sink" in f:
                et.append(act(S[:, 5:6], vc("sink", f["sink"]), ACT.Exp, bias=S[:, 0:1]))
            f["et"] = et

        def soft3(self, f):
            S, E = f["S"], f["E"]
            rs, ss, two = S[:, 6:7], S[:, 3:4], len(f["pieces"]) == 2
            V.wait(*f["et"])
            t = None
            if "sink" in f:
                ss = S[:, 7:8]
                t = ts(ss, S[:, 3:4], S[:, 4:5] if two else 0.0, S[:, 5:6], ALU.add, ALU.add)
            elif two:
                ss = S[:, 7:8]
                t = tt(ss, S[:, 3:4], S[:, 4:5], ALU.add)
            t = V.op(lambda e: e.reciprocal(rs, ss), t)
            if "first" in f:
                f0 = f["first"]
                n = f["pieces"][0][1]
                a, b = f0["E"][:, 0:n], E[:, 0:n]
                t = ts(rs, rs, lam_t[:, 1:2], None, ALU.mult, None, t)
                t = act(b, b, ACT.Copy, t, scale=rs)
                t = stt(a, a, f0["S"][:, 6:7], b, ALU.mult, ALU.add, t, f0["rs_t"])
                f0["ready"] = [t]
                self.e_free[f["e"]] = [t]
            elif f.get("lam"):
                f["rs_t"] = t
            else:
                spans = []
                for _, n, e0, _ in f["pieces"]:
                    if spans and spans[-1][1] == e0:
                        spans[-1][1] = e0 + n
                    else:
                        spans.append([e0, e0 + n])
                f["ready"] = [ts(E[:, c0:c1], E[:, c0:c1], rs, None, ALU.mult, None, t) for c0, c1 in spans]
                f["ready"] += f["pad_t"]

        def queue(self, u):
            fr = [f for f in u["fronts"] if "first" not in f]
            for f in fr:
                self.e_unread[f["e"]] = True
            kts = u["keys"]
            groups = [kts[i:i + 2] for i in range(0, len(kts), 2)]
            ob = self.o_banks[self.np % len(self.o_banks)]
            self.np += 1
            O = PS[:, 512 * ob:512 * ob + 256]
            st_ = {}

            def turn_over(g):
                if g == 0:
                    PE.wait(*[f["ready"] for f in fr])
                b = self.pt_banks[self.nb % len(self.pt_banks)]
                self.nb += 1
                PE.wait(*bank_free[b])
                i = 0
                for e0, _, _ in groups[g]:
                    for f in fr:
                        m = self.turn(PS[:, 512 * b + i:512 * b + i + 128], f["E"][:, e0:e0 + 128])
                        i += 128
                r = self.nr % self.npt
                self.nr += 1
                h, l_, s = self.pth[r][:, 0:i], self.ptl[r][:, 0:i], PS[:, 512 * b:512 * b + i]
                toks = split(h, l_, s, m, self.pt_free[r])
                bank_free[b] = toks
                st_[g] = (r, toks)
                if g == len(groups) - 1:
                    for f in fr:
                        self.e_free[f["e"]] = [m]
                        self.e_unread[f["e"]] = False

            def multiply(g):
                r, toks = st_[g]
                PE.wait(*toks)
                if g == 0:
                    PE.wait(*bank_free[ob])
                last = g == len(groups) - 1
                for i, (_, vh, vl) in enumerate(groups[g]):
                    s = slice(256 * i, 256 * i + 256)
                    h, l_ = self.pth[r][:, s], self.ptl[r][:, s]
                    m = mm(O, vh, h, g == 0 and i == 0, False)
                    m = mm(O, vh, l_, False, False)
                    m = mm(O, vl, h, False, last and i == len(groups[g]) - 1)
                self.pt_free[r] = [m]
                if last:
                    bank_free[ob] = u["evac"](O, m)

            def step_of(g):
                def fn():
                    turn_over(g)
                    if self.behind:
                        self.behind()
                    self.behind = lambda: multiply(g)
                return fn

            self.todo += [step_of(g) for g in range(len(groups))]

        def turn(self, o, s):
            return PE.op(lambda e: e.transpose(o, s, ident))

        def step(self):
            self.todo.pop(0)()

        def run(self, units, ready, fill=None):
            self.start()
            one = len(self.s_at) == 1
            slots = sum(1 if one else -(-cn // 512) for u in units for f in u["fronts"] for _, cn, _ in f["chunks"])
            PE.wait(*ready)
            late = None
            for u in units:
                fr = u["fronts"]
                left = 0
                for i, f in enumerate(fr):
                    pieces = self.qk(f)
                    if i == 0:
                        left = (1 if one else len(pieces)) * (len(fr) - 1)
                    for a, (o, terms) in enumerate(pieces):
                        for x, (L, Rr) in enumerate(terms):
                            f["tok"] = mm3(o, L, Rr, x == 0, x == len(terms) - 1)
                        end = a == len(pieces) - 1
                        if end:
                            self.soft1(f)
                            if late:
                                self.finish(late)
                            late = (u, f)
                        elif one:
                            continue
                        n = 0
                        if i:
                            n = -(-len(self.todo) // max(1, left))
                            left -= 1
                        fn = -(-fill.left // max(1, slots)) if fill else 0
                        slots -= 1
                        if fill:
                            fill.pull(fn - fn * n // (n + 1))
                        for k in range(n):
                            if end and k == SOFT2_AT:
                                self.soft2(f)
                            if self.todo:
                                self.step()
                            if fill:
                                fill.pull(-(-fn // (n + 1)))
                        if end and n <= SOFT2_AT:
                            self.soft2(f)
            self.finish(late)
            while self.todo:
                if fill:
                    fill.pull(4)
                self.step()
            self.behind()
            if fill:
                fill.pull(fill.left)
            for s, banks in enumerate(self.s_banks):
                for b in banks:
                    bank_free[b] = self.s_free[s]
            return PE.last

        def finish(self, late):
            u, f = late
            self.soft3(f)
            if f is u["fronts"][-1]:
                while self.todo:
                    self.step()
                self.queue(u)

    class Keys:

        def __init__(self, hi, lo, p0, p1, a):
            self.hi, self.lo, self.p0, self.p1, self.a = hi, lo, p0, p1, a

        def __call__(self, n):
            return self.hi[self.p0:self.p1, self.a:self.a + n], self.lo[self.p0:self.p1, self.a:self.a + n]

        def after(self, n):
            return Keys(self.hi, self.lo, self.p0, self.p1, self.a + n)

    def pair(hi, lo, p0, p1, a, n):
        return hi[p0:p1, a:a + n], lo[p0:p1, a:a + n]

    def s_start(n):
        return 128 if n % 512 == 128 and n > 512 else 0

    def y_store(j, yt, n, *waits):
        return move(y_d[j][:, 0:n], yt[:, 0:n], *waits)

    with mem:
        X = mem([P, 8, T])
        t_x = [move(X[:, :, :], xT.rearrange("k p t -> p k t"))]
        norm_split(lambda k, t0, tn: X[:, k, t0:t0 + tn], 8, cc("o1024"), CH1,
                   lambda k, c: vc("g_mix", k), None, t_x,
                   lambda k, t0, tn: Hh[:, k, t0:t0 + tn], lambda k, t0, tn: Hl[:, k, t0:t0 + tn])
        barrier()

    with mem:
        score = [mem([P, 128 * (b + 1)]) for b in range(8)]
        with mem:
            iqh, iql = [mem([P, T], R) for _ in range(2)], [mem([P, T], R) for _ in range(2)]
            ikh, ikl = mem([P, T], R), mem([P, T], R)
            z = [mem([P, T]) for _ in range(3)]
            tmp = [mem([P, 512]) for _ in range(4)]
            relu = [mem([P, T]) for _ in range(2)]
            wi = mem([P, 8, 4])
            ev = []
            for j, name in enumerate(("iq0", "iq1", "ikw")):
                r = P if j < 2 else 68
                e_ = copy_to(lambda t0, tn, j=j, r=r: z[j][0:r, t0:t0 + tn])
                linear(name, h_rhs, CH1, e_, rows=r)
                ev.append(e_.toks)
            PE.wait(*ev[2])
            b = take()
            for i in range(8):
                o = PS[:, 512 * b + 4 * i:512 * b + 4 * i + 4]
                s = z[2][64:68, 128 * i:128 * i + 128]
                m = PE.op(lambda e, o=o, s=s: e.transpose(o, s, ident[64:68, 64:68]))
            o = PS[:, 512 * b:512 * b + 32].rearrange("p (a c) -> p a c", c=4)
            t_w = ts(wi[:, :, :], o, 0.0625, None, ALU.mult, None, m)
            bank_free[b] = [t_w]
            k_t = q_t = post([(z[2], 64, CH1, vc("ik_g"), "swap32", ikh, ikl, ev[2])]
                             + [(z[j], P, CH1, None, "swap32", iqh[j], iql[j], ev[j]) for j in range(2)], tmp)
            d1 = move(ikh[64:128, :], ikh[0:64, :], *k_t)
            d2 = move(ikl[64:128, :], ikl[0:64, :], *k_t)
            PE.wait(*q_t, *k_t, d1, d2)
            r_free = [[], []]
            nr = 0
            prev = None
            t_w = [t_w]
            for b in range(2, 8):
                n = 128 * (b + 1)
                sc = score[b]
                for h in range(4):
                    p0 = 64 * (h % 2)
                    s0 = (nr % 3) * 2
                    banks = list(range(s0, s0 + (n + 511) // 512))
                    for x_ in banks:
                        PE.wait(*bank_free[x_])
                    for c0 in range(0, n, 512):
                        cn = min(512, n - c0)
                        m = mm3(PS[:, 512 * s0 + c0:512 * s0 + c0 + cn],
                                pair(iqh[h // 2], iql[h // 2], p0, p0 + 64, 128 * b, 128),
                                pair(ikh, ikl, p0, p0 + 64, c0, cn), True, True)
                    rl = relu[nr % 2][:, 0:n]
                    t = act(rl, PS[:, 512 * s0:512 * s0 + n], ACT.Relu, m, r_free[nr % 2])
                    for x_ in banks:
                        bank_free[x_] = [t]
                    if h == 0:
                        prev = ts(sc[:, :], rl, wi[:, b, 0:1], None, ALU.mult, None, t, *t_w)
                    else:
                        prev = stt(sc[:, :], rl, wi[:, b, h:h + 1], sc[:, :], ALU.mult, ALU.add, t, prev)
                    r_free[nr % 2] = [prev]
                    nr += 1
                prev = V.op(lambda e, sc=sc, n=n: e.memset(sc[0:64, n - 64:n], OUT_OF_RANGE), prev)
            barrier()

        with mem:
            m8 = [mem([P, 8]) for _ in range(2)]
            for b0 in (2, 4, 6):
                last = {b0: None, b0 + 1: None}
                for it in range(32):
                    for b in (b0, b0 + 1):
                        sc, mx = score[b], m8[b % 2]
                        t = V.op(lambda e, mx=mx, sc=sc: e.max(mx[:, :], sc[:, :]), last[b])
                        last[b] = t
                    for b in (b0, b0 + 1):
                        sc, mx = score[b], m8[b % 2]
                        last[b] = V.op(lambda e, mx=mx, sc=sc: e.match_replace(sc[:, :], mx[:, :], sc[:, :], TAKEN),
                                       last[b])
                for b in (b0, b0 + 1):
                    sc = score[b]
                    ts(sc[:, :], sc[:, :], TAKEN, NEG, ALU.not_equal, ALU.mult, last[b])
            for b in range(2):
                n = 128 * (b + 1)
                t = V.op(lambda e, b=b: e.memset(score[b][:, :], 0.0))
                V.op(lambda e, b=b, n=n: e.memset(score[b][0:64, n - 64:n], NEG), t)
            st["lo"] = G
            lw = mem([P, 4, 2, 128])
            t_l = move(lw[:, :, :, :], lruw)
            xc = [mem([P, T + 3]) for _ in range(4)]
            gl = [mem([P, T]) for _ in range(4)]
            gate = [mem([P, 512]) for _ in range(4)]
            for c in range(4):
                t_z = G.op(lambda e, c=c: e.memset(xc[c][:, 0:3], 0.0))
            xc_t, gl_t = [], []
            for c in range(4):
                e1 = copy_to(lambda t0, tn: xc[c][:, 3 + t0:3 + t0 + tn])
                linear(f"cx{c}", h_rhs, CH1, e1)
                xc_t.append(e1.toks + [t_z])
                e1 = copy_to(lambda t0, tn: gl[c][:, t0:t0 + tn])
                linear(f"cy{c}", h_rhs, CH1, e1)
                gl_t.append(e1.toks)
            g_free = [None] * 4
            for d in range(8):
                for i in range(3):
                    def ev_s(o, t0, tn, tok):
                        n = (6 * d + 2 * i + t0 // 512) % 4
                        t = act(gate[n][:, :], o, ACT.Sigmoid, tok, g_free[n], bias=vc("b_gate", 8 * i + d))
                        g_free[n] = move(g_d[8 * i + d][:, t0:t0 + tn], gate[n][:, :], t)
                        return [t]
                    linear(f"gt{i}_{d}", h_rhs, CH1, ev_s)
            t = act(csil[:, :], vc("cond", 0, 16), ACT.Silu)
            PE.wait(t)
            m_bank, m_t = {}, {}
            for kind in ("ev", "od"):
                b = m_bank[kind] = take()
                for m_ in range(24):
                    get, kt, release = w_get(f"{kind[0]}a{m_}")
                    for k in range(8):
                        m = mm(PS[:, 512 * b + 2 * m_:512 * b + 2 * m_ + 2], get(k), csil[:, 2 * k:2 * k + 2],
                               k == 0, k == 7)
                    release(m)
                m_t[kind] = m
            st["lo"] = V
            for kind in ("ev", "od"):
                b, (mod, gs) = m_bank[kind], mods[kind]
                o = PS[:, 512 * b:512 * b + 48].rearrange("p (a c) -> p a c", c=2)
                bb = vc(f"{kind}_b", 0, 24).rearrange("p (a c) -> p a c", c=1).to_broadcast([P, 24, 2])
                t = tt(mod[:, :, :], o, bb, ALU.add, m_t[kind])
                bank_free[b] = [t]
                for s in range(2):
                    stt(gs[:, :, s], mod[:, 8:16, s], 1.0, vc(f"{kind}_g", 0, 8), ALU.add, ALU.mult, t)

            c8, nc8, sa, sb_, sc_, sd_ = (mem([P, 4]) for _ in range(6))
            lam = vc("lam", 0, 4)
            t = ts(sa[:, :], lam, -1.0, None, ALU.mult, None)
            t = tt(sb_[:, :], sa[:, :], lam, ALU.max, t)
            t1 = act(sb_[:, :], sb_[:, :], ACT.Exp, t, scale=-1.0)
            t = ts(sc_[:, :], sb_[:, :], 2.0, None, ALU.add, None, t1)
            t = V.op(lambda e: e.reciprocal(sc_[:, :], sc_[:, :]), t)
            t = tt(sb_[:, :], sb_[:, :], sc_[:, :], ALU.mult, t)
            t = tt(sc_[:, :], sb_[:, :], sb_[:, :], ALU.mult, t)
            t = ts(sd_[:, :], sc_[:, :], 1.0 / 17.0, None, ALU.mult, None, t)
            for n in (15, 13, 11, 9, 7, 5, 3):
                t = stt(sd_[:, :], sd_[:, :], 1.0 / n, sc_[:, :], ALU.add, ALU.mult, t)
            t = stt(sd_[:, :], sd_[:, :], 1.0, sb_[:, :], ALU.add, ALU.mult, t)
            t = ts(sa[:, :], sa[:, :], 0.0, None, ALU.max, None, t)
            t = stt(sd_[:, :], sd_[:, :], 2.0, sa[:, :], ALU.mult, ALU.add, t)
            t = ts(c8[:, :], sd_[:, :], -8.0, None, ALU.mult, None, t)
            t_s = [ts(nc8[:, :], sd_[:, :], 8.0, None, ALU.mult, None, t), t]
            A.wait(*t_s)
            PE.wait(t_l)
            u, r, i_, a_, th, yc = (mem([P, T]) for _ in range(6))
            t_y = None
            prev_scan = None
            for c in range(4):
                s = c
                tg = act(gl[c][:, :], gl[c][:, :], ACT.Gelu_apprx_tanh, gl_t[c])
                A.wait(prev_scan)
                t = ts(u[:, :], xc[s][:, 0:T], vc("conv_w", c), vc("conv_b", c), ALU.mult, ALU.add, *xc_t[c], prev_scan)
                for j in range(1, 4):
                    t = stt(u[:, :], xc[s][:, j:j + T], vc("conv_w", 4 * j + c), u[:, :], ALU.mult, ALU.add, t)
                PE.wait(t)
                for w_i, (dst, bn) in enumerate(((r, "lru_ba"), (i_, "lru_bx"))):
                    for t0, tn in CH1:
                        b = take()
                        m = mm(bank(b), lw[:, c, w_i, :], u[:, t0:t0 + tn])
                        ts_ = act(dst[:, t0:t0 + tn], bank(b), ACT.Sigmoid, m, bias=vc(bn, c))
                        bank_free[b] = [ts_]
                ta = act(a_[:, :], r[:, :], ACT.Exp, ts_, scale=c8[:, c:c + 1])
                tth = act(th[:, :], r[:, :], ACT.Tanh, scale=nc8[:, c:c + 1])
                t = tt(i_[:, :], i_[:, :], u[:, :], ALU.mult, ts_)
                t1 = tt(r[:, :], a_[:, :], a_[:, :], ALU.mult, ta, tth)
                t1 = stt(r[:, :], r[:, :], 1.0, th[:, :], ALU.add, ALU.mult, t1, tth)
                t2 = act(r[:, :], r[:, :], ACT.Sqrt, t1)
                t = tt(i_[:, :], i_[:, :], r[:, :], ALU.mult, t, t2)
                t = V.op(lambda e: e.tensor_tensor_scan(th[:, :], a_[:, :], i_[:, :], 0.0, ALU.mult, ALU.add), t, ta)
                t = tt(yc[:, :], th[:, :], gl[s][:, :], ALU.mult, t, tg, t_y)
                prev_scan = t
                t_y = y_store(4 + c, yc, T, t)
            barrier()

        with mem:
            zq, zk, zv = (mem([P, T]) for _ in range(3))
            yt = zv
            qh, ql, kh, kl = (mem([P, T], R) for _ in range(4))
            vh, vl = mem([P, 8, 128], R), mem([P, 8, 128], R)
            g2 = {kind: mem([P, 1]) for kind in "ab"}
            bias = mem([P, 2, 640])
            at = Attention([[0, 1], [2, 3]], [4, 5], [6], [7], T)
            bufs = [x[:, a:a + 512] for x in at.E for a in (0, 512)]
            t_g = {kind: ts(g2[kind][:, :], vc(f"{kind}q_g"), 0.125, None, ALU.mult, None) for kind in "ab"}
            ev = {}

            def qk_jobs(kind, j, banks):
                for s, z in (("q", zq), ("k", zk)):
                    e_ = copy_to(lambda t0, tn: z[:, t0:t0 + tn])
                    yield from linear_steps(f"{kind}{s}{j}", h_rhs, CH1, e_, banks=banks)
                    ev[s] = e_.toks

            order_ab = [("a", 0), ("a", 1), ("b", 0), ("b", 1)]
            for _ in qk_jobs("a", 0, None):
                pass
            t_y = None
            for n_ab, (kind, j) in enumerate(order_ab):
                if kind == "a":
                    t_b = move(bias[:, :, :], biasA[:, 2 * j:2 * j + 2, :])
                    V.wait(t_b)
                    for i in range(2):
                        for d in (bias[0:64, i, 576:640], bias[64:128, i, 0:64]):
                            V.op(lambda e, d=d: e.memset(d, NEG))
                sw = "swap32" if kind == "b" else None
                e_ = copy_to(lambda t0, tn: zv[:, t0:t0 + tn])
                A.wait(t_y)
                v_fill = Fill(linear_steps(f"{kind}v{j}", h_rhs, CH1, e_), 16)
                ready = post([(zq, P, CH1, g2[kind], sw, qh, ql, ev["q"] + [t_g[kind]]),
                              (zk, P, CH1, vc(f"{kind}k_g"), sw, kh, kl, ev["k"])], bufs, lambda: v_fill.pull(8))
                v_fill.pull(16)
                ready += to_token_major(zv, 8, [(vh, vl, 0, 0, 128)], e_.toks)
                barrier()
                units = []
                for b0 in range(0, 8, 2):
                    lo = max(0, b0 - 4) if kind == "a" else 0
                    tiles = range(lo, b0 + 2)
                    for i in range(2):
                        rows = slice(64 * i, 64 * i + 64)
                        fronts = []
                        for b in (b0, b0 + 1):
                            first = max(0, b - 4) if kind == "a" else 0
                            n = 128 * (b + 1 - first)
                            bi = bias[:, i, 640 - n:640] if kind == "a" else score[b][:, :]
                            q = pair(qh, ql, 64 * i, 64 * i + 64, 128 * b, 128)
                            s0 = s_start(n)
                            fronts.append({
                                "pieces": [(s0, n, 128 * (first - lo), bi)],
                                "chunks": [(s0, n, [(q, Keys(kh, kl, 64 * i, 64 * i + 64, 128 * first))])],
                                "pads": [128 * (y - lo) for y in tiles if not first <= y <= b]})
                        yd = yt[rows, 128 * b0:128 * b0 + 256]
                        units.append({"fronts": fronts,
                                      "keys": [(128 * (y - lo), vh[:, y, :], vl[:, y, :]) for y in tiles],
                                      "evac": lambda o, m, yd=yd, rows=rows: [act(yd, o[rows, :], ACT.Copy, m)]})
                fill = Fill(qk_jobs(*order_ab[n_ab + 1], at.fill_banks), 32) if n_ab < 3 else None
                at.run(units, ready, fill)
                t_y = y_store((0 if kind == "a" else 2) + j, yt, T, A.last)
                barrier()

    with mem:
        Yh, Yl = mem([P, 8, T], R), mem([P, 8, T], R)
        gate = [mem([P, 512]) for _ in range(10)]
        mg = mem([P, 512])
        t1b = mem([P, 512])
        with mem:
            src_free = [[], []]
        yl2 = [mg, t1b]
        nl = 0
        for k in range(8):
            for t0, tn in CH1:
                s = yl2[nl % 2]
                t_d = move(s[:, :], y_d[k][:, t0:t0 + tn], *src_free[nl % 2])
                src_free[nl % 2] = split(Yh[:, k, t0:t0 + tn], Yl[:, k, t0:t0 + tn], s[:, :], t_d)
                nl += 1
        y_ready = list(src_free[0]) + list(src_free[1])
        A.wait(*y_ready)
        PE.wait(*y_ready)
        V.wait(*y_ready)
        g_free = [[] for _ in range(10)]
        gate_at = [(8 * i + d, t0, tn) for d in range(8) for t0, tn in CH1 for i in range(3)]
        sig, t_m = [], None
        for d in range(8):
            get, kt, release = w_get(f"wb{d}")
            for c, (t0, tn) in enumerate(CH1):
                last = None
                for i, (k0, k1) in enumerate(((0, 2), (2, 4), (4, 8))):
                    b = take()
                    for k in range(k0, k1):
                        m = mm3(bank(b), get(k), (Yh[:, k, t0:t0 + tn], Yl[:, k, t0:t0 + tn]), k == k0, k == k1 - 1)
                    n = 6 * d + 3 * c + i
                    while len(sig) < min(n + 8, 48):
                        g, g0, gn = gate_at[len(sig)]
                        sig.append(move(gate[len(sig) % 10][:, :], g_d[g][:, g0:g0 + gn], *g_free[len(sig) % 10]))
                    if i == 0:
                        last = tt(mg[:, :], bank(b), gate[n % 10][:, :], ALU.mult, m, sig[n], t_m)
                        bank_free[b] = [last]
                    else:
                        t = tt(t1b[:, :], bank(b), gate[n % 10][:, :], ALU.mult, m, sig[n], last)
                        bank_free[b] = [t]
                        last = tt(mg[:, :], mg[:, :], t1b[:, :], ALU.add, t, last)
                    g_free[n % 10] = [last]
                t_m = move(m_d[d][:, t0:t0 + tn], mg[:, :], last)
            release(m)
        barrier()

    def load_split(src_d, n):
        with mem:
            s = [mem([P, TC]) for _ in range(3)]
            fr = [[], [], []]
            for k in range(8):
                t_d = move(s[k % 3][:, 0:n], src_d[k][:, 0:n], *fr[k % 3])
                fr[k % 3] = split(Hh[:, k, 0:n], Hl[:, k, 0:n], s[k % 3][:, 0:n], t_d)
        return [t for f in fr for t in f]

    with mem:
        X = mem([P, 8, TC])
        t_x = [move(X[:, :, 0:T], xT.rearrange("k p t -> p k t")),
               move(X[:, :, T:TC], ctxT.rearrange("k p t -> p k t"))]
        PE.wait(*load_split(m_d, T))
        V.wait(*t_x)

        def add_to(d):
            def evac(o, t0, tn, tok):
                return [tt(X[:, d, t0:t0 + tn], X[:, d, t0:t0 + tn], o, ALU.add, tok)]
            return evac

        for d in range(8):
            linear(f"wo{d}", h_rhs, CH1, add_to(d))
        barrier()
        norm_split(lambda k, t0, tn: X[:, k, t0:t0 + tn], 8, cc("o1024"), CH1,
                   lambda k, c: vc("g_ffn", k), None, [],
                   lambda k, t0, tn: Hh[:, k, t0:t0 + tn], lambda k, t0, tn: Hl[:, k, t0:t0 + tn])
        barrier()
        with mem:
            GM = max(FFN_GROUPS)
            uh, ul = mem([P, GM, T], R), mem([P, GM, T], R)
            sg = [mem([P, 512]) for _ in range(2)]
            sg_free = [[], []]
            f0 = 0
            for n, g in enumerate(FFN_GROUPS):
                fin_t = []
                for f in range(g):
                    sil = {}

                    def ev_g(o, t0, tn, tok):
                        c = t0 // 512
                        sil[c] = act(sg[c][:, :], o, ACT.Silu, tok, sg_free[c])
                        return [sil[c]]

                    def ev_u(o, t0, tn, tok):
                        c = t0 // 512
                        t = tt(sg[c][:, :], sg[c][:, :], o, ALU.mult, tok, sil[c])
                        sg_free[c] = split(uh[:, f, t0:t0 + tn], ul[:, f, t0:t0 + tn], sg[c][:, :], t)
                        return [t]
                    if f == 0:
                        A.wait(PE.last)
                        V.wait(PE.last)
                    linear(f"fg{f0 + f}", h_rhs, CH1, ev_g)
                    linear(f"fu{f0 + f}", h_rhs, CH1, ev_u)
                    fin_t = [sg_free[0], sg_free[1]]
                PE.wait(*fin_t)
                for d in range(8):
                    linear(f"fo{n}_{d}", lambda k, t0, tn: (uh[:, k, t0:t0 + tn], ul[:, k, t0:t0 + tn]), CH1,
                           add_to(d))
                f0 += g
        barrier()
        move(x1_d.rearrange("k p t -> p k t"), X[:, :, 0:T])

        def cond_of(c):
            return 1 if c == 2 else 0

        mod, gs = mods["ev"]
        norm_split(lambda k, t0, tn: X[:, k, t0:t0 + tn], 8, cc("o1024"), CH2,
                   lambda k, c: gs[:, k, cond_of(c):cond_of(c) + 1],
                   lambda k, c: mod[:, k, cond_of(c):cond_of(c) + 1], [],
                   lambda k, t0, tn: Hh[:, k, t0:t0 + tn], lambda k, t0, tn: Hl[:, k, t0:t0 + tn])
        barrier()

    t_tab = move(tabs[:, :, :], tab_d[1].rearrange("a p t -> p a t"))
    for q in (A, V, G):
        q.wait(t_tab)
    with mem:
        ld = mem([P, 64])
        bl = [vc("blam", 64 * i, 64) for i in range(4)]
        t = None
        for i in range(2):
            t = V.op(lambda e, i=i: e.tensor_tensor_reduce(ld[:, :], bl[2 * i], bl[2 * i + 1], 1.0, 0.0, ALU.mult,
                                                           ALU.add, lam_t[:, 2 + i:3 + i]), t)
        t = act(lam_t[:, 4:6], lam_t[:, 2:4], ACT.Exp, t)
        t = tt(lam_t[:, 0:1], lam_t[:, 4:5], lam_t[:, 5:6], ALU.subtract, t)
        t = ts(lam_t[:, 1:2], lam_t[:, 0:1], 0.8 - 0.6, -1.0, ALU.add, ALU.mult, t)
        t = ts(nsink[:, :], vc("sink", 0, 8), -1.0, None, ALU.mult, None, t)
        barrier()

    def gate_evac(gt, n=TC):
        toks = []

        def evac(o, t0, tn, tok):
            toks.append(act(gt[:, t0:t0 + tn], o, ACT.Silu, tok))
            return [toks[-1]]
        evac.toks = toks
        return evac

    def plain(yt, rows, b0):
        yd = yt[rows, 128 * b0:128 * b0 + 256]
        return lambda o, m: [act(yd, o[rows, :], ACT.Copy, m)]

    def gated(yt, gt, rows, b0):
        yd, gd = yt[rows, 128 * b0:128 * b0 + 256], gt[rows, 128 * b0:128 * b0 + 256]
        return lambda o, m: [tt(yd, o[rows, :], gd, ALU.mult, m)]

    with mem:
        zq, zk, zg, yt = (mem([P, TC]) for _ in range(4))
        qh, ql, kh, kl = (mem([P, TC], R) for _ in range(4))
        ev, eg = {}, [None]

        def jobs(chunks, gate, nxt, banks):
            if gate:
                eg[0] = copy_to(lambda t0, tn: zg[:, t0:t0 + tn])
                yield from linear_steps(gate, h_rhs, chunks["g"], eg[0], banks=banks)
            for s, z, scale in (("q", zq, 0.125), ("k", zk, 1.0)):
                if s in nxt:
                    e_ = copy_to(lambda t0, tn: z[:, t0:t0 + tn], scale)
                    yield from linear_steps(nxt[s], h_rhs, chunks[s], e_, banks=banks)
                    ev[s] = e_.toks

        def steps_of(chunks, gate, nxt):
            return 8 * ((len(chunks["g"]) if gate else 0) + sum(len(chunks[s]) for s in nxt))

        CHE = {"g": CH2, "q": CH2, "k": CH2}
        for _ in jobs(CHE, None, {"q": "eq0", "k": "ek0"}, None):
            pass
        with mem:
            vh, vl = [mem([P, 10, 128], R) for _ in range(2)], [mem([P, 10, 128], R) for _ in range(2)]
            at = Attention([[0, 1], [2, 3]], [4, 5], [6], [7], 768)
            bufs = [x[:, 0:512] for x in at.E]
            for j in range(4):
                kv = j // 2
                items = [(zq, P, CH2, None, "swap16", qh, ql, ev["q"])]
                if j % 2 == 0:
                    items.append((zk, P, CH2, None, "swap16", kh, kl, ev["k"]))
                ready = post(items, bufs)
                if j == 0:
                    e_ = copy_to(lambda t0, tn: zg[:, t0:t0 + tn])
                    linear("ev", h_rhs, CH2, e_)
                    ready += to_token_major(zg, 10, [(vh[i], vl[i], c, 64 * i, 64) for i in range(2)
                                                     for c in (0, 64)], e_.toks)
                barrier()
                units = []
                for b0 in range(0, 10, 2):
                    tiles = range(max(0, b0 - 1), min(8, b0 + 3)) if b0 < 8 else []
                    for i in range(2):
                        rows = slice(64 * i, 64 * i + 64)
                        fronts = []
                        for b in (b0, b0 + 1):
                            q = pair(qh, ql, 64 * i, 64 * i + 64, 128 * b, 128)
                            f = {"sink": 2 * j + i, "pieces": [(512, 256, 512, None)], "pads": [],
                                 "chunks": [(512, 256, [(q, Keys(kh, kl, 64 * i, 64 * i + 64, T))])]}
                            if b < 8:
                                first, end = max(0, b - 1), min(8, b + 2)
                                n = 128 * (end - first)
                                m0 = C_AT["win"][0] + (128 if b == 0 else 0)
                                f["pieces"].insert(0, (0, n, 128 * (first - b0 + 1), cst[:, m0:m0 + n]))
                                f["chunks"].insert(0, (0, n, [(q, Keys(kh, kl, 64 * i, 64 * i + 64, 128 * first))]))
                                f["pads"] = [128 * (y - b0 + 1) for y in tiles if not first <= y < end]
                            fronts.append(f)
                        kt = [(512, 8), (640, 9)] + [(128 * (y - b0 + 1), y) for y in tiles]
                        units.append({"fronts": fronts, "keys": [(e0, vh[kv][:, y, :], vl[kv][:, y, :]) for e0, y in kt],
                                      "evac": plain(yt, rows, b0)})
                nxt = {"q": f"eq{j + 1}"} if j < 3 else {"q": "fq0", "k": "fk0"}
                if j == 1:
                    nxt["k"] = "ek1"
                at.run(units, ready, Fill(jobs(CHE, f"eg{j}", nxt, at.fill_banks), steps_of(CHE, True, nxt)))
                t = act(zg[:, :], zg[:, :], ACT.Silu, A.last, *eg[0].toks)
                t = tt(yt[:, :], yt[:, :], zg[:, :], ALU.mult, t)
                y_store(j, yt, TC, t)
                barrier()

        with mem:
            vh, vl = mem([P, 10, 128], R), mem([P, 10, 128], R)
            g8 = mem([P, 1])
            at = Attention([[0, 1, 2]], [3, 4], [5], [6, 7], TC, 2, 1)
            bufs = [x[:, a:a + 512] for x in at.E for a in (0, 512)]
            t_g8 = ts(g8[:, :], vc("subln"), 1.0 - (0.8 - 0.6), None, ALU.mult, None)
            for h in range(4):
                ready = post([(zq, P, CH2, None, "swap16", qh, ql, ev["q"]),
                              (zk, P, CH2, None, "swap16", kh, kl, ev["k"])], bufs)
                e_ = copy_to(lambda t0, tn: zg[:, t0:t0 + tn])
                linear(f"fv{h}", h_rhs, CH2, e_)
                ready += to_token_major(zg, 10, [(vh, vl, 0, 0, 128)], e_.toks)
                barrier()
                units = []
                for b0 in range(0, 10, 2):
                    n, k0 = (TC, 0) if b0 < 8 else (256, T)
                    fronts = []
                    for b in (b0, b0 + 1):
                        for i in range(2):
                            q = pair(qh, ql, 64 * i, 64 * i + 64, 128 * b, 128)
                            f = {"pieces": [(0, n, 0, None)], "lam": True,
                                 "chunks": [(0, n, [(q, Keys(kh, kl, 64 * i, 64 * i + 64, k0))])]}
                            if i:
                                f["first"], f["second"] = fronts[-1], True
                            fronts.append(f)
                    yd = yt[:, 128 * b0:128 * b0 + 256]
                    units.append({"fronts": fronts,
                                  "keys": [(128 * y, vh[:, k0 // 128 + y, :], vl[:, k0 // 128 + y, :])
                                           for y in range(n // 128)],
                                  "evac": lambda o, m, yd=yd: [act(yd, o, ACT.Copy, m)]})
                nxt = {"q": f"fq{h + 1}", "k": f"fk{h + 1}"} if h < 3 else {}
                at.run(units, ready, Fill(jobs(CHE, f"eg{4 + h}", nxt, at.fill_banks), steps_of(CHE, True, nxt)))
                barrier()
                t_s = act(zg[:, :], zg[:, :], ACT.Silu)
                for n, (t0, tn) in enumerate(CH2):
                    yc, s, r = yt[:, t0:t0 + tn], bufs[2 * n][:, 0:tn], bufs[2 * n + 1][:, 0:tn]
                    t = act(s, yc, ACT.Square)
                    PE.wait(t)
                    b = take()
                    m = mm(bank(b)[:, 0:tn], cc("o128"), s)
                    t, ta = root(r, bank(b)[:, 0:tn], m)
                    bank_free[b] = [ta]
                    t = stt(yc, yc, g8[:, 0:1], r, ALU.mult, ALU.mult, t)
                    t = tt(yc, yc, zg[:, t0:t0 + tn], ALU.mult, t, t_s)
                y_store(4 + h, yt, TC, t)
                barrier()

    with mem:
        X = mem([P, 8, TC])
        t_x = [move(X[:, :, 0:T], x1_d.rearrange("k p t -> p k t")),
               move(X[:, :, T:TC], ctxT.rearrange("k p t -> p k t"))]
        PE.wait(*load_split(y_d, TC))
        V.wait(*t_x)

        def add_gated(d):
            def evac(o, t0, tn, tok):
                s = 1 if t0 >= T else 0
                return [stt(X[:, d, t0:t0 + tn], o, mod[:, 16 + d, s:s + 1], X[:, d, t0:t0 + tn], ALU.mult, ALU.add,
                            tok)]
            return evac

        for d in range(8):
            linear(f"eo{d}", h_rhs, CH2, add_gated(d))
        barrier()
        move(x1_d.rearrange("k p t -> p k t"), X[:, :, 0:T])
        mod, gs = mods["od"]
        norm_split(lambda k, t0, tn: X[:, k, t0:t0 + tn], 8, cc("o1024"), CH2,
                   lambda k, c: gs[:, k, cond_of(c):cond_of(c) + 1],
                   lambda k, c: mod[:, k, cond_of(c):cond_of(c) + 1], [],
                   lambda k, t0, tn: Hh[:, k, t0:t0 + tn], lambda k, t0, tn: Hl[:, k, t0:t0 + tn])
        barrier()

    with mem:
        zq, zk, zg, yt = mem([P, T]), mem([P, TC]), mem([P, TC]), mem([P, T])
        qh, ql = mem([P, T], R), mem([P, T], R)
        kh, kl = mem([P, TC], R), mem([P, TC], R)
        vh, vl = mem([P, 10, 128], R), mem([P, 10, 128], R)
        bt = [mem([P, 14, 64]) for _ in range(2)]
        bi = [mem([P, 640]) for _ in range(2)]
        at = Attention([[0, 1], [2, 3]], [4, 5], [6], [7], T)
        CHO = {"g": CH1, "q": CH1, "k": CH2}
        for _ in jobs(CHO, None, {"q": "dq0", "k": "dk0"}, None):
            pass
        START = {0: (0, 7), 1: (0, 5), 6: (8, 3), 7: (8, 1)}
        for j in range(4):
            t_b = []
            for i in range(2):
                t = move(bt[i][:, :, :], biasD[2 * j + i])
                cm = cc("col").rearrange("p (a c) -> p a c", a=1).to_broadcast([P, 14, 64])
                t = tt(bt[i][:, :, :], bt[i][:, :, :], cm, ALU.add, t, q=G)
                t = V.op(lambda e, i=i: e.tensor_copy(bi[i][:, :], bt[i][:, 2:12, :].rearrange("p a c -> p (a c)")), t)
                for rows, c0, c1 in (((0, 64), 512, 640), ((64, 128), 0, 64), ((64, 128), 576, 640)):
                    t = V.op(lambda e, i=i, rows=rows, c0=c0, c1=c1: e.memset(bi[i][rows[0]:rows[1], c0:c1], NEG), t)
                t_b.append(t)
            V.wait(*t_b)

            ready = split(qh[:, :], ql[:, :], zq[:, :], *ev["q"]) + split(kh[:, :], kl[:, :], zk[:, :], *ev["k"])
            e_ = copy_to(lambda t0, tn: zg[:, t0:t0 + tn])
            linear(f"dv{j}", h_rhs, CH2, e_)
            ready += to_token_major(zg, 10, [(vh, vl, 0, 0, 128)], e_.toks)
            barrier()
            units = []
            for b0 in range(0, 8, 2):
                inner = 2 <= b0 <= 4
                tiles = range(b0 - 2, b0 + 4) if inner else range(0, 4) if b0 == 0 else range(4, 8)
                for i in range(2):
                    rows = slice(64 * i, 64 * i + 64)
                    fronts = []
                    for b in (b0, b0 + 1):
                        q = pair(qh, ql, 64 * i, 64 * i + 64, 128 * b, 128)
                        if inner:
                            first, n, s0, bias = b - 2, 640, 128, bi[i][:, :]
                        else:
                            first, n, s0 = tiles[0], 512, 0
                            v0 = START[b][1] - 1
                            bias = bt[i][:, v0:v0 + 8, :].rearrange("p a c -> p (a c)")
                        keys = [Keys(kh, kl, 64 * i, 64 * i + 64, a) for a in (128 * first, T)]
                        fronts.append({
                            "pieces": [(s0, n, 128 * (first - tiles[0]), bias), (s0 + n, 256, 768, None)],
                            "chunks": [(s0, n, [(q, keys[0])]), (s0 + n, 256, [(q, keys[1])])],
                            "pads": [128 * (y - tiles[0]) for y in tiles if not first <= y < first + n // 128]})
                    kt = [(768, 8), (896, 9)] + [(128 * (y - tiles[0]), y) for y in tiles]
                    units.append({"fronts": fronts, "keys": [(e0, vh[:, y, :], vl[:, y, :]) for e0, y in kt],
                                  "evac": plain(yt, rows, b0)})
            nxt = {"q": f"dq{j + 1}", "k": f"dk{j + 1}"} if j < 3 else {}
            at.run(units, ready, Fill(jobs(CHO, f"og{4 + j}", nxt, at.fill_banks), steps_of(CHO, True, nxt)))
            t = act(zg[:, 0:T], zg[:, 0:T], ACT.Silu, A.last, *eg[0].toks)
            t = tt(yt[:, :], yt[:, :], zg[:, 0:T], ALU.mult, t)
            y_store(4 + j, yt, T, t)
            barrier()

    SC = 192.0 ** -0.5
    with mem:
        cqh, cql = mem([P, 2, T], R), mem([P, 2, T], R)
        ckh, ckl = mem([P, TC], R), mem([P, TC], R)
        rph, rpl = mem([P, TC], R), mem([P, TC], R)
        gts = [mem([P, T]) for _ in range(4)]
        with mem:
            zc = mem([P, 2, T])
            zk, zr = mem([P, TC]), mem([P, TC])
            tmp = [mem([P, 512]) for _ in range(4)]
            evs = []
            for j in range(2):
                e_ = copy_to(lambda t0, tn, j=j: zc[:, j, t0:t0 + tn])
                linear(f"cq{j}", h_rhs, CH1, e_)
                evs += e_.toks
            ek = copy_to(lambda t0, tn: zk[:, t0:t0 + tn])
            linear("ckv", h_rhs, CH2, ek)
            er = copy_to(lambda t0, tn: zr[:, t0:t0 + tn])
            linear("ckr", h_rhs, CH2, er)
            half = [g[:, a:a + 512] for g in gts for a in (0, 512)]
            norm_split(lambda k, t0, tn: zc[:, k, t0:t0 + tn], 2, cc("o256"), CH1,
                       lambda k, c: vc("qn_g", k), None, evs,
                       lambda k, t0, tn: cqh[:, k, t0:t0 + tn], lambda k, t0, tn: cql[:, k, t0:t0 + tn], half)
            barrier()
            norm_split(lambda k, t0, tn: zk[:, t0:t0 + tn], 1, cc("o128"), CH2,
                       lambda k, c: vc("kvn_g"), None, ek.toks,
                       lambda k, t0, tn: ckh[:, t0:t0 + tn], lambda k, t0, tn: ckl[:, t0:t0 + tn], half)
            post([(zr, P, CH2, None, "swap16", rph, rpl, er.toks)], tmp)
            barrier()
            for h in range(4):
                linear(f"og{h}", h_rhs, CH1, gate_evac(gts[h]))
            barrier()
        with mem.over(h_at):
            zq = mem([P, TC])
            qnh, qnl = mem([P, T], R), mem([P, T], R)
            qph, qpl = mem([P, T], R), mem([P, T], R)
            knh, knl = mem([P, TC], R), mem([P, TC], R)
            vh, vl = mem([P, 10, 128], R), mem([P, 10, 128], R)
            at = Attention([[0, 1, 2], [3, 4, 5]], [6], [7], [], TC)
            tmp = [x[:, a:a + 512] for x in at.E for a in (0, 512)]
            yt = zq

            def q_rhs(k, t0, tn):
                return cqh[:, k, t0:t0 + tn], cql[:, k, t0:t0 + tn]

            def kv_rhs(k, t0, tn):
                return ckh[:, t0:t0 + tn], ckl[:, t0:t0 + tn]

            def ev_split(hi, lo):
                toks = []

                def evac(o, t0, tn, tok):
                    t = split(hi[:, t0:t0 + tn], lo[:, t0:t0 + tn], o, tok)
                    toks.extend(t)
                    return t
                evac.toks = toks
                return evac

            for h in range(4):
                ready = []
                if h % 2 == 0:
                    e_ = copy_to(lambda t0, tn: zq[:, t0:t0 + tn])
                    linear(f"qp{h // 2}", q_rhs, CH1, e_)
                    ready += post([(zq, P, CH1, None, "swap16", qph, qpl, e_.toks)], tmp)
                e1 = ev_split(qnh, qnl)
                linear(f"qn{h}", q_rhs, CH1, e1)
                e2 = ev_split(knh, knl)
                linear(f"kn{h}", kv_rhs, CH2, e2)
                A.wait(*ready)
                e3 = copy_to(lambda t0, tn: zq[:, t0:t0 + tn])
                linear(f"vn{h}", kv_rhs, CH2, e3)
                ready += to_token_major(zq, 10, [(vh, vl, 0, 0, 128)], e3.toks)
                barrier()
                p0 = 64 * (h % 2)
                units = []
                for b0 in range(0, 8, 2):
                    fronts = []
                    for b in (b0, b0 + 1):
                        terms = [(pair(qnh, qnl, 0, P, 128 * b, 128), Keys(knh, knl, 0, P, 0)),
                                 (pair(qph, qpl, p0, p0 + 64, 128 * b, 128), Keys(rph, rpl, p0, p0 + 64, 0))]
                        fronts.append({"pieces": [(0, TC, 0, None)], "chunks": [(0, TC, terms)], "scale": SC})
                    units.append({"fronts": fronts, "keys": [(128 * y, vh[:, y, :], vl[:, y, :]) for y in range(10)],
                                  "evac": gated(yt, gts[h], slice(0, P), b0)})
                at.run(units, ready + e1.toks + e2.toks)
                y_store(h, yt, T, V.last)
                barrier()

    with mem:
        X = mem([P, 8, T])
        t_x = [move(X[:, :, :], x1_d.rearrange("k p t -> p k t"))]
        PE.wait(*load_split(y_d, T))
        V.wait(*t_x)
        for d in range(8):
            linear(f"oo{d}", h_rhs, CH1, add_gated(d))
        barrier()
        sq = [mem([P, 512]) for _ in range(2)]
        rs = [mem([P, 512]) for _ in range(2)]
        n, sq_free = 0, [[], []]
        for c, (t0, tn) in enumerate(CH1):
            b = take()
            for k in range(8):
                s = sq[n % 2]
                t = act(s[:, :], X[:, k, t0:t0 + tn], ACT.Square, sq_free[n % 2])
                PE.wait(t)
                m = mm(bank(b), cc("o1024"), s[:, :], k == 0, k == 7)
                sq_free[n % 2] = [m]
                n += 1
            t, ta = root(rs[c][:, :], bank(b), m)
            bank_free[b] = [ta]
            for k in range(8):
                t1 = stt(X[:, k, t0:t0 + tn], X[:, k, t0:t0 + tn], vc("fin_g", k), rs[c][:, :], ALU.mult, ALU.mult, t)
        s_out = Slot(sem("s_out"))
        t_o = SP.dma(out.rearrange("k p t -> p k t"), X[:, :, :], s_out, t1)
        SP.wait(t_o)
        barrier()

    queues = (PE, A, V, G, SP)
    for q in queues:
        q.number()
    with nc.Block() as block:
        @block.tensor
        def _(e):
            PE.emit(e)

        @block.scalar
        def _(e):
            A.emit(e)

        @block.vector
        def _(e):
            V.emit(e)

        @block.gpsimd
        def _(e):
            G.emit(e)

        @block.sync
        def _(e):
            SP.emit(e)




def columns(v):
    return np.ascontiguousarray(np.asarray(v).reshape(-1, P).T)


def constants():
    p = np.arange(P)
    out = {"ident": np.eye(P)}
    for n in (1024, 256, 128):
        out[f"o{n}"] = np.full((P, P), 1.0 / n)
    out["o64"] = (p[:, None] // 64 == p[None, :] // 64) / 64.0
    out["swap32"] = (p[:, None] == (p ^ 32)[None, :]) * 1.0
    out["swap16"] = (p[:, None] == (p ^ 16)[None, :]) * 1.0
    j = np.arange(384)
    out["win"] = np.where(np.abs(p[:, None] - j[None, :] + 128) <= 128, 0.0, NEG)
    c = np.arange(64)
    cs = np.clip(p % 64 - 8, 0, 48)[:, None]
    out["col"] = np.where((c[None, :] >= cs) & (c[None, :] < cs + 16), 0.0, NEG)
    cst = np.concatenate([out[n] for n, _ in CONSTS], axis=1).astype(np.float32)

    f = np.float32
    e = np.arange(0, 64, 2, dtype=f) / f(64)
    inv = f(1) / (10000.0 ** e.astype(np.float64)).astype(f)
    t = np.arange(T)
    ang = (t.astype(f)[:, None] * inv[None, :]).astype(f)
    ang1 = np.concatenate([ang, ang], axis=1)
    inv2 = (10000.0 ** (-np.arange(16) / 16)).astype(f)
    ar = ((t // 64).astype(f)[:, None] * inv2[None, :]).astype(f)
    ac = ((t % 64).astype(f)[:, None] * inv2[None, :]).astype(f)
    ang2 = np.concatenate([ar, ar, ac, ac], axis=1)
    d = np.arange(64)
    tabs = []
    for a, sign in ((ang1, np.where(d % 64 < 32, -1.0, 1.0)), (ang2, np.where(d % 32 < 16, -1.0, 1.0))):
        a = a.astype(np.float64)
        tabs.append([np.tile(np.cos(a).T, (2, 1)), np.tile((np.sin(a) * sign[None, :]).T, (2, 1))])
    return cst, np.array(tabs).astype(f)


def layout(inp):
    i = {k: np.asarray(v) for k, v in inp.items()}
    wi = i["w_in"][0]
    cuts = np.cumsum([256] * 6 + [256, 64, 4, 512, 512])
    aq, ak, av, bq, bk, bv, iq, ik, iw, cx, cy, gtw = np.split(wi, cuts, axis=1)
    ev = np.split(i["ev_w_in_2"][0], np.cumsum([512, 128, 128, 512, 512, 512]), axis=1)
    od = np.split(i["od_w_in_2"][0], np.cumsum([256, 128, 64, 512, 512, 512]), axis=1)
    wqb = i["od_c_w_qb_2"][0].reshape(256, 4, 192)
    wkv = i["od_c_w_kvb_2"][0].reshape(128, 4, 256)
    fi, fo = i["w_ffn_in"][0], i["w_ffn_out"][0]
    DFF = fo.shape[0]
    parts = {}

    def cols(a, j):
        return a[:, 128 * j:128 * j + 128]

    for j in range(2):
        for n, a in (("iq", iq), ("aq", aq), ("ak", ak), ("av", av), ("bq", bq), ("bk", bk), ("bv", bv)):
            parts[f"{n}{j}"] = cols(a, j)
        k_ = ev[1][:, 64 * j:64 * j + 64]
        parts[f"ek{j}"] = np.concatenate([k_, k_], axis=1)
        parts[f"qp{j}"] = wqb[:, 2 * j:2 * j + 2, 128:].reshape(256, 128)
        parts[f"cq{j}"] = cols(od[0], j)
    parts["ikw"] = np.concatenate([ik, iw], axis=1)
    parts["ev"] = ev[2]
    parts["ckv"] = od[1]
    parts["ckr"] = np.concatenate([od[2], od[2]], axis=1)
    for j in range(4):
        for n, a in (("cx", cx), ("cy", cy), ("eq", ev[0]), ("fq", ev[3]), ("fk", ev[4]), ("fv", ev[5]),
                     ("dq", od[3]), ("dk", od[4]), ("dv", od[5])):
            parts[f"{n}{j}"] = cols(a, j)
        parts[f"qn{j}"] = wqb[:, j, :128]
        parts[f"kn{j}"] = wkv[:, j, :128]
        parts[f"vn{j}"] = wkv[:, j, 128:]
    for d in range(8):
        for n in range(3):
            parts[f"gt{n}_{d}"] = cols(gtw, 8 * n + d)
        for n, a in (("wb", i["w_branch"][0]), ("wo", i["w_out"][0]), ("eo", i["ev_w_out_2"][0]),
                     ("oo", i["od_w_out_2"][0]), ("eg", ev[6]), ("og", od[6])):
            parts[f"{n}{d}"] = cols(a, d)
        f0 = 0
        for n, g in enumerate(FFN_GROUPS):
            parts[f"fo{n}_{d}"] = fo[128 * f0:128 * (f0 + g), 128 * d:128 * d + 128]
            f0 += g
    for f in range(DFF // 128):
        parts[f"fg{f}"] = cols(fi, f)
        parts[f"fu{f}"] = cols(fi[:, DFF:], f)
    for m in range(24):
        parts[f"ea{m}"] = cols(i["ev_w_ada_2"][0], m)
        parts[f"oa{m}"] = cols(i["od_w_ada_2"][0], m)
    at, total = weight_offsets()
    w = np.empty(total, np.float32)
    for name, (a, kt, m) in at.items():
        w[a:a + P * kt * m] = parts[name].reshape(kt, P, m).transpose(1, 0, 2).reshape(-1)

    def two(v):
        return np.concatenate([v, v])[:, None]

    vecs = {
        "g_mix": columns(i["g_mix"][0]), "aq_g": two(i["qk_gain_a"][0, 0]), "ak_g": two(i["qk_gain_a"][0, 1]),
        "bq_g": two(i["qk_gain_b"][0, 0]), "bk_g": two(i["qk_gain_b"][0, 1]), "ik_g": two(i["g_idx_k"][0]),
        "conv_w": np.concatenate([columns(i["conv_w"][0, j]) for j in range(4)], axis=1),
        "conv_b": columns(i["conv_b"][0]), "lru_ba": columns(i["lru_ba"][0]), "lru_bx": columns(i["lru_bx"][0]),
        "lam": columns(i["lru_lambda"][0]), "b_gate": columns(i["b_gate"][0]), "g_ffn": columns(i["g_ffn"][0]),
        "ev_g": columns(i["ev_norm_g_2"][0]), "ev_b": columns(i["ev_b_ada_2"][0]),
        "sink": np.broadcast_to(i["ev_a_sink_2"][0], (P, 8)),
        "blam": np.broadcast_to(i["ev_b_lambda_2"][0].reshape(1, 256), (P, 256)),
        "subln": i["ev_b_subln_g_2"][0][:, None], "od_g": columns(i["od_norm_g_2"][0]),
        "od_b": columns(i["od_b_ada_2"][0]), "qn_g": columns(i["od_c_q_norm_g_2"][0]),
        "kvn_g": columns(i["od_c_kv_norm_g_2"][0]), "fin_g": columns(i["final_norm_g_2"]),
        "cond": np.stack([columns(i["c_2"][0]), columns(i["c_ctx_2"])], axis=2).reshape(P, 16),
    }
    vec = np.concatenate([vecs[n] for n, _ in VECS], axis=1).astype(np.float32)
    cst, tabs = constants()
    xT = np.ascontiguousarray(i["x"][0].T).reshape(8, P, T)
    ctxT = np.ascontiguousarray(i["ctx_2"][0].T).reshape(8, P, 256)
    p, j = np.arange(P)[:, None], np.arange(640)[None, :]
    biasA = np.ascontiguousarray(i["rel_bias"][0][:, np.clip(512 + p - j, -128, 128) + 128].transpose(1, 0, 2))
    dc = np.clip(np.arange(64)[None, :] - (np.arange(P) % 64)[:, None] + 15, 0, 30)
    v = np.arange(1, 15)[None, :] - (np.arange(P) >= 64)[:, None]
    biasD = np.ascontiguousarray(i["od_d_rpb_2"][0][:, v[:, :, None], dc[:, None, :]])
    lru = np.zeros((P, 4, 2, P), np.float32)
    for n, a in enumerate((i["lru_wa"][0], i["lru_wx"][0])):
        for g in range(8):
            o = 64 * (g % 2)
            lru[o:o + 64, g // 2, n, o:o + 64] = a[g]
    return {"w": w, "vec": vec, "cst": cst, "tab": tabs, "xT": xT, "ctxT": ctxT, "biasA": biasA, "biasD": biasD,
            "lru": lru}


def kernel(**inputs):
    import concourse.bacc as _bacc
    from concourse.bass_utils import run_bass_kernel_spmd as _run

    arrays = layout(inputs)
    nc = _bacc.Bacc("TRN2", target_bir_lowering=False, num_devices=1)
    feed, args = {}, []
    for name, a in arrays.items():
        feed[f"in_{name}"] = np.ascontiguousarray(a)
        args.append(nc.dram_tensor(f"in_{name}", a.shape, F, kind="ExternalInput").ap())
    out = nc.dram_tensor("out_0", (8, P, T), F, kind="ExternalOutput").ap()
    build(nc, *args, out)
    r = _run(nc, [feed], core_ids=[0])
    got = r.results[0]["out_0"]
    return np.ascontiguousarray(np.asarray(got).reshape(1024, T).T).reshape(1, T, 1024)
```

```python
import numpy as np
import concourse.bass as bass
from concourse import mybir

F = mybir.dt.float32
R = mybir.dt.float32r
ACT = mybir.ActivationFunctionType
ALU = mybir.AluOpType
AX = mybir.AxisListType

P = 128
T = 1024
TC = 1280
EPS = 1e-6
NEG = -1e30
OUT_OF_RANGE = -3.0e38
TAKEN = -3.3e38
FFN_GROUPS = [4, 4, 4, 4, 3, 3]
CH1 = [(0, 512), (512, 512)]
CH2 = [(0, 512), (512, 512), (1024, 256)]



def weight_tiles():
    tiles = [("iq0", 8, 128), ("iq1", 8, 128), ("ikw", 8, 68)]
    for j in range(4):
        tiles += [(f"cx{j}", 8, 128), (f"cy{j}", 8, 128)]
    tiles += [(f"gt{i}_{d}", 8, 128) for d in range(8) for i in range(3)]
    tiles += [(f"{x}{m}", 8, 128) for x in ("ea", "oa") for m in range(24)]
    tiles += [("aq0", 8, 128), ("ak0", 8, 128)]
    pairs = ["a0", "a1", "b0", "b1"]
    for n, x in enumerate(pairs):
        tiles += [(f"{x[0]}v{x[1]}", 8, 128)]
        if n < 3:
            tiles += [(f"{pairs[n + 1][0]}{s}{pairs[n + 1][1]}", 8, 128) for s in "qk"]
    for d in range(8):
        tiles += [(f"wb{d}", 8, 128)]
    tiles += [(f"wo{d}", 8, 128) for d in range(8)]
    f0 = 0
    for n, g in enumerate(FFN_GROUPS):
        for f in range(f0, f0 + g):
            tiles += [(f"fg{f}", 8, 128), (f"fu{f}", 8, 128)]
        tiles += [(f"fo{n}_{d}", g, 128) for d in range(8)]
        f0 += g
    tiles += [("eq0", 8, 128), ("ek0", 8, 128), ("ev", 8, 128)]
    for j in range(4):
        tiles += [(f"eq{j + 1}", 8, 128)] if j < 3 else [(f"f{s}0", 8, 128) for s in "qkv"]
        if j == 1:
            tiles += [("ek1", 8, 128)]
        tiles += [(f"eg{j}", 8, 128)]
    for h in range(4):
        if h < 3:
            tiles += [(f"f{s}{h + 1}", 8, 128) for s in "qkv"]
        tiles += [(f"eg{4 + h}", 8, 128)]
    tiles += [(f"eo{d}", 8, 128) for d in range(8)]
    tiles += [("dq0", 8, 128), ("dk0", 8, 128), ("dv0", 8, 128)]
    for j in range(4):
        if j < 3:
            tiles += [(f"d{s}{j + 1}", 8, 128) for s in "qkv"]
        tiles += [(f"og{4 + j}", 8, 128)]
    tiles += [("cq0", 8, 128), ("cq1", 8, 128), ("ckv", 8, 128), ("ckr", 8, 128)]
    tiles += [(f"og{h}", 8, 128) for h in range(4)]
    for h in range(4):
        if h % 2 == 0:
            tiles += [(f"qp{h // 2}", 2, 128)]
        tiles += [(f"qn{h}", 2, 128), (f"kn{h}", 1, 128), (f"vn{h}", 1, 128)]
    tiles += [(f"oo{d}", 8, 128) for d in range(8)]
    return tiles


def weight_offsets():
    at, out = 0, {}
    for name, kt, m in weight_tiles():
        out[name] = (at, kt, m)
        at += P * kt * m
    return out, at


VECS = [("g_mix", 8), ("aq_g", 1), ("ak_g", 1), ("bq_g", 1), ("bk_g", 1), ("ik_g", 1), ("conv_w", 16),
        ("conv_b", 4), ("lru_ba", 4), ("lru_bx", 4), ("lam", 4), ("b_gate", 24), ("g_ffn", 8),
        ("ev_g", 8), ("ev_b", 24), ("sink", 8), ("subln", 1), ("od_g", 8), ("od_b", 24),
        ("qn_g", 2), ("kvn_g", 1), ("fin_g", 8), ("cond", 16), ("blam", 256)]
CONSTS = [("ident", 128), ("o1024", 128), ("o64", 128), ("o256", 128), ("o128", 128), ("swap32", 128),
          ("swap16", 128), ("win", 384), ("col", 64)]


def offsets(table):
    at, out = 0, {}
    for name, n in table:
        out[name] = (at, n)
        at += n
    return out, at




class Tok:
    def __init__(self, sem, value=None):
        self.sem, self.value, self.wanted = sem, value, False


class Slot:

    def __init__(self, sem):
        self.sem, self.count = sem, 0


class Queue:
    def __init__(self, sem):
        self.sem, self.items, self.last = sem, [], None

    def wait(self, *toks):
        for t in toks:
            if isinstance(t, (list, tuple)):
                self.wait(*t)
            elif t is not None:
                t.wanted = True
                self.items.append((None, t))

    def op(self, fn, *waits):
        self.wait(*waits)
        t = Tok(self.sem)
        self.items.append((fn, t))
        self.last = t
        return t

    def dma(self, out, in_, slot, *waits):
        self.wait(*waits)
        slot.count += 16
        t = Tok(slot.sem, slot.count)
        self.items.append((lambda e: e.dma_start(out, in_), t))
        return t

    def number(self):
        n = 0
        for fn, t in self.items:
            if fn is not None and t.sem is self.sem and t.wanted:
                n += 1
                t.value = n

    def emit(self, e):
        seen = {}
        for fn, t in self.items:
            if fn is None:
                if seen.get(id(t.sem), 0) < t.value:
                    e.wait_ge(t.sem, t.value)
                    seen[id(t.sem)] = t.value
            else:
                ins = fn(e)
                if t.sem is not self.sem:
                    ins.then_inc(t.sem, 16)
                elif t.wanted:
                    ins.then_inc(t.sem, 1)


class Memory:

    def __init__(self, nc):
        self.nc, self.at, self.n, self.marks = nc, (nc.sbuf_base + 63) // 64 * 64, 0, []

    def __call__(self, shape, dt=F):
        size = 4
        for s in shape[1:]:
            size *= s
        t = self.nc.alloc_sbuf_tensor_at(f"m{self.n}", list(shape), dt, offset=self.at)
        self.n += 1
        self.at += (size + 63) // 64 * 64
        assert self.at <= self.nc.sbuf_usable_end, (self.at, self.nc.sbuf_usable_end)
        return t

    def __enter__(self):
        self.marks.append(self.at)
        return self

    def __exit__(self, *a):
        self.at = self.marks.pop()

    def over(self, at):
        self.marks.append(self.at)
        self.at = at
        return _Over(self)


class _Over:
    def __init__(self, mem):
        self.mem = mem

    def __enter__(self):
        return self.mem

    def __exit__(self, *a):
        self.mem.at = self.mem.marks.pop()


def build(nc, w, vec_d, cst_d, tab_d, xT, ctxT, biasA, biasD, lruw, out):
    W_AT, _ = weight_offsets()
    V_AT, NVEC = offsets(VECS)
    C_AT, NCST = offsets(CONSTS)

    sems = {}

    def sem(name):
        sems[name] = nc.alloc_semaphore(name)
        return sems[name]

    PE, A, V, G, SP = (Queue(sem(f"s_{n}")) for n in ("pe", "act", "dve", "pool", "sp"))
    free_slots = [Slot(sem(f"s_dma{i}")) for i in range(12)]
    hw_slots = [Slot(sem(f"s_hw{i}")) for i in range(4)]
    pending = []

    mem = Memory(nc)
    PS = nc.alloc_psum_tensor("PS", [P, 4096], F)
    x1_d = nc.dram_tensor("x1_scratch", [8, P, T], F, kind="Internal").ap()
    y_d = nc.dram_tensor("y_scratch", [8, P, TC], F, kind="Internal").ap()
    g_d = nc.dram_tensor("g_scratch", [24, P, T], F, kind="Internal").ap()


    def move(out_ap, in_ap, *waits, q=None):
        q = q or G
        pool = free_slots if q is G else hw_slots
        s = pool[0]
        pool.append(pool.pop(0))
        if s.count:
            q.wait(Tok(s.sem, s.count))
        t = q.dma(out_ap, in_ap, s, *waits)
        pending.append(t)
        return t

    def barrier():
        lasts = [q.last for q in (PE, A, V, G) if q.last is not None]
        for q in (PE, A, V, G):
            q.wait(*[t for t in lasts if t is not q.last], *pending)
        pending.clear()

    bank_free = [[] for _ in range(8)]
    turn, fill_turn = [0], [0]

    def bank(b):
        return PS[:, 512 * b:512 * b + 512]

    def take(first=0, n=6):
        b = first + turn[0] % n
        turn[0] += 1
        PE.wait(*bank_free[b])
        return b

    def fill_bank(banks):
        if not banks:
            return take()
        b = banks[fill_turn[0] % len(banks)]
        fill_turn[0] += 1
        PE.wait(*bank_free[b])
        return b

    h_at = mem.at
    Hh = mem([P, 8, TC], R)
    Hl = mem([P, 8, TC], R)
    NRAW, NSPL = 2, 2
    raw = [mem([P, 1024]) for _ in range(NRAW)]
    whi = [mem([P, 1024], R) for _ in range(NSPL)]
    wlo = [mem([P, 1024], R) for _ in range(NSPL)]
    NVEC -= 256
    vec = mem([P, NVEC])
    cst = mem([P, NCST])
    tabs = mem([P, 2, T])
    epst = mem([P, 1])
    lam_t = mem([P, 8])
    mods = {kind: (mem([P, 24, 2]), mem([P, 8, 2])) for kind in ("ev", "od")}
    csil = mem([P, 16])
    nsink = mem([P, 8])

    def vc(name, i=0, n=1):
        a = V_AT[name][0] + i
        return vec[:, a:a + n]

    def cc(name, r=P, n=None):
        a, m = C_AT[name]
        return cst[0:r, a:a + (n or m)]

    ident = cc("ident")

    order = [x for x in weight_tiles() if x[0][:2] != "ea"]
    raw_slot = [Slot(sem(f"s_w{i}")) for i in range(NRAW)]
    raw_free = [[] for _ in range(NRAW)]
    spl_free = [[] for _ in range(NSPL)]
    st = {"load": 0, "prep": 0, "use": 0, "spl": 0, "lo": V}
    loaded, parts = {}, {}

    def w_load(upto):
        while st["load"] < min(upto, len(order)):
            i = st["load"]
            name, kt, m = order[i]
            s = i % NRAW
            at = W_AT[name][0]
            loaded[i] = SP.dma(raw[s][:, 0:kt * m],
                               w[at:at + P * kt * m].rearrange("(p c) -> p c", p=P), raw_slot[s], *raw_free[s])
            st["load"] += 1

    def w_prep(upto):
        while st["prep"] < min(upto, len(order)):
            i = st["prep"]
            name, kt, m = order[i]
            if name[:2] not in ("ea", "oa"):
                s, c, r = st["spl"] % NSPL, kt * m, i % NRAW
                hi, lo, src = whi[s][:, 0:c], wlo[s][:, 0:c], raw[r][:, 0:c]
                t1 = A.op(lambda e, hi=hi, src=src: e.copy(hi, src), loaded[i], spl_free[s])
                t2 = st["lo"].op(lambda e, hi=hi, lo=lo, src=src: e.tensor_tensor(lo, src, hi.bitcast(F), ALU.subtract),
                                 loaded[i], spl_free[s], t1)
                raw_free[r] = [t1, t2]
                parts[i] = (s, [t1, t2])
                st["spl"] += 1
            st["prep"] += 1

    def w_get(name):
        i = st["use"]
        assert order[i][0] == name, (order[i], name)
        st["use"] += 1
        _, kt, m = order[i]
        w_load(i + NRAW)
        w_prep(i + 2)
        if i not in parts:
            r = i % NRAW
            PE.wait(loaded[i])

            def release(tok):
                raw_free[r] = [tok]
            return (lambda k: raw[r][:, k * m:(k + 1) * m]), kt, release
        s, toks = parts[i]
        PE.wait(*toks)

        def release(tok):
            spl_free[s] = [tok]
        return (lambda k: (whi[s][:, k * m:(k + 1) * m], wlo[s][:, k * m:(k + 1) * m])), kt, release

    def mm3(o, L, Rr, start, stop):
        PE.op(lambda e: e.matmul(o, L[0], Rr[0], start=start, stop=False))
        PE.op(lambda e: e.matmul(o, L[0], Rr[1], start=False, stop=False))
        return PE.op(lambda e: e.matmul(o, L[1], Rr[0], start=False, stop=stop))

    def mm(o, L, Rr, start=True, stop=True):
        return PE.op(lambda e: e.matmul(o, L, Rr, start=start, stop=stop))

    def linear_steps(name, rhs, chunks, evac, rows=P, banks=None):
        get, kt, release = w_get(name)
        for n, (t0, tn) in enumerate(chunks):
            b = fill_bank(banks)
            o = bank(b)[0:rows, 0:tn]
            for k in range(kt):
                tok = mm3(o, get(k), rhs(k, t0, tn), k == 0, k == kt - 1)
                if k == kt - 1:
                    bank_free[b] = evac(o, t0, tn, tok)
                    if n == len(chunks) - 1:
                        release(tok)
                yield

    def linear(*args, **kw):
        for _ in linear_steps(*args, **kw):
            pass

    class Fill:

        def __init__(self, jobs, steps):
            self.jobs, self.left, self.done = jobs, steps, 0

        def pull(self, n):
            for _ in range(n):
                if next(self.jobs, self) is self:
                    self.left = 0
                    return
                self.left, self.done = max(0, self.left - 1), self.done + 1

        def drain(self):
            for _ in self.jobs:
                pass
            self.left = 0

    h_ready = {}

    def h_rhs(k, t0, tn):
        PE.wait(*h_ready.get((k, t0), []))
        return Hh[:, k, t0:t0 + tn], Hl[:, k, t0:t0 + tn]

    def act(out_, in_, f, *waits, **kw):
        return A.op(lambda e: e.activation(out_, in_, f, **kw), *waits)

    def split(hi, lo, src, *waits):
        t1 = A.op(lambda e: e.copy(hi, src), *waits)
        t2 = V.op(lambda e: e.tensor_tensor(lo, src, hi.bitcast(F), ALU.subtract), *waits, t1)
        return [t1, t2]

    def tt(out_, a, b, op, *waits, q=None):
        return (q or V).op(lambda e: e.tensor_tensor(out_, a, b, op), *waits)

    def ts(out_, a, s1, s2, o0, o1, *waits):
        if s2 is None:
            return V.op(lambda e: e.tensor_scalar(out_, a, s1, None, o0), *waits)
        return V.op(lambda e: e.tensor_scalar(out_, a, s1, s2, o0, o1), *waits)

    def stt(out_, a, s, b, o0, o1, *waits, q=None):
        return (q or V).op(lambda e: e.scalar_tensor_tensor(out=out_, in0=a, scalar=s, in1=b, op0=o0, op1=o1), *waits)

    def root(rs, ps, tok):
        n = rs.shape[0]
        t = act(rs, ps, ACT.Sqrt, tok, bias=epst[0:n, 0:1])
        return V.op(lambda e: e.reciprocal(rs, rs), t), t

    class Squares:

        def __init__(self, rs, sq):
            self.rs, self.sq = rs, sq
            self.free, self.n, self.t = [[] for _ in sq], 0, {}

        def add(self, c, x, tn, *waits):
            r = self.rs[c][:, 0:tn]
            if c not in self.t:
                self.t[c] = act(r, x, ACT.Square, *waits)
                return
            i = self.n % len(self.sq)
            self.n += 1
            q = self.sq[i][:, 0:tn]
            t = act(q, x, ACT.Square, *waits, self.free[i])
            self.t[c] = tt(r, r, q, ALU.add, self.t[c], t)
            self.free[i] = [self.t[c]]

    def norm_bufs(ns, nr, nt, pieces=None):
        pieces = pieces or [mem([P, 512]) for _ in range(ns + nr + nt)]
        return pieces[0:ns], pieces[ns:ns + nr], pieces[ns + nr:ns + nr + nt]

    def norm_split(src, kt, ones, chunks, g, shift, ready, hi, lo, bufs, sums=None):
        sq, rs, tmp = bufs
        if sums is None:
            sums = Squares(rs, sq)
            for c, (t0, tn) in enumerate(chunks):
                for k in range(kt):
                    sums.add(c, src(k, t0, tn), tn, ready(k) if callable(ready) else ready)
        means = []
        for c, (t0, tn) in enumerate(chunks):
            PE.wait(sums.t[c])
            b = take()
            o = bank(b)[:, 0:tn]
            means.append((b, o, mm(o, ones, rs[c][:, 0:tn])))
        root_t = []
        for c, (t0, tn) in enumerate(chunks):
            b, o, m = means[c]
            t, ta = root(rs[c][:, 0:tn], o, m)
            bank_free[b] = [ta]
            root_t.append(t)
        n, out_toks, tmp_free = 0, {}, [[] for _ in tmp]
        for c, (t0, tn) in enumerate(chunks):
            r = rs[c][:, 0:tn]
            for k in range(kt):
                i = n % len(tmp)
                q = tmp[i][:, 0:tn]
                t1 = stt(q, src(k, t0, tn), g(k, c), r, ALU.mult, ALU.mult, root_t[c], tmp_free[i],
                         ready(k) if callable(ready) else ready)
                h, l_ = hi(k, t0, tn), lo(k, t0, tn)
                sh = shift(k, c) if shift else None
                on = G if n % 3 else V
                if sh is None:
                    t2 = A.op(lambda e, h=h, q=q: e.copy(h, q), t1)
                    t3 = tt(l_, q, h.bitcast(F), ALU.subtract, t2, q=on)
                elif n % 2:
                    t2 = act(q, q, ACT.Identity, t1, bias=sh)
                    t2 = A.op(lambda e, h=h, q=q: e.copy(h, q), t2)
                    t3 = tt(l_, q, h.bitcast(F), ALU.subtract, t2, q=G)
                else:
                    t2 = act(h, q, ACT.Identity, t1, bias=sh)
                    t3 = stt(l_, q, sh, h.bitcast(F), ALU.add, ALU.subtract, t2)
                tmp_free[i] = [t3]
                n += 1
                out_toks[k, t0] = [t2, t3]
        return out_toks

    with mem:
        mem([P, 7872])
        low_end = mem.at
        X = mem([P, 8, T])
        bufs = [norm_bufs(2, 1, 3) for _ in CH1]
        ld, blam = mem([P, 64]), mem([P, 256])
    t_c = [move(vec[:, :], vec_d[:, 0:NVEC]), move(cst[:, :], cst_d)]
    t_x = {(k, t0): move(X[:, k, t0:t0 + tn], xT[k][:, t0:t0 + tn]) for t0, tn in CH1 for k in range(8)}
    t_blam = move(blam[:, :], vec_d[:, NVEC:NVEC + 256])
    t_tab = move(tabs[:, :, :], tab_d[0].rearrange("a p t -> p a t"))
    t_e = V.op(lambda e: e.memset(epst[:, :], EPS))
    w_load(NRAW)
    for q in (PE, A, V, G):
        q.wait(*t_c, t_e)

    def copy_to(dst, scale=1.0):
        toks = []

        def evac(o, t0, tn, tok):
            d = dst(t0, tn)
            if scale == 1.0:
                t = A.op(lambda e: e.copy(d, o), tok)
            else:
                t = A.op(lambda e: e.mul(d, o, scale), tok)
            toks.append(t)
            return [t]
        evac.toks = toks
        return evac

    def post(items, bufs, between=None, after=()):
        work = [(it, t0, tn) for it in items for t0, tn in it[2]]
        out_t, old = [], list(after)
        deep = len(bufs) // 2
        for w0 in range(0, len(work), deep):
            batch = []
            for n, ((z, rows, _, gain, swap, hi, lo, toks), t0, tn) in enumerate(work[w0:w0 + deep]):
                batch.append({"z": z[0:rows, t0:t0 + tn], "rows": rows, "t0": t0, "tn": tn, "gain": gain,
                              "swap": swap if t0 < T else None, "hi": hi[0:rows, t0:t0 + tn],
                              "lo": lo[0:rows, t0:t0 + tn], "t": list(toks) + list(after),
                              "x": bufs[2 * n][0:rows, 0:tn], "y": bufs[2 * n + 1][0:rows, 0:tn]})
            normed = [c for c in batch if c["gain"] is not None]
            for c in normed:
                t = act(c["x"], c["z"], ACT.Square, *c["t"], *old)
                PE.wait(t)
                c["b"] = take()
                c["o"] = bank(c["b"])[0:c["rows"], 0:c["tn"]]
                c["m"] = mm(c["o"], cc("o64", c["rows"], c["rows"]), c["x"])
            if normed and between:
                between()
            for c in normed:
                t, ta = root(c["x"], c["o"], c["m"])
                bank_free[c["b"]] = [ta]
                c["t"] = [stt(c["z"], c["z"], c["gain"][0:c["rows"], :], c["x"], ALU.mult, ALU.mult, t, *c["t"])]
            for c in batch:
                if c["swap"]:
                    PE.wait(*c["t"])
                    b = take()
                    o = bank(b)[0:c["rows"], 0:c["tn"]]
                    m = mm(o, cc(c["swap"], c["rows"], c["rows"]), c["z"])
                    cos, sin = (tabs[0:c["rows"], i, c["t0"]:c["t0"] + c["tn"]] for i in range(2))
                    tg = tt(c["x"], c["z"], cos, ALU.mult, *c["t"], *old, q=G)
                    tv = tt(c["y"], o, sin, ALU.mult, m, *old)
                    bank_free[b] = [tv]
                    c["t"] = [tg, tv, m]
            if between:
                between()
            last = []
            for c in batch:
                if c["swap"]:
                    c["t"] = [tt(c["z"], c["x"], c["y"], ALU.add, *c["t"])]
                last += split(c["hi"], c["lo"], c["z"], *c["t"])
            old = last
            out_t += last
        return out_t

    def to_token_major(z, tiles, parts_, z_toks):
        out_t = []
        for _ in token_major_steps(z, tiles, parts_, z_toks, None, out_t):
            pass
        return out_t

    def token_major_steps(z, tiles, parts_, z_toks, banks, out_t):
        PE.wait(*z_toks)
        for k0 in range(0, tiles, 4):
            n = min(4, tiles - k0)
            b = fill_bank(banks)
            for i in range(n):
                o = PS[:, 512 * b + 128 * i:512 * b + 128 * i + 128]
                src = z[:, (k0 + i) * 128:(k0 + i) * 128 + 128]
                m = PE.op(lambda e, o=o, src=src: e.transpose(o, src, ident))
            o = PS[:, 512 * b:512 * b + 128 * n].rearrange("p (a c) -> p a c", c=128)
            t_h = [act(vh[:, k0:k0 + n, c0:c0 + fn], o[:, :, f0:f0 + fn], ACT.Copy, m)
                   for vh, _, c0, f0, fn in parts_]
            bank_free[b] = [tt(vl[:, k0:k0 + n, c0:c0 + fn], o[:, :, f0:f0 + fn],
                               vh[:, k0:k0 + n, c0:c0 + fn].bitcast(F), ALU.subtract, *t_h)
                            for vh, vl, c0, f0, fn in parts_]
            out_t += bank_free[b]
            yield

    def post_steps(items, bufs, banks, done):
        free = [[] for _ in bufs]
        work = [(it, t0, tn) for it in items for t0, tn in it[1]]
        for w0 in range(0, len(work), len(bufs)):
            batch = []
            for i, ((z, _, gain, swap, toks), t0, tn) in enumerate(work[w0:w0 + len(bufs)]):
                batch.append({"i": i, "z": z[:, t0:t0 + tn], "x": bufs[i][:, 0:tn], "t": list(toks), "t0": t0,
                              "tn": tn, "gain": gain, "swap": swap if t0 < T else None})
            normed = [c for c in batch if c["gain"] is not None]
            for c in normed:
                c["sq"] = act(c["x"], c["z"], ACT.Square, *c["t"], free[c["i"]])
                yield
            for c in normed:
                PE.wait(c["sq"])
                b = fill_bank(banks)
                o = bank(b)[:, 0:c["tn"]]
                m = mm(o, cc("o64"), c["x"])
                t, ta = root(c["x"], o, m)
                bank_free[b] = [ta]
                c["t"] = free[c["i"]] = [stt(c["z"], c["z"], c["gain"], c["x"], ALU.mult, ALU.mult, t, *c["t"])]
                yield
                yield
            for c in batch:
                if c["swap"]:
                    PE.wait(*c["t"])
                    b = fill_bank(banks)
                    o = bank(b)[:, 0:c["tn"]]
                    m = mm(o, cc(c["swap"]), c["z"])
                    cos, sin = (tabs[:, a, c["t0"]:c["t0"] + c["tn"]] for a in range(2))
                    tg = tt(c["z"], c["z"], cos, ALU.mult, m, *c["t"], q=G)
                    tv = tt(c["x"], o, sin, ALU.mult, m, free[c["i"]])
                    bank_free[b] = [tv]
                    c["t"] = free[c["i"]] = [tt(c["z"], c["z"], c["x"], ALU.add, tg, tv)]
                    yield
                done += c["t"]

    def weave(main, side, every):
        for n, _ in enumerate(main):
            yield
            if n % every == every - 1:
                next(side, None)
        yield from side

    class Attention:

        def __init__(self, s_banks, pt_banks, o_banks, fill_banks, width, npt=2, second=0):
            self.s_at = [512 * b[0] for b in s_banks]
            self.s_banks, self.pt_banks, self.o_banks, self.fill_banks = s_banks, pt_banks, o_banks, fill_banks
            self.E = [mem([P, width]) for _ in range(4 + second)]
            self.second = second
            self.S = [mem([P, 8]) for _ in range(4 + second)]
            self.pth = [mem([P, 512], R) for _ in range(npt)]
            self.ptl = [mem([P, 512], R) for _ in range(npt)]
            self.npt = npt
            ne = len(self.E)
            self.e_free = [[] for _ in range(ne)]
            self.e_unread = [False] * ne
            self.pt_free = [[] for _ in range(self.npt)]
            self.ns = self.nb = self.nr = self.np = 0
            self.n_e = [0, 0]

        def start(self):
            self.s_free = [[t for b in banks for t in bank_free[b]] for banks in self.s_banks]
            self.todo, self.behind = [], None

        def qk(self, f):
            s = f["s"] = self.ns % len(self.s_at)
            self.ns += 1
            out_ = []
            for c0, cn, terms in f["chunks"]:
                at = self.s_at[s] + c0
                while cn:
                    m = min(cn, 512 - at % 512)
                    out_.append((PS[:, at:at + m], [(L, kf(m)) for L, kf in terms]))
                    terms = [(L, kf.after(m)) for L, kf in terms]
                    at, cn = at + m, cn - m
            PE.wait(*self.s_free[s])
            return out_

        def soft1(self, f):
            k = 1 if f.get("second") else 0
            e = 4 + self.n_e[1] % self.second if k else self.n_e[0] % 4
            self.n_e[k] += 1
            while self.e_unread[e]:
                self.step()
            f["e"], free = e, self.e_free[e]
            E, S = self.E[e], self.S[e]
            f["E"], f["S"] = E, S
            f["pad_t"] = []
            for c in f.get("pads", ()):
                pad = E[:, c:c + 128]
                f["pad_t"].append(G.op(lambda e_: e_.memset(pad, 0.0), *free))
            V.wait(f["tok"], free)
            scale, pieces = f.get("scale", 1.0), f["pieces"]
            base = self.s_at[f["s"]]
            mt, f["exp"] = [], []
            for a, (c0, n, e0, bias) in enumerate(pieces):
                src, d = PS[:, base + c0:base + c0 + n], E[:, e0:e0 + n]
                if bias is None:
                    neg = len(pieces) == 1 and scale == 1.0
                    o = S[:, 0:1] if neg else S[:, 1 + a:2 + a]
                    mt.append(self.reduce(o, src, neg))
                    f["exp"].append((d, src, a))
                else:
                    mt.append(self.biased(d, src, bias, S[:, 1 + a:2 + a]))
                    f["exp"].append((d, d, a))
            nm, t = S[:, 0:1], mt[-1]
            if len(pieces) == 2:
                t = ts(nm, S[:, 1:2], S[:, 2:3], -scale, ALU.max, ALU.mult, *mt)
            elif not (pieces[0][3] is None and scale == 1.0):
                t = ts(nm, S[:, 1:2], -scale, None, ALU.mult, None, *mt)
            if "sink" in f:
                t = ts(nm, nm, nsink[:, f["sink"]:f["sink"] + 1], None, ALU.min, None, t)
            f["nm_t"], f["mt"] = t, mt

        def reduce(self, o, src, neg):
            return V.op(lambda e: e.tensor_reduce(o, src, AX.X, ALU.max, negate=neg))

        def biased(self, d, src, bias, o):
            return V.op(lambda e: e.tensor_tensor_reduce(d, src, bias, 1.0, OUT_OF_RANGE, ALU.add, ALU.max, o))

        def soft2(self, f):
            S, scale = f["S"], f.get("scale", 1.0)
            A.wait(f["nm_t"], self.e_free[f["e"]])
            et = []
            for d, src, a in f["exp"]:
                et.append(act(d, src, ACT.Exp, bias=S[:, 0:1], scale=scale, accum_out=S[:, 3 + a:4 + a]))
            self.s_free[f["s"]] = [f["mt"][-1], et[-1]]
            if "sink" in f:
                et.append(act(S[:, 5:6], vc("sink", f["sink"]), ACT.Exp, bias=S[:, 0:1]))
            f["et"] = et

        def soft3(self, f):
            S, E = f["S"], f["E"]
            rs, ss, two = S[:, 6:7], S[:, 3:4], len(f["pieces"]) == 2
            V.wait(*f["et"])
            t = None
            if "sink" in f:
                ss = S[:, 7:8]
                t = ts(ss, S[:, 3:4], S[:, 4:5] if two else 0.0, S[:, 5:6], ALU.add, ALU.add)
            elif two:
                ss = S[:, 7:8]
                t = tt(ss, S[:, 3:4], S[:, 4:5], ALU.add)
            t = V.op(lambda e: e.reciprocal(rs, ss), t)
            if "first" in f:
                f0 = f["first"]
                n = f["pieces"][0][1]
                a, b = f0["E"][:, 0:n], E[:, 0:n]
                t = ts(rs, rs, lam_t[:, 1:2], None, ALU.mult, None, t)
                t = stt(a, b, rs, a, ALU.mult, ALU.add, t, f0["ready"])
                f0["ready"] = [t]
                self.e_free[f["e"]] = [t]
            elif f.get("lam"):
                a = E[:, 0:f["pieces"][0][1]]
                f["ready"] = [G.op(lambda e: e.tensor_scalar(a, a, rs, None, ALU.mult), t)]
            else:
                spans = []
                for _, n, e0, _ in f["pieces"]:
                    if spans and spans[-1][1] == e0:
                        spans[-1][1] = e0 + n
                    else:
                        spans.append([e0, e0 + n])
                f["ready"] = [ts(E[:, c0:c1], E[:, c0:c1], rs, None, ALU.mult, None, t) for c0, c1 in spans]
                f["ready"] += f["pad_t"]

        def queue(self, u):
            fr = [f for f in u["fronts"] if "first" not in f]
            for f in fr:
                self.e_unread[f["e"]] = True
            kts = u["keys"]
            groups = [kts[i:i + 2] for i in range(0, len(kts), 2)]
            ob = self.o_banks[self.np % len(self.o_banks)]
            self.np += 1
            O = PS[:, 512 * ob:512 * ob + 256]
            st_ = {}

            def turn_over(g):
                if g == 0:
                    PE.wait(*[f["ready"] for f in fr])
                b = self.pt_banks[self.nb % len(self.pt_banks)]
                self.nb += 1
                PE.wait(*bank_free[b])
                i = 0
                for e0, _, _ in groups[g]:
                    for f in fr:
                        m = self.turn(PS[:, 512 * b + i:512 * b + i + 128], f["E"][:, e0:e0 + 128])
                        i += 128
                r = self.nr % self.npt
                self.nr += 1
                h, l_, s = self.pth[r][:, 0:i], self.ptl[r][:, 0:i], PS[:, 512 * b:512 * b + i]
                toks = split(h, l_, s, m, self.pt_free[r])
                bank_free[b] = toks
                st_[g] = (r, toks)
                if g == len(groups) - 1:
                    for f in fr:
                        self.e_free[f["e"]] = [m]
                        self.e_unread[f["e"]] = False

            def multiply(g):
                r, (hi_t, lo_t) = st_[g]
                PE.wait(hi_t)
                if g == 0:
                    PE.wait(*bank_free[ob])
                last = g == len(groups) - 1
                for i, (_, vh, vl) in enumerate(groups[g]):
                    h = self.pth[r][:, 256 * i:256 * i + 256]
                    mm(O, vh, h, g == 0 and i == 0, False)
                    mm(O, vl, h, False, False)
                PE.wait(lo_t)
                for i, (_, vh, vl) in enumerate(groups[g]):
                    l_ = self.ptl[r][:, 256 * i:256 * i + 256]
                    m = mm(O, vh, l_, False, last and i == len(groups[g]) - 1)
                self.pt_free[r] = [m]
                if last:
                    bank_free[ob] = u["evac"](O, m)

            def step_of(g):
                def fn():
                    turn_over(g)
                    if self.behind:
                        self.behind()
                    self.behind = lambda: multiply(g)
                return fn

            self.todo += [step_of(g) for g in range(len(groups))]

        def turn(self, o, s):
            return PE.op(lambda e: e.transpose(o, s, ident))

        def step(self):
            self.todo.pop(0)()

        def run(self, units, ready, fill=None, head=0, tail=None, rest=None):
            self.start()
            one = len(self.s_at) == 1
            at2 = 0 if one else 1
            slots = sum(1 if one else -(-cn // 512) for u in units for f in u["fronts"] for _, cn, _ in f["chunks"])
            PE.wait(*ready)
            late = None
            for nu, u in enumerate(units):
                fr = u["fronts"]
                left = 0
                for i, f in enumerate(fr):
                    pieces = self.qk(f)
                    if i == 0:
                        left = (1 if one else len(pieces)) * (len(fr) - 1)
                    for a, (o, terms) in enumerate(pieces):
                        for x, (L, Rr) in enumerate(terms):
                            f["tok"] = mm3(o, L, Rr, x == 0, x == len(terms) - 1)
                        end = a == len(pieces) - 1
                        if end:
                            if late:
                                self.finish(late)
                            self.soft1(f)
                            late = (u, f)
                        elif one:
                            continue
                        n = 0
                        if i:
                            n = -(-len(self.todo) // max(1, left))
                            left -= 1
                        fn = -(-fill.left // max(1, slots)) if fill else 0
                        if one and len(fr) == 4:
                            fn = fn * 5 // 2 if i == 0 else fn // 2
                        slots -= 1
                        if fill:
                            fill.pull(fn - fn * n // (n + 1))
                        for k in range(n):
                            if end and k == at2:
                                self.soft2(f)
                            if self.todo:
                                self.step()
                            if fill:
                                fill.pull(-(-fn // (n + 1)))
                        if end and n <= at2:
                            self.soft2(f)
                if fill and nu == 0:
                    fill.pull(max(0, head - fill.done))
                if "hook" in u:
                    u["hook"]()
            self.finish(late)
            if fill:
                fill.drain()
            if tail:
                tail(late[1]["tok"])
            while self.todo:
                if rest:
                    rest.pull(-(-rest.left // (len(self.todo) + 1)))
                self.step()
            self.behind()
            if rest:
                rest.drain()
            for s, banks in enumerate(self.s_banks):
                for b in banks:
                    bank_free[b] = self.s_free[s]
            return PE.last

        def finish(self, late):
            u, f = late
            self.soft3(f)
            if f is u["fronts"][-1]:
                while self.todo:
                    self.step()
                self.queue(u)

    class Keys:

        def __init__(self, hi, lo, p0, p1, a):
            self.hi, self.lo, self.p0, self.p1, self.a = hi, lo, p0, p1, a

        def __call__(self, n):
            return self.hi[self.p0:self.p1, self.a:self.a + n], self.lo[self.p0:self.p1, self.a:self.a + n]

        def after(self, n):
            return Keys(self.hi, self.lo, self.p0, self.p1, self.a + n)

    def pair(hi, lo, p0, p1, a, n):
        return hi[p0:p1, a:a + n], lo[p0:p1, a:a + n]

    def s_start(n):
        return 128 if n % 512 == 128 and n > 512 else 0

    def y_store(j, yt, n, *waits):
        return move(y_d[j][:, 0:n], yt[:, 0:n], *waits)

    for c, (t0, tn) in enumerate(CH1):
        h_ready.update(norm_split(
            lambda k, t0, tn: X[:, k, t0:t0 + tn], 8, cc("o1024"), [(t0, tn)], lambda k, _: vc("g_mix", k), None,
            lambda k: t_x[k, t0], lambda k, t0, tn: Hh[:, k, t0:t0 + tn], lambda k, t0, tn: Hl[:, k, t0:t0 + tn],
            bufs[c]))
    for q in (V, G):
        q.wait(t_tab)
    bl = [blam[:, 64 * i:64 * i + 64] for i in range(4)]
    t = t_blam
    for i in range(2):
        t = V.op(lambda e, i=i: e.tensor_tensor_reduce(ld[:, :], bl[2 * i], bl[2 * i + 1], 1.0, 0.0, ALU.mult,
                                                       ALU.add, lam_t[:, 2 + i:3 + i]), t)
    t = act(lam_t[:, 4:6], lam_t[:, 2:4], ACT.Exp, t)
    t = tt(lam_t[:, 0:1], lam_t[:, 4:5], lam_t[:, 5:6], ALU.subtract, t)
    t = ts(lam_t[:, 1:2], lam_t[:, 0:1], 0.8 - 0.6, -1.0, ALU.add, ALU.mult, t)
    t_lam = ts(nsink[:, :], vc("sink", 0, 8), -1.0, None, ALU.mult, None, t)

    with mem:
        score = [mem([P, 128 * (b + 1)]) for b in range(8)]
        with mem:
            z = [mem([P, T]) for _ in range(3)]
            assert mem.at <= low_end
            iqh, iql = [mem([P, T], R) for _ in range(2)], [mem([P, T], R) for _ in range(2)]
            ikh, ikl = mem([P, T], R), mem([P, T], R)
            tmp = [mem([P, 512]) for _ in range(4)]
            relu = [mem([P, T]) for _ in range(2)]
            wi = mem([P, 8, 4])
            ev = []
            for j, name in enumerate(("iq0", "iq1", "ikw")):
                r = P if j < 2 else 68
                e_ = copy_to(lambda t0, tn, j=j, r=r: z[j][0:r, t0:t0 + tn])
                linear(name, h_rhs, CH1, e_, rows=r)
                ev.append(e_.toks)
            PE.wait(*ev[2], t_lam)
            A.wait(t_lam)
            G.wait(t_lam)
            b = take()
            for i in range(8):
                o = PS[:, 512 * b + 4 * i:512 * b + 4 * i + 4]
                s = z[2][64:68, 128 * i:128 * i + 128]
                m = PE.op(lambda e, o=o, s=s: e.transpose(o, s, ident[64:68, 64:68]))
            o = PS[:, 512 * b:512 * b + 32].rearrange("p (a c) -> p a c", c=4)
            t_w = ts(wi[:, :, :], o, 0.0625, None, ALU.mult, None, m)
            bank_free[b] = [t_w]
            k_t = q_t = post([(z[2], 64, CH1, vc("ik_g"), "swap32", ikh, ikl, ev[2])]
                             + [(z[j], P, CH1, None, "swap32", iqh[j], iql[j], ev[j]) for j in range(2)], tmp)
            d1 = move(ikh[64:128, :], ikh[0:64, :], *k_t)
            d2 = move(ikl[64:128, :], ikl[0:64, :], *k_t)
            PE.wait(*q_t, *k_t, d1, d2)
            r_free = [[], []]
            nr = 0
            prev = None
            t_w = [t_w]
            for b in range(2, 8):
                n = 128 * (b + 1)
                sc = score[b]
                for h in range(4):
                    p0 = 64 * (h % 2)
                    s0 = (nr % 3) * 2
                    banks = list(range(s0, s0 + (n + 511) // 512))
                    for x_ in banks:
                        PE.wait(*bank_free[x_])
                    for c0 in range(0, n, 512):
                        cn = min(512, n - c0)
                        m = mm3(PS[:, 512 * s0 + c0:512 * s0 + c0 + cn],
                                pair(iqh[h // 2], iql[h // 2], p0, p0 + 64, 128 * b, 128),
                                pair(ikh, ikl, p0, p0 + 64, c0, cn), True, True)
                    rl = relu[nr % 2][:, 0:n]
                    t = act(rl, PS[:, 512 * s0:512 * s0 + n], ACT.Relu, m, r_free[nr % 2])
                    for x_ in banks:
                        bank_free[x_] = [t]
                    if h == 0:
                        prev = ts(sc[:, :], rl, wi[:, b, 0:1], None, ALU.mult, None, t, *t_w)
                    else:
                        prev = stt(sc[:, :], rl, wi[:, b, h:h + 1], sc[:, :], ALU.mult, ALU.add, t, prev)
                    r_free[nr % 2] = [prev]
                    nr += 1
                prev = V.op(lambda e, sc=sc, n=n: e.memset(sc[0:64, n - 64:n], OUT_OF_RANGE), prev)
            barrier()

        with mem:
            m8 = [mem([P, 8]) for _ in range(2)]
            for b0 in (2, 4, 6):
                last = {b0: None, b0 + 1: None}
                for it in range(32):
                    for b in (b0, b0 + 1):
                        sc, mx = score[b], m8[b % 2]
                        t = V.op(lambda e, mx=mx, sc=sc: e.max(mx[:, :], sc[:, :]), last[b])
                        last[b] = t
                    for b in (b0, b0 + 1):
                        sc, mx = score[b], m8[b % 2]
                        last[b] = V.op(lambda e, mx=mx, sc=sc: e.match_replace(sc[:, :], mx[:, :], sc[:, :], TAKEN),
                                       last[b])
                for b in (b0, b0 + 1):
                    sc = score[b]
                    ts(sc[:, :], sc[:, :], TAKEN, NEG, ALU.not_equal, ALU.mult, last[b])
            for b in range(2):
                n = 128 * (b + 1)
                t = V.op(lambda e, b=b: e.memset(score[b][:, :], 0.0))
                V.op(lambda e, b=b, n=n: e.memset(score[b][0:64, n - 64:n], NEG), t)
            st["lo"] = G
            lw = mem([P, 4, 2, 128])
            t_l = move(lw[:, :, :, :], lruw)
            xc = [mem([P, T + 3]) for _ in range(4)]
            gl = [mem([P, T]) for _ in range(4)]
            gate = [mem([P, T]) for _ in range(2)]
            for c in range(4):
                t_z = G.op(lambda e, c=c: e.memset(xc[c][:, 0:3], 0.0))
            xc_t, gl_t = [], []
            for c in range(4):
                e1 = copy_to(lambda t0, tn: xc[c][:, 3 + t0:3 + t0 + tn])
                linear(f"cx{c}", h_rhs, CH1, e1)
                xc_t.append(e1.toks + [t_z])
                e1 = copy_to(lambda t0, tn: gl[c][:, t0:t0 + tn])
                linear(f"cy{c}", h_rhs, CH1, e1)
                gl_t.append(e1.toks)
            u, r, i_, a_, th, yc = ring = [mem([P, T]) for _ in range(6)]
            t = act(csil[:, :], vc("cond", 0, 16), ACT.Silu)
            PE.wait(t)
            m_bank = {"ev": 6, "od": 7}
            for b in (6, 7):
                PE.wait(*bank_free[b])
            m_order = [(kind, m_) for kind in ("od",) for m_ in range(24)]

            def modulate(n):
                for kind, m_ in m_order[:n]:
                    get, kt, release = w_get(f"{kind[0]}a{m_}")
                    for k in range(8):
                        m = mm(PS[:, 512 * m_bank[kind] + 2 * m_:512 * m_bank[kind] + 2 * m_ + 2], get(k),
                               csil[:, 2 * k:2 * k + 2], k == 0, k == 7)
                    release(m)
                del m_order[:n]
                return m

            e_slot, e_load, e_done = [Slot(sem(f"s_e{i}")) for i in range(6)], [], []

            def e_fetch(upto):
                while len(e_load) < min(upto, 24):
                    n = len(e_load)
                    at_ = W_AT[f"ea{n}"][0]
                    e_load.append(SP.dma(ring[n % 6][:, :], w[at_:at_ + P * 1024].rearrange("(p c) -> p c", p=P),
                                         e_slot[n % 6], *e_done[n - 6:n - 5] if n >= 6 else []))

            def modulate_first(n):
                PE.wait(e_load[n])
                for k in range(8):
                    m = mm(PS[:, 512 * m_bank["ev"] + 2 * n:512 * m_bank["ev"] + 2 * n + 2],
                           ring[n % 6][:, 128 * k:128 * k + 128], csil[:, 2 * k:2 * k + 2], k == 0, k == 7)
                e_done.append(m)
                e_fetch(n + 6)

            e_fetch(5)
            g_free = [None] * 2
            for d in range(8):
                for i in range(3):
                    x = (3 * d + i) % 2
                    gd, gf, g_t = gate[x], g_free[x], []

                    def ev_s(o, t0, tn, tok):
                        g_t.append(act(gd[:, t0:t0 + tn], o, ACT.Sigmoid, tok, gf, bias=vc("b_gate", 8 * i + d)))
                        return [g_t[-1]]
                    linear(f"gt{i}_{d}", h_rhs, CH1, ev_s)
                    modulate_first(3 * d + i)
                    g_free[x] = move(g_d[8 * i + d], gd[:, :], *g_t, q=A)
            c8, nc8, sa, sb_, sc_, sd_ = (mem([P, 4]) for _ in range(6))
            lam = vc("lam", 0, 4)
            t = ts(sa[:, :], lam, -1.0, None, ALU.mult, None)
            t = tt(sb_[:, :], sa[:, :], lam, ALU.max, t)
            t1 = act(sb_[:, :], sb_[:, :], ACT.Exp, t, scale=-1.0)
            t = ts(sc_[:, :], sb_[:, :], 2.0, None, ALU.add, None, t1)
            t = V.op(lambda e: e.reciprocal(sc_[:, :], sc_[:, :]), t)
            t = tt(sb_[:, :], sb_[:, :], sc_[:, :], ALU.mult, t)
            t = tt(sc_[:, :], sb_[:, :], sb_[:, :], ALU.mult, t)
            t = ts(sd_[:, :], sc_[:, :], 1.0 / 17.0, None, ALU.mult, None, t)
            for n in (15, 13, 11, 9, 7, 5, 3):
                t = stt(sd_[:, :], sd_[:, :], 1.0 / n, sc_[:, :], ALU.add, ALU.mult, t)
            t = stt(sd_[:, :], sd_[:, :], 1.0, sb_[:, :], ALU.add, ALU.mult, t)
            t = ts(sa[:, :], sa[:, :], 0.0, None, ALU.max, None, t)
            t = stt(sd_[:, :], sd_[:, :], 2.0, sa[:, :], ALU.mult, ALU.add, t)
            t = ts(c8[:, :], sd_[:, :], -8.0, None, ALU.mult, None, t)
            t_s = [ts(nc8[:, :], sd_[:, :], 8.0, None, ALU.mult, None, t), t]
            A.wait(*t_s)
            for q in (A, V):
                q.wait(e_done[-1])
            t_y = None
            prev_scan = None
            for c in range(4):
                s = c
                tg = act(gl[c][:, :], gl[c][:, :], ACT.Gelu_apprx_tanh, gl_t[c])
                A.wait(prev_scan)
                t = ts(u[:, :], xc[s][:, 0:T], vc("conv_w", c), vc("conv_b", c), ALU.mult, ALU.add, *xc_t[c], prev_scan)
                for j in range(1, 4):
                    t = stt(u[:, :], xc[s][:, j:j + T], vc("conv_w", 4 * j + c), u[:, :], ALU.mult, ALU.add, t)
                m_t = modulate(6)
                PE.wait(t, t_l)
                for w_i, (dst, bn) in enumerate(((r, "lru_ba"), (i_, "lru_bx"))):
                    for t0, tn in CH1:
                        b = take()
                        m = mm(bank(b), lw[:, c, w_i, :], u[:, t0:t0 + tn])
                        ts_ = act(dst[:, t0:t0 + tn], bank(b), ACT.Sigmoid, m, bias=vc(bn, c))
                        bank_free[b] = [ts_]
                ta = act(a_[:, :], r[:, :], ACT.Exp, ts_, scale=c8[:, c:c + 1])
                tth = act(th[:, :], r[:, :], ACT.Tanh, scale=nc8[:, c:c + 1])
                t = tt(i_[:, :], i_[:, :], u[:, :], ALU.mult, ts_)
                t1 = tt(r[:, :], a_[:, :], a_[:, :], ALU.mult, ta, tth)
                t1 = stt(r[:, :], r[:, :], 1.0, th[:, :], ALU.add, ALU.mult, t1, tth)
                t2 = act(r[:, :], r[:, :], ACT.Sqrt, t1)
                t = tt(i_[:, :], i_[:, :], r[:, :], ALU.mult, t, t2)
                t = V.op(lambda e: e.tensor_tensor_scan(th[:, :], a_[:, :], i_[:, :], 0.0, ALU.mult, ALU.add), t, ta)
                t = tt(yc[:, :], th[:, :], gl[s][:, :], ALU.mult, t, tg, t_y)
                prev_scan = t
                t_y = y_store(4 + c, yc, T, t)
            st["lo"] = V
            for kind in ("ev", "od"):
                b, (mod, gs) = m_bank[kind], mods[kind]
                o = PS[:, 512 * b:512 * b + 48].rearrange("p (a c) -> p a c", c=2)
                bb = vc(f"{kind}_b", 0, 24).rearrange("p (a c) -> p a c", c=1).to_broadcast([P, 24, 2])
                t = tt(mod[:, :, :], o, bb, ALU.add, m_t)
                bank_free[b] = [t]
                for s in range(2):
                    stt(gs[:, :, s], mod[:, 8:16, s], 1.0, vc(f"{kind}_g", 0, 8), ALU.add, ALU.mult, t)
            barrier()

        with mem:
            zq, zk, zv = (mem([P, T]) for _ in range(3))
            yt = zv
            qh, ql, kh, kl = (mem([P, T], R) for _ in range(4))
            vh, vl = mem([P, 8, 128], R), mem([P, 8, 128], R)
            g2 = {kind: mem([P, 1]) for kind in "ab"}
            bias = mem([P, 2, 640])
            at = Attention([[0, 1], [2, 3]], [4, 5], [6], [7], T)
            bufs = [x[:, a:a + 512] for x in at.E for a in (0, 512)]
            pieces = [mem([P, 512]) for _ in range(2)]
            t_g = {kind: ts(g2[kind][:, :], vc(f"{kind}q_g"), 0.125, None, ALU.mult, None) for kind in "ab"}
            ev = {}

            def qk_job(s, z, kind, j, banks):
                e_ = copy_to(lambda t0, tn: z[:, t0:t0 + tn])
                yield from linear_steps(f"{kind}{s}{j}", h_rhs, CH1, e_, banks=banks)
                ev[s] = e_.toks

            order_ab = [("a", 0), ("a", 1), ("b", 0), ("b", 1)]
            for s, z in (("q", zq), ("k", zk)):
                for _ in qk_job(s, z, "a", 0, None):
                    pass
            t_y = None
            bias_t = [move(bias[:, :, :], biasA[:, 0:2, :])]
            ready = []
            for n_ab, (kind, j) in enumerate(order_ab):
                if kind == "a":
                    V.wait(*bias_t)
                    for i in range(2):
                        for d in (bias[0:64, i, 576:640], bias[64:128, i, 0:64]):
                            t = V.op(lambda e, d=d: e.memset(d, NEG))
                    V.wait(t)
                nxt = order_ab[n_ab + 1:n_ab + 2]
                done = []

                def value_steps(banks):
                    A.wait(t_y)
                    e_ = copy_to(lambda t0, tn: zv[:, t0:t0 + tn])
                    yield from linear_steps(f"{kind}v{j}", h_rhs, CH1, e_, banks=banks)
                    ev["v"] = e_.toks

                def steps():
                    if n_ab:
                        yield from value_steps(at.fill_banks)
                        yield from token_major_steps(zv, 8, [(vh, vl, 0, 0, 128)], ev["v"], at.fill_banks, [])
                    for k_, j_ in nxt:
                        sw = "swap32" if k_ == "b" else None
                        yield from qk_job("q", zq, k_, j_, at.fill_banks)
                        yield from weave(qk_job("k", zk, k_, j_, at.fill_banks),
                                         post_steps([(zq, CH1, g2[k_][:, :], sw, ev["q"] + [t_g[k_]])],
                                                    pieces, at.pt_banks, done), 2)
                        yield from post_steps([(zk, CH1, vc(f"{k_}k_g"), sw, ev["k"] + done)], pieces, at.pt_banks, done)

                def tail(tok):
                    if nxt == [("a", 1)]:
                        bias_t[:] = [move(bias[:, :, :], biasA[:, 2:4, :], V.last)]
                    if nxt:
                        ready[:] = split(kh[:, :], kl[:, :], zk[:, :], *done, tok)
                        ready.extend(split(qh[:, :], ql[:, :], zq[:, :], *done, tok))

                if n_ab == 0:
                    v_fill = Fill(value_steps(None), 16)
                    ready += post([(zq, P, CH1, g2[kind], None, qh, ql, ev["q"] + [t_g[kind]]),
                                   (zk, P, CH1, vc(f"{kind}k_g"), None, kh, kl, ev["k"])], bufs,
                                  lambda: v_fill.pull(8))
                    v_fill.drain()
                    ready += to_token_major(zv, 8, [(vh, vl, 0, 0, 128)], ev["v"])
                    barrier()
                units = []
                for b0 in range(0, 8, 2):
                    lo = max(0, b0 - 4) if kind == "a" else 0
                    tiles = range(lo, b0 + 2)
                    for i in range(2):
                        rows = slice(64 * i, 64 * i + 64)
                        fronts = []
                        for b in (b0, b0 + 1):
                            first = max(0, b - 4) if kind == "a" else 0
                            n = 128 * (b + 1 - first)
                            bi = bias[:, i, 640 - n:640] if kind == "a" else score[b][:, :]
                            q = pair(qh, ql, 64 * i, 64 * i + 64, 128 * b, 128)
                            s0 = s_start(n)
                            fronts.append({
                                "pieces": [(s0, n, 128 * (first - lo), bi)],
                                "chunks": [(s0, n, [(q, Keys(kh, kl, 64 * i, 64 * i + 64, 128 * first))])],
                                "pads": [128 * (y - lo) for y in tiles if not first <= y <= b]})
                        yd = yt[rows, 128 * b0:128 * b0 + 256]
                        units.append({"fronts": fronts,
                                      "keys": [(128 * (y - lo), vh[:, y, :], vl[:, y, :]) for y in tiles],
                                      "evac": lambda o, m, yd=yd, rows=rows: [act(yd, o[rows, :], ACT.Copy, m)]})
                more = (8 if nxt and nxt[0][0] == "b" else 6) + 32 if nxt else 0
                at.run(units, ready, Fill(steps(), more + (18 if n_ab else 0)), 18 if n_ab else 0, tail)
                t_y = y_store((0 if kind == "a" else 2) + j, yt, T, A.last)
            barrier()

    with mem:
        Yh, Yl = mem([P, 8, T], R), mem([P, 8, T], R)
        t_tab = move(tabs[:, :, :], tab_d[1].rearrange("a p t -> p a t"))
        gate = [mem([P, T]) for _ in range(5)]
        mg = mem([P, 512])
        t1b = mem([P, 512])
        g_free = [[] for _ in range(5)]
        y_ready = []
        for k in range(8):
            t_d = move(gate[k % 5][:, :], y_d[k][:, 0:T], *g_free[k % 5])
            g_free[k % 5] = split(Yh[:, k, :], Yl[:, k, :], gate[k % 5][:, :], t_d)
            y_ready += g_free[k % 5]
        PE.wait(*y_ready)
        sig, t_m = [], []
        for d in range(8):
            get, kt, release = w_get(f"wb{d}")
            for c, (t0, tn) in enumerate(CH1):
                last = None
                for i, (k0, k1) in enumerate(((0, 2), (2, 4), (4, 8))):
                    b = take()
                    for k in range(k0, k1):
                        m = mm3(bank(b), get(k), (Yh[:, k, t0:t0 + tn], Yl[:, k, t0:t0 + tn]), k == k0, k == k1 - 1)
                    n = 3 * d + i
                    while len(sig) < min(n + 3, 24):
                        x = len(sig)
                        sig.append(move(gate[(x + 3) % 5][:, :], g_d[8 * (x % 3) + x // 3], *g_free[(x + 3) % 5]))
                    if i == 0:
                        last = tt(mg[:, :], bank(b), gate[(n + 3) % 5][:, t0:t0 + tn], ALU.mult, m, sig[n], *t_m)
                        bank_free[b] = [last]
                    else:
                        t = tt(t1b[:, :], bank(b), gate[(n + 3) % 5][:, t0:t0 + tn], ALU.mult, m, sig[n], last)
                        bank_free[b] = [t]
                        last = tt(mg[:, :], mg[:, :], t1b[:, :], ALU.add, t, last)
                    g_free[(n + 3) % 5] = [last]
                t_m = split(Hh[:, d, t0:t0 + tn], Hl[:, d, t0:t0 + tn], mg[:, :], last)
            release(m)
        barrier()

    with mem:
        X = mem([P, 8, TC])
        GM = max(FFN_GROUPS)
        uh, ul = mem([P, GM, T], R), mem([P, GM, T], R)
        sg = [mem([P, 512]) for _ in range(2)]
        bufs = norm_bufs(1, 3, 2)
        t_x = [move(X[:, :, 0:T], xT.rearrange("k p t -> p k t")),
               move(X[:, :, T:TC], ctxT.rearrange("k p t -> p k t"))]
        V.wait(*t_x)

        def add_to(d, sums=None):
            def evac(o, t0, tn, tok):
                x = X[:, d, t0:t0 + tn]
                t = tt(x, x, o, ALU.add, tok)
                if sums:
                    sums.add(t0 // 512, x, tn, t)
                return [t]
            return evac

        def x_at(k, t0, tn):
            return X[:, k, t0:t0 + tn]

        def hh_at(k, t0, tn):
            return Hh[:, k, t0:t0 + tn]

        def hl_at(k, t0, tn):
            return Hl[:, k, t0:t0 + tn]

        sums = Squares(bufs[1], bufs[0])
        for d in range(8):
            linear(f"wo{d}", h_rhs, CH1, add_to(d, sums))
        h_ready = norm_split(x_at, 8, cc("o1024"), CH1, lambda k, c: vc("g_ffn", k), None, [], hh_at, hl_at, bufs, sums)
        sums = Squares(bufs[1], bufs[0])
        for d in range(8):
            sums.add(2, x_at(d, T, 256), 256, *t_x, *h_ready[7, 512])
        sg_free = [[], []]
        f0 = 0
        for n, g in enumerate(FFN_GROUPS):
            fin_t = []
            for f in range(g):
                sil = {}

                def ev_g(o, t0, tn, tok):
                    c = t0 // 512
                    sil[c] = act(sg[c][:, :], o, ACT.Silu, tok, sg_free[c])
                    return [sil[c]]

                def ev_u(o, t0, tn, tok):
                    c = t0 // 512
                    t = tt(sg[c][:, :], sg[c][:, :], o, ALU.mult, tok, sil[c])
                    sg_free[c] = split(uh[:, f, t0:t0 + tn], ul[:, f, t0:t0 + tn], sg[c][:, :], t)
                    return [t]
                if f == 0:
                    A.wait(PE.last)
                    V.wait(PE.last)
                linear(f"fg{f0 + f}", h_rhs, CH1, ev_g)
                linear(f"fu{f0 + f}", h_rhs, CH1, ev_u)
                fin_t = [sg_free[0], sg_free[1]]
            PE.wait(*fin_t)
            for d in range(8):
                linear(f"fo{n}_{d}", lambda k, t0, tn: (uh[:, k, t0:t0 + tn], ul[:, k, t0:t0 + tn]), CH1,
                       add_to(d, sums if n == len(FFN_GROUPS) - 1 else None))
            f0 += g
        t_store = move(x1_d.rearrange("k p t -> p k t"), X[:, :, 0:T], V.last)

        def cond_of(c):
            return 1 if c == 2 else 0

        def modulated(kind, bufs, sums):
            m_, g_ = mods[kind]
            return norm_split(x_at, 8, cc("o1024"), CH2, lambda k, c: g_[:, k, cond_of(c):cond_of(c) + 1],
                              lambda k, c: m_[:, k, cond_of(c):cond_of(c) + 1], [], hh_at, hl_at, bufs, sums)

        mod, gs = mods["ev"]
        h_ready = modulated("ev", bufs, sums)
        x_done = [t_store] + [t for x in h_ready.values() for t in x]

    def gate_evac(gt, n=TC):
        toks = []

        def evac(o, t0, tn, tok):
            toks.append(act(gt[:, t0:t0 + tn], o, ACT.Silu, tok))
            return [toks[-1]]
        evac.toks = toks
        return evac

    def plain(yt, rows, b0, free):
        yd = yt[rows, 128 * b0:128 * b0 + 256]
        return lambda o, m: [act(yd, o[rows, :], ACT.Copy, m, *free)]

    def gated(yt, gt, rows, b0):
        yd, gd = yt[rows, 128 * b0:128 * b0 + 256], gt[rows, 128 * b0:128 * b0 + 256]
        return lambda o, m: [tt(yd, o[rows, :], gd, ALU.mult, m)]

    with mem:
        inner_at = mem.at
        mem([P, 11136])
        z_at = mem.at
        zq, zk, zv, zg, yt = (mem([P, TC]) for _ in range(5))
        qh, ql, kh, kl = (mem([P, TC], R) for _ in range(4))
        pieces = [zg[:, 0:512], zg[:, 512:1024]]
        ev = {}

        def next_steps(chunks, nxt, banks):
            for s, z, scale in (("q", zq, 0.125), ("k", zk, 1.0), ("v", zv, 1.0)):
                if s in nxt:
                    e_ = copy_to(lambda t0, tn: z[:, t0:t0 + tn], scale)
                    yield from linear_steps(nxt[s], h_rhs, chunks[s], e_, banks=banks)
                    ev[s] = e_.toks

        def rotate_steps(nxt, banks, done):
            yield from post_steps([(z, CH2, None, "swap16", ev[s]) for s, z in (("k", zk), ("q", zq)) if s in nxt],
                                  pieces, banks, done)

        def gate_steps(name, chunks, free, banks):
            A.wait(*free)
            e_ = copy_to(lambda t0, tn: zg[:, t0:t0 + tn])
            yield from linear_steps(name, h_rhs, chunks, e_, banks=banks)

        def parts_of(nxt, *waits):
            toks = split(kh[:, :], kl[:, :], zk[:, :], *waits) if "k" in nxt else []
            return toks + split(qh[:, :], ql[:, :], zq[:, :], *waits)

        CHE = {s: CH2 for s in "qkv"}
        for _ in next_steps(CHE, {"q": "eq0", "k": "ek0", "v": "ev"}, None):
            pass
        for q in (A, V, G):
            q.wait(*x_done)
        done = []
        for _ in rotate_steps("qk", None, done):
            pass
        ready = parts_of("qk", *done)
        y_free = []
        with mem.over(inner_at):
            vh, vl = [mem([P, 10, 128], R) for _ in range(2)], [mem([P, 10, 128], R) for _ in range(2)]
            at = Attention([[0, 1], [2, 3]], [4, 5], [6], [7], 768)
            assert mem.at <= z_at
            for j in range(4):
                kv = j // 2
                nxt = {"q": f"eq{j + 1}"} if j < 3 else {"q": "fq0", "k": "fk0", "v": "fv0"}
                if j == 1:
                    nxt["k"] = "ek1"
                done = []

                def steps():
                    if j == 0:
                        yield from token_major_steps(zv, 10, [(vh[i], vl[i], c, 64 * i, 64) for i in range(2)
                                                              for c in (0, 64)], ev["v"], at.fill_banks, [])
                    yield from next_steps(CHE, nxt, at.fill_banks)
                    yield from rotate_steps(nxt, at.fill_banks, done)

                def tail(tok):
                    ready[:] = parts_of(nxt, *done, tok)
                units = []
                for b0 in range(0, 10, 2):
                    tiles = range(max(0, b0 - 1), min(8, b0 + 3)) if b0 < 8 else []
                    for i in range(2):
                        rows = slice(64 * i, 64 * i + 64)
                        fronts = []
                        for b in (b0, b0 + 1):
                            q = pair(qh, ql, 64 * i, 64 * i + 64, 128 * b, 128)
                            f = {"sink": 2 * j + i, "pieces": [(512, 256, 512, None)], "pads": [],
                                 "chunks": [(512, 256, [(q, Keys(kh, kl, 64 * i, 64 * i + 64, T))])]}
                            if b < 8:
                                first, end = max(0, b - 1), min(8, b + 2)
                                n = 128 * (end - first)
                                m0 = C_AT["win"][0] + (128 if b == 0 else 0)
                                f["pieces"].insert(0, (0, n, 128 * (first - b0 + 1), cst[:, m0:m0 + n]))
                                f["chunks"].insert(0, (0, n, [(q, Keys(kh, kl, 64 * i, 64 * i + 64, 128 * first))]))
                                f["pads"] = [128 * (y - b0 + 1) for y in tiles if not first <= y < end]
                            fronts.append(f)
                        kt = [(512, 8), (640, 9)] + [(128 * (y - b0 + 1), y) for y in tiles]
                        units.append({"fronts": fronts, "keys": [(e0, vh[kv][:, y, :], vl[kv][:, y, :]) for e0, y in kt],
                                      "evac": plain(yt, rows, b0, y_free)})
                at.run(units, ready, Fill(steps(), 3 * (j == 0) + 24 * len(nxt) + 2 * min(2, len(nxt))), 3, tail,
                       Fill(gate_steps(f"eg{j}", CH2, done, at.fill_banks), 24))
                t = act(zg[:, :], zg[:, :], ACT.Silu, A.last)
                t = tt(yt[:, :], yt[:, :], zg[:, :], ALU.mult, t)
                y_free[:] = [y_store(j, yt, TC, t)]
            barrier()

        with mem.over(inner_at):
            vh, vl = mem([P, 10, 128], R), mem([P, 10, 128], R)
            g8 = mem([P, 1])
            at = Attention([[0, 1, 2]], [3, 4], [5], [6, 7], TC, 2, 1)
            assert mem.at <= z_at
            t_g8 = ts(g8[:, :], vc("subln"), 1.0 - (0.8 - 0.6), None, ALU.mult, None)

            stored, y_parts = [], []

            def load_steps():
                free = [[PE.last, *ready], [PE.last, *ready]]
                for k in range(7):
                    z = (zk, zv)[k % 2]
                    t = move(z[:, :], y_d[k], *free[k % 2], *stored)
                    for _ in range(4):
                        yield
                    free[k % 2] = split(Hh[:, k, :], Hl[:, k, :], z[:, :], t)
                    y_parts.extend(free[k % 2])

            def finish_steps(h, free, banks):
                t_s = act(zg[:, :], zg[:, :], ACT.Silu, A.last)
                for t0, tn in CH2:
                    yc, r = yt[:, t0:t0 + tn], zq[:, t0:t0 + tn]
                    t = act(r, yc, ACT.Square, *free)
                    yield
                    PE.wait(t)
                    b = fill_bank(banks)
                    m = mm(bank(b)[:, 0:tn], cc("o128"), r)
                    t, ta = root(r, bank(b)[:, 0:tn], m)
                    bank_free[b] = [ta]
                    t = stt(yc, yc, g8[:, 0:1], r, ALU.mult, ALU.mult, t, t_g8)
                    t = tt(yc, yc, zg[:, t0:t0 + tn], ALU.mult, t, t_s)
                    yield
                y_free[:] = [y_store(4 + h, yt, TC, t) if h < 3 else t]
                stored.extend(y_free)
                A.wait(t)

            for h in range(4):
                nxt = {s: f"f{s}{h + 1}" for s in "qkv"} if h < 3 else {}
                done = []

                def steps():
                    if h:
                        yield from finish_steps(h - 1, ready, at.fill_banks)
                    yield from token_major_steps(zv, 10, [(vh, vl, 0, 0, 128)], ev["v"], at.fill_banks, [])
                    if h < 3:
                        yield from next_steps(CHE, nxt, at.fill_banks)
                        yield from rotate_steps(nxt, at.fill_banks, done)
                    else:
                        yield from gate_steps("eg7", CH2, done, at.fill_banks)
                        yield from load_steps()

                def tail(tok):
                    if h < 3:
                        ready[:] = parts_of("qk", *done, tok)
                units = []
                for b0 in range(0, 10, 2):
                    n, k0 = (TC, 0) if b0 < 8 else (256, T)
                    fronts = []
                    for b in (b0, b0 + 1):
                        for i in range(2):
                            q = pair(qh, ql, 64 * i, 64 * i + 64, 128 * b, 128)
                            f = {"pieces": [(0, n, 0, None)], "lam": True,
                                 "chunks": [(0, n, [(q, Keys(kh, kl, 64 * i, 64 * i + 64, k0))])]}
                            if i:
                                f["first"], f["second"] = fronts[-1], True
                            fronts.append(f)
                    yd = yt[:, 128 * b0:128 * b0 + 256]
                    units.append({"fronts": fronts,
                                  "keys": [(128 * y, vh[:, k0 // 128 + y, :], vl[:, k0 // 128 + y, :])
                                           for y in range(n // 128)],
                                  "evac": lambda o, m, yd=yd: [act(yd, o, ACT.Copy, m, *y_free)]})
                at.run(units, ready, Fill(steps(), 10 + (76 if h < 3 else 52)), 10, tail,
                       Fill(gate_steps(f"eg{4 + h}", CH2, done, at.fill_banks), 24) if h < 3 else None)
            for _ in finish_steps(3, ready, None):
                pass
            y_parts += split(Hh[:, 7, :], Hl[:, 7, :], yt[:, :], V.last)
            barrier()

    with mem:
        X = mem([P, 8, TC])
        PE.wait(*y_parts)
        mem([P, 9216])
        bufs = norm_bufs(1, 3, 2)
        t_x = [move(X[:, :, 0:T], x1_d.rearrange("k p t -> p k t")),
               move(X[:, :, T:TC], ctxT.rearrange("k p t -> p k t"))]
        V.wait(*t_x)

        def add_gated(d, sums=None):
            def evac(o, t0, tn, tok):
                s, x = 1 if t0 >= T else 0, X[:, d, t0:t0 + tn]
                t = stt(x, o, mod[:, 16 + d, s:s + 1], x, ALU.mult, ALU.add, tok)
                if sums:
                    sums.add(t0 // 512, x, tn, t)
                return [t]
            return evac

        h_ready = {}
        sums = Squares(bufs[1], bufs[0])
        for d in range(8):
            linear(f"eo{d}", h_rhs, CH2, add_gated(d, sums))
        t_store = move(x1_d.rearrange("k p t -> p k t"), X[:, :, 0:T], V.last)
        mod, gs = mods["od"]
        h_ready = modulated("od", bufs, sums)
        x_done = [t_store] + [t for x in h_ready.values() for t in x]

    with mem:
        vh, vl = mem([P, 10, 128], R), mem([P, 10, 128], R)
        bt = [mem([P, 14, 64]) for _ in range(2)]
        bi = [mem([P, 640]) for _ in range(2)]
        at = Attention([[0, 1], [2, 3]], [4, 5], [6], [7], T)
        zq, zk, zv, zg, yt = mem([P, T]), mem([P, TC]), mem([P, TC]), mem([P, T]), mem([P, T])
        qh, ql = mem([P, T], R), mem([P, T], R)
        kh, kl = mem([P, TC], R), mem([P, TC], R)
        CHO = {"q": CH1, "k": CH2, "v": CH2}
        for _ in next_steps(CHO, {s: f"d{s}0" for s in "qkv"}, None):
            pass
        for q in (A, V, G):
            q.wait(*x_done)
        START = {0: (0, 7), 1: (0, 5), 6: (8, 3), 7: (8, 1)}

        def bias_load(j, *free):
            toks = []
            for i in range(2):
                t = move(bt[i][:, :, :], biasD[2 * j + i], *free)
                cm = cc("col").rearrange("p (a c) -> p a c", a=1).to_broadcast([P, 14, 64])
                toks.append(tt(bt[i][:, :, :], bt[i][:, :, :], cm, ALU.add, t, q=G))
            return toks

        def bias_inner(toks):
            V.wait(*toks)
            for i in range(2):
                t = V.op(lambda e, i=i: e.tensor_copy(bi[i][:, :], bt[i][:, 2:12, :].rearrange("p a c -> p (a c)")))
                for rows, c0, c1 in (((0, 64), 512, 640), ((64, 128), 0, 64), ((64, 128), 576, 640)):
                    t = V.op(lambda e, i=i, rows=rows, c0=c0, c1=c1: e.memset(bi[i][rows[0]:rows[1], c0:c1], NEG), t)

        bias_inner(bias_load(0))
        ready = parts_of("qk", *ev["q"], *ev["k"])
        y_free[:] = []
        for j in range(4):
            nxt = {s: f"d{s}{j + 1}" for s in "qkv"} if j < 3 else {}
            bias_t = []

            def steps():
                yield from token_major_steps(zv, 10, [(vh, vl, 0, 0, 128)], ev["v"], at.fill_banks, [])
                yield from next_steps(CHO, nxt, at.fill_banks)

            def hook():
                if j < 3:
                    bias_t[:] = bias_load(j + 1, V.last)

            def tail(tok):
                if j < 3:
                    ready[:] = parts_of("qk", *ev["q"], *ev["k"], tok)
                    bias_inner(bias_t)
            units = []
            for b0 in (0, 6, 2, 4):
                inner = 2 <= b0 <= 4
                tiles = range(b0 - 2, b0 + 4) if inner else range(0, 4) if b0 == 0 else range(4, 8)
                for i in range(2):
                    rows = slice(64 * i, 64 * i + 64)
                    fronts = []
                    for b in (b0, b0 + 1):
                        q = pair(qh, ql, 64 * i, 64 * i + 64, 128 * b, 128)
                        if inner:
                            first, n, s0, bias = b - 2, 640, 128, bi[i][:, :]
                        else:
                            first, n, s0 = tiles[0], 512, 0
                            v0 = START[b][1] - 1
                            bias = bt[i][:, v0:v0 + 8, :].rearrange("p a c -> p (a c)")
                        keys = [Keys(kh, kl, 64 * i, 64 * i + 64, a) for a in (128 * first, T)]
                        fronts.append({
                            "pieces": [(s0, n, 128 * (first - tiles[0]), bias), (s0 + n, 256, 768, None)],
                            "chunks": [(s0, n, [(q, keys[0])]), (s0 + n, 256, [(q, keys[1])])],
                            "pads": [128 * (y - tiles[0]) for y in tiles if not first <= y < first + n // 128]})
                    kt = [(768, 8), (896, 9)] + [(128 * (y - tiles[0]), y) for y in tiles]
                    units.append({"fronts": fronts, "keys": [(e0, vh[:, y, :], vl[:, y, :]) for e0, y in kt],
                                  "evac": plain(yt, rows, b0, y_free)})
            units[3]["hook"] = hook
            at.run(units, ready, Fill(steps(), 3 + (64 if j < 3 else 0)), 3, tail,
                   Fill(gate_steps(f"og{4 + j}", CH1, [], at.fill_banks), 16))
            t = act(zg[:, :], zg[:, :], ACT.Silu, A.last)
            t = tt(yt[:, :], yt[:, :], zg[:, :], ALU.mult, t)
            y_free[:] = [y_store(4 + j, yt, T, t)]
        barrier()

    SC = 192.0 ** -0.5
    with mem:
        cqh, cql = mem([P, 2, T], R), mem([P, 2, T], R)
        ckh, ckl = mem([P, TC], R), mem([P, TC], R)
        rph, rpl = mem([P, TC], R), mem([P, TC], R)
        gts = [mem([P, T]) for _ in range(4)]
        with mem:
            zc = mem([P, 2, T])
            zk, zr = mem([P, TC]), mem([P, TC])
            tmp = [mem([P, 512]) for _ in range(4)]
            evs = []
            for j in range(2):
                e_ = copy_to(lambda t0, tn, j=j: zc[:, j, t0:t0 + tn])
                linear(f"cq{j}", h_rhs, CH1, e_)
                evs += e_.toks
            ek = copy_to(lambda t0, tn: zk[:, t0:t0 + tn])
            linear("ckv", h_rhs, CH2, ek)
            er = copy_to(lambda t0, tn: zr[:, t0:t0 + tn])
            linear("ckr", h_rhs, CH2, er)
            half = [g[:, a:a + 512] for g in gts[1:] for a in (0, 512)]
            norm_split(lambda k, t0, tn: zc[:, k, t0:t0 + tn], 2, cc("o256"), CH1,
                       lambda k, c: vc("qn_g", k), None, evs,
                       lambda k, t0, tn: cqh[:, k, t0:t0 + tn], lambda k, t0, tn: cql[:, k, t0:t0 + tn],
                       norm_bufs(1, 2, 2))
            kv_t = norm_split(lambda k, t0, tn: zk[:, t0:t0 + tn], 1, cc("o128"), CH2,
                       lambda k, c: vc("kvn_g"), None, ek.toks,
                       lambda k, t0, tn: ckh[:, t0:t0 + tn], lambda k, t0, tn: ckl[:, t0:t0 + tn],
                       norm_bufs(1, 3, 2, half))
            post([(zr, P, CH2, None, "swap16", rph, rpl, er.toks)], tmp)
            for h in range(4):
                if h == 1:
                    A.wait(*kv_t.values())
                linear(f"og{h}", h_rhs, CH1, gate_evac(gts[h]))
            barrier()
        early = [4, 5, 6, 7]
        Yh, Yl = mem([P, 4, T], R), mem([P, 4, T], R)
        y_parts = []

        def load_steps():
            free = [[V.last], [V.last]]
            for i, k in enumerate(early):
                t = move(gts[i % 2][:, :], y_d[k][:, 0:T], *free[i % 2])
                for _ in range(4):
                    yield
                free[i % 2] = split(Yh[:, i, :], Yl[:, i, :], gts[i % 2][:, :], t)
                y_parts.extend(free[i % 2])

        with mem.over(h_at):
            zq = mem([P, TC])
            qnh, qnl = mem([P, T], R), mem([P, T], R)
            qph, qpl = mem([P, T], R), mem([P, T], R)
            knh, knl = mem([P, TC], R), mem([P, TC], R)
            vh, vl = mem([P, 10, 128], R), mem([P, 10, 128], R)
            at = Attention([[0, 1, 2], [3, 4, 5]], [6], [7], [], TC)
            tmp = [x[:, a:a + 512] for x in at.E for a in (0, 512)]
            yt = zq

            def q_rhs(k, t0, tn):
                return cqh[:, k, t0:t0 + tn], cql[:, k, t0:t0 + tn]

            def kv_rhs(k, t0, tn):
                return ckh[:, t0:t0 + tn], ckl[:, t0:t0 + tn]

            def ev_split(hi, lo):
                toks = []

                def evac(o, t0, tn, tok):
                    t = split(hi[:, t0:t0 + tn], lo[:, t0:t0 + tn], o, tok)
                    toks.extend(t)
                    return t
                evac.toks = toks
                return evac

            for h in range(4):
                ready = []
                if h % 2 == 0:
                    e_ = copy_to(lambda t0, tn: zq[:, t0:t0 + tn])
                    linear(f"qp{h // 2}", q_rhs, CH1, e_)
                    ready += post([(zq, P, CH1, None, "swap16", qph, qpl, e_.toks)], tmp)
                e1 = ev_split(qnh, qnl)
                linear(f"qn{h}", q_rhs, CH1, e1)
                e2 = ev_split(knh, knl)
                linear(f"kn{h}", kv_rhs, CH2, e2)
                A.wait(*ready)
                e3 = copy_to(lambda t0, tn: zq[:, t0:t0 + tn])
                linear(f"vn{h}", kv_rhs, CH2, e3)
                ready += to_token_major(zq, 10, [(vh, vl, 0, 0, 128)], e3.toks)
                barrier()
                p0 = 64 * (h % 2)
                units = []
                for b0 in range(0, 8, 2):
                    fronts = []
                    for b in (b0, b0 + 1):
                        terms = [(pair(qnh, qnl, 0, P, 128 * b, 128), Keys(knh, knl, 0, P, 0)),
                                 (pair(qph, qpl, p0, p0 + 64, 128 * b, 128), Keys(rph, rpl, p0, p0 + 64, 0))]
                        fronts.append({"pieces": [(0, TC, 0, None)], "chunks": [(0, TC, terms)], "scale": SC})
                    units.append({"fronts": fronts, "keys": [(128 * y, vh[:, y, :], vl[:, y, :]) for y in range(10)],
                                  "evac": gated(yt, gts[h], slice(0, P), b0)})
                at.run(units, ready + e1.toks + e2.toks, Fill(load_steps(), 16) if h == 3 else None)
                if h < 3:
                    y_store(h, yt, T, V.last)
                barrier()

    with mem.over(h_at):
        mem([P, TC])
        late = [(mem([P, T], R), mem([P, T], R)) for _ in range(4)]
        X = mem([P, 8, T])
        t_d = [move(gts[k][:, :], y_d[k][:, 0:T]) for k in range(3)]
        t_x = [move(X[:, k, :], x1_d[k]) for k in range(8)]
        late_t = split(late[3][0][:, :], late[3][1][:, :], yt[:, 0:T])
        for k in range(3):
            late_t += split(late[k][0][:, :], late[k][1][:, :], gts[k][:, :], t_d[k])
        PE.wait(*late_t)

        def y_rhs(k, t0, tn):
            if k in early:
                i = early.index(k)
                return Yh[:, i, t0:t0 + tn], Yl[:, i, t0:t0 + tn]
            h, l_ = late[k]
            return h[:, t0:t0 + tn], l_[:, t0:t0 + tn]

        V.wait(*t_x)
        sq = [mem([P, 512]) for _ in range(2)]
        rs = [mem([P, 512]) for _ in range(2)]
        sums = Squares(rs, sq)
        for d in range(8):
            linear(f"oo{d}", y_rhs, CH1, add_gated(d, sums))
        means = []
        for c in range(2):
            PE.wait(sums.t[c])
            b = take()
            means.append((b, mm(bank(b), cc("o1024"), rs[c][:, :])))
        outs = []
        for c, (t0, tn) in enumerate(CH1):
            b, m = means[c]
            t, ta = root(rs[c][:, :], bank(b), m)
            bank_free[b] = [ta]
            for k in range(8):
                x = X[:, k, t0:t0 + tn]
                if k % 3 == 2:
                    t1 = tt(x, x, rs[c][:, :], ALU.mult, t, q=G)
                    t1 = A.op(lambda e, x=x, k=k: e.activation(x, x, ACT.Copy, scale=vc("fin_g", k)), t1)
                else:
                    t1 = stt(x, x, vc("fin_g", k), rs[c][:, :], ALU.mult, ALU.mult, t)
                outs.append((k, t0, tn, t1))
        s_out = Slot(sem("s_out"))
        for k, t0, tn, t1 in outs:
            t_o = SP.dma(out[k][:, t0:t0 + tn], X[:, k, t0:t0 + tn], s_out, t1)
        SP.wait(t_o)
        barrier()

    queues = (PE, A, V, G, SP)
    for q in queues:
        q.number()
    with nc.Block() as block:
        @block.tensor
        def _(e):
            PE.emit(e)

        @block.scalar
        def _(e):
            A.emit(e)

        @block.vector
        def _(e):
            V.emit(e)

        @block.gpsimd
        def _(e):
            G.emit(e)

        @block.sync
        def _(e):
            SP.emit(e)




def columns(v):
    return np.ascontiguousarray(np.asarray(v).reshape(-1, P).T)


def constants():
    p = np.arange(P)
    out = {"ident": np.eye(P)}
    for n in (1024, 256, 128):
        out[f"o{n}"] = np.full((P, P), 1.0 / n)
    out["o64"] = (p[:, None] // 64 == p[None, :] // 64) / 64.0
    out["swap32"] = (p[:, None] == (p ^ 32)[None, :]) * 1.0
    out["swap16"] = (p[:, None] == (p ^ 16)[None, :]) * 1.0
    j = np.arange(384)
    out["win"] = np.where(np.abs(p[:, None] - j[None, :] + 128) <= 128, 0.0, NEG)
    c = np.arange(64)
    cs = np.clip(p % 64 - 8, 0, 48)[:, None]
    out["col"] = np.where((c[None, :] >= cs) & (c[None, :] < cs + 16), 0.0, NEG)
    cst = np.concatenate([out[n] for n, _ in CONSTS], axis=1).astype(np.float32)

    f = np.float32
    e = np.arange(0, 64, 2, dtype=f) / f(64)
    inv = f(1) / (10000.0 ** e.astype(np.float64)).astype(f)
    t = np.arange(T)
    ang = (t.astype(f)[:, None] * inv[None, :]).astype(f)
    ang1 = np.concatenate([ang, ang], axis=1)
    inv2 = (10000.0 ** (-np.arange(16) / 16)).astype(f)
    ar = ((t // 64).astype(f)[:, None] * inv2[None, :]).astype(f)
    ac = ((t % 64).astype(f)[:, None] * inv2[None, :]).astype(f)
    ang2 = np.concatenate([ar, ar, ac, ac], axis=1)
    d = np.arange(64)
    tabs = []
    for a, sign in ((ang1, np.where(d % 64 < 32, -1.0, 1.0)), (ang2, np.where(d % 32 < 16, -1.0, 1.0))):
        a = a.astype(np.float64)
        tabs.append([np.tile(np.cos(a).T, (2, 1)), np.tile((np.sin(a) * sign[None, :]).T, (2, 1))])
    return cst, np.array(tabs).astype(f)


def layout(inp):
    i = {k: np.asarray(v) for k, v in inp.items()}
    wi = i["w_in"][0]
    cuts = np.cumsum([256] * 6 + [256, 64, 4, 512, 512])
    aq, ak, av, bq, bk, bv, iq, ik, iw, cx, cy, gtw = np.split(wi, cuts, axis=1)
    ev = np.split(i["ev_w_in_2"][0], np.cumsum([512, 128, 128, 512, 512, 512]), axis=1)
    od = np.split(i["od_w_in_2"][0], np.cumsum([256, 128, 64, 512, 512, 512]), axis=1)
    wqb = i["od_c_w_qb_2"][0].reshape(256, 4, 192)
    wkv = i["od_c_w_kvb_2"][0].reshape(128, 4, 256)
    fi, fo = i["w_ffn_in"][0], i["w_ffn_out"][0]
    DFF = fo.shape[0]
    parts = {}

    def cols(a, j):
        return a[:, 128 * j:128 * j + 128]

    for j in range(2):
        for n, a in (("iq", iq), ("aq", aq), ("ak", ak), ("av", av), ("bq", bq), ("bk", bk), ("bv", bv)):
            parts[f"{n}{j}"] = cols(a, j)
        k_ = ev[1][:, 64 * j:64 * j + 64]
        parts[f"ek{j}"] = np.concatenate([k_, k_], axis=1)
        parts[f"qp{j}"] = wqb[:, 2 * j:2 * j + 2, 128:].reshape(256, 128)
        parts[f"cq{j}"] = cols(od[0], j)
    parts["ikw"] = np.concatenate([ik, iw], axis=1)
    parts["ev"] = ev[2]
    parts["ckv"] = od[1]
    parts["ckr"] = np.concatenate([od[2], od[2]], axis=1)
    for j in range(4):
        for n, a in (("cx", cx), ("cy", cy), ("eq", ev[0]), ("fq", ev[3]), ("fk", ev[4]), ("fv", ev[5]),
                     ("dq", od[3]), ("dk", od[4]), ("dv", od[5])):
            parts[f"{n}{j}"] = cols(a, j)
        parts[f"qn{j}"] = wqb[:, j, :128]
        parts[f"kn{j}"] = wkv[:, j, :128]
        parts[f"vn{j}"] = wkv[:, j, 128:]
    for d in range(8):
        for n in range(3):
            parts[f"gt{n}_{d}"] = cols(gtw, 8 * n + d)
        for n, a in (("wb", i["w_branch"][0]), ("wo", i["w_out"][0]), ("eo", i["ev_w_out_2"][0]),
                     ("oo", i["od_w_out_2"][0]), ("eg", ev[6]), ("og", od[6])):
            parts[f"{n}{d}"] = cols(a, d)
        f0 = 0
        for n, g in enumerate(FFN_GROUPS):
            parts[f"fo{n}_{d}"] = fo[128 * f0:128 * (f0 + g), 128 * d:128 * d + 128]
            f0 += g
    for f in range(DFF // 128):
        parts[f"fg{f}"] = cols(fi, f)
        parts[f"fu{f}"] = cols(fi[:, DFF:], f)
    for m in range(24):
        parts[f"ea{m}"] = cols(i["ev_w_ada_2"][0], m)
        parts[f"oa{m}"] = cols(i["od_w_ada_2"][0], m)
    at, total = weight_offsets()
    w = np.empty(total, np.float32)
    for name, (a, kt, m) in at.items():
        w[a:a + P * kt * m] = parts[name].reshape(kt, P, m).transpose(1, 0, 2).reshape(-1)

    def two(v):
        return np.concatenate([v, v])[:, None]

    vecs = {
        "g_mix": columns(i["g_mix"][0]), "aq_g": two(i["qk_gain_a"][0, 0]), "ak_g": two(i["qk_gain_a"][0, 1]),
        "bq_g": two(i["qk_gain_b"][0, 0]), "bk_g": two(i["qk_gain_b"][0, 1]), "ik_g": two(i["g_idx_k"][0]),
        "conv_w": np.concatenate([columns(i["conv_w"][0, j]) for j in range(4)], axis=1),
        "conv_b": columns(i["conv_b"][0]), "lru_ba": columns(i["lru_ba"][0]), "lru_bx": columns(i["lru_bx"][0]),
        "lam": columns(i["lru_lambda"][0]), "b_gate": columns(i["b_gate"][0]), "g_ffn": columns(i["g_ffn"][0]),
        "ev_g": columns(i["ev_norm_g_2"][0]), "ev_b": columns(i["ev_b_ada_2"][0]),
        "sink": np.broadcast_to(i["ev_a_sink_2"][0], (P, 8)),
        "blam": np.broadcast_to(i["ev_b_lambda_2"][0].reshape(1, 256), (P, 256)),
        "subln": i["ev_b_subln_g_2"][0][:, None], "od_g": columns(i["od_norm_g_2"][0]),
        "od_b": columns(i["od_b_ada_2"][0]), "qn_g": columns(i["od_c_q_norm_g_2"][0]),
        "kvn_g": columns(i["od_c_kv_norm_g_2"][0]), "fin_g": columns(i["final_norm_g_2"]),
        "cond": np.stack([columns(i["c_2"][0]), columns(i["c_ctx_2"])], axis=2).reshape(P, 16),
    }
    vec = np.concatenate([vecs[n] for n, _ in VECS], axis=1).astype(np.float32)
    cst, tabs = constants()
    xT = np.ascontiguousarray(i["x"][0].T).reshape(8, P, T)
    ctxT = np.ascontiguousarray(i["ctx_2"][0].T).reshape(8, P, 256)
    p, j = np.arange(P)[:, None], np.arange(640)[None, :]
    biasA = np.ascontiguousarray(i["rel_bias"][0][:, np.clip(512 + p - j, -128, 128) + 128].transpose(1, 0, 2))
    dc = np.clip(np.arange(64)[None, :] - (np.arange(P) % 64)[:, None] + 15, 0, 30)
    v = np.arange(1, 15)[None, :] - (np.arange(P) >= 64)[:, None]
    biasD = np.ascontiguousarray(i["od_d_rpb_2"][0][:, v[:, :, None], dc[:, None, :]])
    lru = np.zeros((P, 4, 2, P), np.float32)
    for n, a in enumerate((i["lru_wa"][0], i["lru_wx"][0])):
        for g in range(8):
            o = 64 * (g % 2)
            lru[o:o + 64, g // 2, n, o:o + 64] = a[g]
    return {"w": w, "vec": vec, "cst": cst, "tab": tabs, "xT": xT, "ctxT": ctxT, "biasA": biasA, "biasD": biasD,
            "lru": lru}


def kernel(**inputs):
    import concourse.bacc as _bacc
    from concourse.bass_utils import run_bass_kernel_spmd as _run

    arrays = layout(inputs)
    nc = _bacc.Bacc("TRN2", target_bir_lowering=False, num_devices=1)
    feed, args = {}, []
    for name, a in arrays.items():
        feed[f"in_{name}"] = np.ascontiguousarray(a)
        args.append(nc.dram_tensor(f"in_{name}", a.shape, F, kind="ExternalInput").ap())
    out = nc.dram_tensor("out_0", (8, P, T), F, kind="ExternalOutput").ap()
    build(nc, *args, out)
    r = _run(nc, [feed], core_ids=[0])
    got = r.results[0]["out_0"]
    return np.ascontiguousarray(np.asarray(got).reshape(1024, T).T).reshape(1, T, 1024)
```
